# Optimizing a Trainium2 kernel written in Bass

```python
import jax, jax.numpy as jnp
from jax import lax
import numpy as np

D_MODEL = 1024
BATCH = 1
SEQ = 512
DEPTH = 2

N_MIXERS = 2
N_RET_LAYERS = (DEPTH + 1) // 2
N_NSA_LAYERS = DEPTH // 2

D_FF = 2816
RMS_EPS = 1e-6

RET_HEADS = 4
RET_DK = D_MODEL // RET_HEADS
RET_DV = 2 * RET_DK
RET_CHUNK = 128
RET_ROPE_BASE = 10000.0
RET_IN = RET_HEADS * (2 * RET_DK + 2 * RET_DV)

NSA_HEADS = 16
NSA_GROUPS = 4
NSA_HPG = NSA_HEADS // NSA_GROUPS
NSA_DH = 64
NSA_KV = NSA_GROUPS * NSA_DH
CMP_LEN = 32
CMP_STRIDE = 16
CMP_HID = 256
SLC_LEN = 64
N_SEL = 8
WINDOW = 512
NSA_QBLOCK = 32
NSA_IN = NSA_HEADS * NSA_DH + 6 * NSA_KV + 3 * NSA_HEADS

NUM_BUCKETS = 32
MAX_DISTANCE = 128

NEG_INF = -1e30
SEL_BIG = 1e9

kernel_name = "hybrid_retention_nsa_macaron"

def rmsnorm(x, g):
    xf = x.astype(jnp.float32)
    y = xf * lax.rsqrt(jnp.mean(xf * xf, axis=-1, keepdims=True) + RMS_EPS)
    return (y * g.astype(jnp.float32)).astype(x.dtype)

def headnorm(a, g):
    af = a.astype(jnp.float32)
    return af * lax.rsqrt(jnp.mean(af * af, axis=-1, keepdims=True) + RMS_EPS) * g.astype(jnp.float32)

def swiglu_ffn(x, norm_g, w_gu, w_down):
    h = rmsnorm(x, norm_g) @ w_gu
    a, b = jnp.split(h, 2, axis=-1)
    return (jax.nn.silu(a) * b) @ w_down

def t5_bucket(dist):
    n = jnp.maximum(dist, 0)
    max_exact = NUM_BUCKETS // 2
    nf = jnp.maximum(n, max_exact).astype(jnp.float32)
    large = max_exact + (jnp.log(nf / max_exact) / np.float32(np.log(MAX_DISTANCE / max_exact))
                         * (NUM_BUCKETS - max_exact)).astype(jnp.int32)
    large = jnp.minimum(large, NUM_BUCKETS - 1)
    return jnp.where(n < max_exact, n, large)

def rotary(x, pos):
    half = x.shape[-1] // 2
    inv_freq = RET_ROPE_BASE ** (-jnp.arange(half, dtype=jnp.float32) / half)
    ang = pos[:, None] * inv_freq[None, :]
    cos, sin = jnp.cos(ang), jnp.sin(ang)
    x1, x2 = x[..., :half], x[..., half:]
    return jnp.concatenate([x1 * cos - x2 * sin, x1 * sin + x2 * cos], axis=-1)

def retention(xn, w_in, w_out):
    B, T, _ = xn.shape
    H, dk, dv, C = RET_HEADS, RET_DK, RET_DV, RET_CHUNK
    N = T // C
    h = xn @ w_in
    q, k, v, g = jnp.split(h, [H * dk, 2 * H * dk, 2 * H * dk + H * dv], axis=-1)
    q = q.reshape(B, T, H, dk).transpose(0, 2, 1, 3).astype(jnp.float32)
    k = k.reshape(B, T, H, dk).transpose(0, 2, 1, 3).astype(jnp.float32)
    v = v.reshape(B, T, H, dv).transpose(0, 2, 1, 3).astype(jnp.float32)
    pos = jnp.arange(T, dtype=jnp.float32)
    q = rotary(q, pos)
    k = rotary(k, pos) * (dk ** -0.5)
    log_gamma = jnp.log(1.0 - 2.0 ** (-5.0 - jnp.arange(H, dtype=jnp.float32)))
    i = jnp.arange(C)
    diff = i[:, None] - i[None, :]
    intra = jnp.where(diff >= 0, jnp.exp(log_gamma[:, None, None] * jnp.maximum(diff, 0)), 0.0)
    q_dec = jnp.exp(log_gamma[:, None] * (i + 1))[:, :, None]
    k_dec = jnp.exp(log_gamma[:, None] * (C - 1 - i))[:, :, None]
    chunk_dec = jnp.exp(log_gamma * C)[:, None, None]

    def to_chunks(a):
        return a.reshape(B, H, N, C, a.shape[-1]).transpose(2, 0, 1, 3, 4)

    def step(S, qkv):
        qc, kc, vc = qkv
        s = jnp.einsum('bhid,bhjd->bhij', qc, kc) * intra
        o = (jnp.einsum('bhij,bhjv->bhiv', s, vc)
             + jnp.einsum('bhid,bhdv->bhiv', qc * q_dec, S))
        S = chunk_dec * S + jnp.einsum('bhjd,bhjv->bhdv', kc * k_dec, vc)
        return S, o

    S0 = jnp.zeros((B, H, dk, dv), jnp.float32)
    _, o = lax.scan(step, S0, (to_chunks(q), to_chunks(k), to_chunks(v)))
    o = o.transpose(1, 2, 0, 3, 4).reshape(B, H, T, dv)
    o = o * lax.rsqrt(jnp.mean(o * o, axis=-1, keepdims=True) + RMS_EPS)
    o = o.transpose(0, 2, 1, 3).reshape(B, T, H * dv)
    o = jax.nn.silu(g.astype(jnp.float32)) * o
    return o.astype(xn.dtype) @ w_out

def masked_softmax(s, valid):
    p = jax.nn.softmax(jnp.where(valid, s, NEG_INF), axis=-1)
    return jnp.where(valid, p, 0.0)

def nsa(xn, w_in, w_out, q_gain, k_gain, cmp_pos, cmp_w1, cmp_w2, rel_bias):
    B, T, _ = xn.shape
    H, G, P, dh, QB = NSA_HEADS, NSA_GROUPS, NSA_HPG, NSA_DH, NSA_QBLOCK
    n_cmp = (T - CMP_LEN) // CMP_STRIDE + 1
    n_slc = T // SLC_LEN
    n_sel = min(N_SEL, n_slc)
    sizes = [H * dh] + [NSA_KV] * 6 + [3 * H]
    parts = jnp.split(xn @ w_in, list(np.cumsum(sizes)[:-1]), axis=-1)
    q_, kc_, vc_, ks_, vs_, kw_, vw_, gate_ = parts

    def heads(a, n):
        return a.reshape(B, T, n, dh).transpose(0, 2, 1, 3)

    q = headnorm(heads(q_, H), q_gain).reshape(B, G, P, T, dh)
    cidx = np.arange(n_cmp)[:, None] * CMP_STRIDE + np.arange(CMP_LEN)[None, :]

    def compress(a, j):
        blocks = a[:, :, cidx] + cmp_pos[j]
        flat = blocks.reshape(B, G, n_cmp, CMP_LEN * dh)
        return jax.nn.gelu(flat @ cmp_w1[j]) @ cmp_w2[j]

    k_cmp = headnorm(compress(heads(kc_, G), 0), k_gain[0])
    v_cmp = compress(heads(vc_, G), 1)
    k_slc = headnorm(heads(ks_, G), k_gain[1]).reshape(B, G, n_slc, SLC_LEN, dh)
    v_slc = heads(vs_, G).reshape(B, G, n_slc, SLC_LEN, dh)
    pad = ((0, 0), (0, 0), (WINDOW, 0), (0, 0))
    k_win = jnp.pad(headnorm(heads(kw_, G), k_gain[2]), pad)
    v_win = jnp.pad(heads(vw_, G), pad)
    gates = jax.nn.sigmoid(gate_.astype(jnp.float32)).reshape(B, T, 3, G, P).transpose(0, 2, 3, 4, 1)

    ci = np.arange(n_cmp) * CMP_STRIDE
    sj = np.arange(n_slc) * SLC_LEN
    overlap = jnp.asarray(((ci[:, None] < sj[None, :] + SLC_LEN) &
                           (ci[:, None] + CMP_LEN > sj[None, :])).astype(np.float32))
    cmp_end = jnp.arange(n_cmp) * CMP_STRIDE + CMP_LEN - 1
    tbl = rel_bias.astype(jnp.float32)
    tbl_hp = tbl.reshape(NUM_BUCKETS, G, P)
    tbl_g = tbl_hp.transpose(1, 0, 2)
    bi = jnp.arange(B)[:, None, None, None]
    gi = jnp.arange(G)[None, :, None, None]
    scale = dh ** -0.5
    blk_ids = jnp.arange(n_slc)

    def dense_bias(dist):
        return tbl_hp[t5_bucket(dist)].transpose(2, 3, 0, 1)

    def block(qb):
        t0 = qb * QB
        qpos = t0 + jnp.arange(QB)
        qblk = lax.dynamic_slice_in_dim(q, t0, QB, axis=3)
        gblk = lax.dynamic_slice_in_dim(gates, t0, QB, axis=4)
        s = (jnp.einsum('bgpqd,bgnd->bgpqn', qblk, k_cmp) * scale
             + dense_bias(qpos[:, None] - cmp_end[None, :]))
        p_c = masked_softmax(s, cmp_end[None, :] <= qpos[:, None])
        o_c = jnp.einsum('bgpqn,bgnd->bgpqd', p_c, v_cmp)
        imp = jnp.einsum('bgpqn,nj->bgqj', p_c, overlap)
        cur = qpos // SLC_LEN
        forced = ((blk_ids[None, :] == 0) | (blk_ids[None, :] == cur[:, None])
                  | (blk_ids[None, :] == cur[:, None] - 1))
        imp = jnp.where(forced, SEL_BIG, jnp.where(blk_ids[None, :] <= cur[:, None], imp, -SEL_BIG))
        _, sel = lax.top_k(imp, n_sel)
        ks = k_slc[bi, gi, sel].reshape(B, G, QB, n_sel * SLC_LEN, dh)
        vs = v_slc[bi, gi, sel].reshape(B, G, QB, n_sel * SLC_LEN, dh)
        kpos = (sel[..., None] * SLC_LEN + jnp.arange(SLC_LEN)).reshape(B, G, QB, n_sel * SLC_LEN)
        dist = qpos[None, None, :, None] - kpos
        bias_s = jnp.moveaxis(tbl_g[gi, t5_bucket(dist)], -1, 2)
        s = jnp.einsum('bgpqd,bgqkd->bgpqk', qblk, ks) * scale + bias_s
        p_s = masked_softmax(s, (dist >= 0)[:, :, None])
        o_s = jnp.einsum('bgpqk,bgqkd->bgpqd', p_s, vs)
        kw = lax.dynamic_slice_in_dim(k_win, t0, QB + WINDOW, axis=2)
        vw = lax.dynamic_slice_in_dim(v_win, t0, QB + WINDOW, axis=2)
        wpos = t0 - WINDOW + jnp.arange(QB + WINDOW)
        dist_w = qpos[:, None] - wpos[None, :]
        valid_w = (dist_w >= 0) & (dist_w < WINDOW) & (wpos[None, :] >= 0)
        s = jnp.einsum('bgpqd,bgkd->bgpqk', qblk, kw) * scale + dense_bias(dist_w)
        p_w = masked_softmax(s, valid_w)
        o_w = jnp.einsum('bgpqk,bgkd->bgpqd', p_w, vw)
        return (gblk[:, 0, ..., None] * o_c + gblk[:, 1, ..., None] * o_s
                + gblk[:, 2, ..., None] * o_w)

    o = lax.map(block, jnp.arange(T // QB))
    o = o.transpose(1, 0, 4, 2, 3, 5).reshape(B, T, H * dh)
    return o.astype(xn.dtype) @ w_out

def setup_inputs(seed: int = 0) -> dict:
    key = jax.random.key(seed)
    ks = jax.random.split(key, 20)
    f32 = jnp.float32

    def w(k, shape, fan_in):
        return jax.random.normal(k, shape, f32) * (fan_in ** -0.5)

    def gain(k, shape):
        return 1.0 + 0.02 * jax.random.normal(k, shape, f32)

    return {
        "x": jax.random.normal(ks[0], (BATCH, SEQ, D_MODEL), f32),
        "ffn1_norm": gain(ks[1], (DEPTH, D_MODEL)),
        "ffn1_w_gu": w(ks[2], (DEPTH, D_MODEL, 2 * D_FF), D_MODEL),
        "ffn1_w_down": w(ks[3], (DEPTH, D_FF, D_MODEL), D_FF),
        "mix_norm": gain(ks[4], (DEPTH, D_MODEL)),
        "ffn2_norm": gain(ks[5], (DEPTH, D_MODEL)),
        "ffn2_w_gu": w(ks[6], (DEPTH, D_MODEL, 2 * D_FF), D_MODEL),
        "ffn2_w_down": w(ks[7], (DEPTH, D_FF, D_MODEL), D_FF),
        "ret_w_in": w(ks[8], (N_RET_LAYERS, D_MODEL, RET_IN), D_MODEL),
        "ret_w_out": w(ks[9], (N_RET_LAYERS, RET_HEADS * RET_DV, D_MODEL), RET_HEADS * RET_DV),
        "nsa_w_in": w(ks[10], (N_NSA_LAYERS, D_MODEL, NSA_IN), D_MODEL),
        "nsa_w_out": w(ks[11], (N_NSA_LAYERS, NSA_HEADS * NSA_DH, D_MODEL), NSA_HEADS * NSA_DH),
        "nsa_q_gain": gain(ks[12], (N_NSA_LAYERS, NSA_DH)),
        "nsa_k_gain": gain(ks[13], (N_NSA_LAYERS, 3, NSA_DH)),
        "nsa_cmp_pos": 0.1 * jax.random.normal(ks[14], (N_NSA_LAYERS, 2, CMP_LEN, NSA_DH), f32),
        "nsa_cmp_w1": w(ks[15], (N_NSA_LAYERS, 2, CMP_LEN * NSA_DH, CMP_HID), CMP_LEN * NSA_DH),
        "nsa_cmp_w2": w(ks[16], (N_NSA_LAYERS, 2, CMP_HID, NSA_DH), CMP_HID),
        "rel_bias": 0.5 * jax.random.normal(ks[17], (NUM_BUCKETS, NSA_HEADS), f32),
    }

def reference(x, ffn1_norm, ffn1_w_gu, ffn1_w_down, mix_norm, ffn2_norm, ffn2_w_gu, ffn2_w_down,
              ret_w_in, ret_w_out, nsa_w_in, nsa_w_out, nsa_q_gain, nsa_k_gain,
              nsa_cmp_pos, nsa_cmp_w1, nsa_cmp_w2, rel_bias):
    for layer in range(DEPTH):
        x = x + 0.5 * swiglu_ffn(x, ffn1_norm[layer], ffn1_w_gu[layer], ffn1_w_down[layer])
        xn = rmsnorm(x, mix_norm[layer])
        j = layer // N_MIXERS
        if layer % N_MIXERS == 0:
            m = retention(xn, ret_w_in[j], ret_w_out[j])
        else:
            m = nsa(xn, nsa_w_in[j], nsa_w_out[j], nsa_q_gain[j], nsa_k_gain[j],
                    nsa_cmp_pos[j], nsa_cmp_w1[j], nsa_cmp_w2[j], rel_bias)
        x = x + m
        x = x + 0.5 * swiglu_ffn(x, ffn2_norm[layer], ffn2_w_gu[layer], ffn2_w_down[layer])
    return x


_drawn_inputs = setup_inputs


def setup_inputs(seed=0):
    import zlib

    import numpy as np

    out = dict(_drawn_inputs(seed))
    spreads = {}
    factors = {'ffn1_norm': 3.98,
     'ffn2_norm': 5.564,
     'nsa_q_gain': 53.716,
     'nsa_k_gain': 47.978,
     'mix_norm': 3.762,
     'nsa_cmp_pos': 6.994,
     'rel_bias': 38.681}
    for name, (base, spread) in spreads.items():
        noise = np.random.default_rng([zlib.crc32(name.encode()), seed]).standard_normal(out[name].shape)
        drawn = base * np.exp(spread * noise) if base else spread * noise
        out[name] = __import__('jax').numpy.asarray(drawn.astype(out[name].dtype))
    for name, factor in factors.items():
        out[name] = (out[name] * factor).astype(out[name].dtype)
    return out
```

```python
from contextlib import ExitStack

import numpy as np
import concourse.bass as bass
from concourse import mybir

F32 = mybir.dt.float32
F32R = mybir.dt.float32r
ALU = mybir.AluOpType
ACT = mybir.ActivationFunctionType

P = 128
D = 1024
T = 512
KT = D // P
TT = T // P
F = 2816
FT = F // P
EPS = 1e-6
RH, DK, DV = 4, 256, 512
NH, NG, HPG, DH = 16, 4, 4, 64
CMP_LEN, CMP_STRIDE = 32, 16
NC = (T - CMP_LEN) // CMP_STRIDE + 1
NCP = NC + 1
GN = NG * NC
LP = CMP_LEN // 2
BUCKETS = 32
REL = 640
BIG = 1e30

SLOTS = 4
CW = 1024
UP, DOWN = 2 * FT, FT
C_FFN = [0, 0, 0, 0]
C_FFN[0] = 0
C_RET = C_FFN[0] + UP + DOWN
C_FFN[1] = C_RET + RH * 16
C_FFN[2] = C_FFN[1] + UP + DOWN
C_NSA = C_FFN[2] + UP + DOWN
C_NOUT = C_NSA + 28
C_FFN[3] = C_NOUT + 8
NCHUNK = C_FFN[3] + UP + DOWN
G_FFN = [4, 0, 0, 0]
G_RET = G_FFN[0] + FT
G_FFN[1] = G_RET + RH * 8
G_FFN[2] = G_FFN[1] + FT
G_NSA = G_FFN[2] + FT
G_FFN[3] = G_NSA + 10
NS, NTT = 12, 9
SLC, WIN, CMPB = 0, 1, 2
LAG = NS - NTT
O_AT = 1
P_OFF = [0, 128, 384, 768]
PB = 1280
PW = 2 * PB + TT * NCP


def p_slice(b, i):
    if b == CMPB:
        return 2 * PB + i * NCP, 7 + 8 * i
    return b * PB + P_OFF[i], P * (i + 1)


def trunk(nc, x_in, stream, norm_g, gate_w, cmp_w2, cmp_pos, qk_gain, rel, c_sq, c_rot, c_dec, c_rel, rel_rows, out):
    ctx = ExitStack()
    with ctx:
        def sem(name):
            return ctx.enter_context(nc.semaphore(name))

        def sb(name, shape, dt=F32, scope=ctx):
            return scope.enter_context(nc.sbuf_tensor(name, shape, dt))

        x = sb("x", [P, KT, T])
        xh = sb("xh", [P, KT, T], F32R)
        xl = sb("xl", [P, KT, T], F32R)
        raw = sb("raw", [P, SLOTS, CW])
        wh = sb("wh", [P, SLOTS, CW], F32R)
        wl = sb("wl", [P, SLOTS, CW], F32R)
        sq = sb("sq", [P, 2, T])
        std = sb("std", [P, 2, T])
        csq = sb("csq", [P, 2 * P + 1])
        ident = csq[:, 0:P]
        bones = csq[:, P:2 * P]
        rowmask = csq[:, 2 * P:2 * P + 1]
        ones = sb("ones", [P, P])
        eps = sb("eps", [P, 1])
        pmark = sb("pmark", [1, 1])
        mark = sb("mark", [1, 16])
        gain = sb("gain", [P, 6, KT])
        qkg = sb("qkg", [P, 4])

        with ExitStack() as s:
            uh = sb("uh", [P, FT, T], F32R, s)
            ul = sb("ul", [P, FT, T], F32R, s)
            uf = sb("uf", [P, 2, T], F32, s)
            bf = sb("bf", [P, 2, T], F32, s)
        with ExitStack() as s:
            rot = sb("rot", [P, 2, T], F32, s)
            dec = sb("dec", [P, RH, T], F32, s)
            rt = sb("rt", [P, 4, T], F32, s)
            qf = sb("qf", [P, 2, T], F32, s)
            qkh = sb("qkh", [P, 2, 2, T], F32R, s)
            qkl = sb("qkl", [P, 2, 2, T], F32R, s)
            vh = sb("vh", [P, TT, DV], F32R, s)
            vl = sb("vl", [P, TT, DV], F32R, s)
            sg = sb("sg", [P, 4, T], F32, s)
            af = sb("af", [P, PB], F32, s)
            ah = sb("ah", [P, PB], F32R, s)
            al = sb("al", [P, PB], F32R, s)
            onf = rt
            onh = sb("onh", [P, 4, T], F32R, s)
            onl = sb("onl", [P, 4, T], F32R, s)
        with ExitStack() as s:
            qn = sb("qn", [P, KT, T], F32, s)
            kh = sb("kh", [P, 2, NG, T], F32R, s)
            kl = sb("kl", [P, 2, NG, T], F32R, s)
            vf = sb("vf", [P, TT, 2, NG, DH], F32, s)
            vst = sb("vst", [P, TT, 2, 2 * DH], F32R, s)
            gates = sb("gates", [P, NH, TT, 3], F32, s)
            kch = sb("kch", [P, NG, NCP], F32R, s)
            kcl = sb("kcl", [P, NG, NCP], F32R, s)
            vcf = sb("vcf", [NCP, NG, DH], F32, s)
            vcst = sb("vcst", [NCP, 2 * DH], F32R, s)
            qs = sb("qs", [P, 2, T], F32R, s)
            mn = sb("mn", [P, 2, NS], F32, s)
            rsum = sb("rsum", [P, 2, NS], F32, s)
            coef = sb("coef", [P, 2, NS], F32, s)
            with ExitStack() as s2:
                z = sb("z", [P, 2, NG, T // 2], F32, s2)
                u = sb("u", [P, 4 * T], F32, s2)
                uch = sb("uch", [P, LP * GN], F32R, s2)
                ucl = sb("ucl", [P, LP * GN], F32R, s2)
                pos = sb("pos", [P, 2, LP], F32, s2)
                w2 = sb("w2", [P, 2, 2, DH], F32, s2)
            with ExitStack() as s2:
                tn = sb("tn", [P, 2, T], F32, s2)
                pr = sb("pr", [P, 2, PW], F32, s2)
                pth = sb("pth", [P, 2, T], F32R, s2)
                ptl = sb("ptl", [P, 2, T], F32R, s2)
        osq = [sq[:, 0, :], sq[:, 1, :], std[:, 0, :], std[:, 1, :]]
        kn = u[:, :].rearrange("p (a t) -> p a t", a=4)
        with ExitStack() as s:
            xin = sb("xin", [P, TT, D], F32, s)
            relw = sb("relw", [BUCKETS + 1, NH], F32, s)
            onehot = sb("onehot", [BUCKETS + 1, REL], F32, s)
            relo = sb("relo", [NH, REL], F32, s)
        ps = ctx.enter_context(nc.psum_tensor("ps", [P, 8, T], F32))
        gwf = vf[:, 0, :, :, :].rearrange("p b g d -> p (b g d)")[:, 0:KT * 48].rearrange("p (k n) -> p k n", k=KT)
        gw2 = vst[:, :, :, :].rearrange("p t b d -> p (t b d)")[:, 0:2 * KT * 48]
        gwh, gwl = [gw2[:, i * KT * 48:(i + 1) * KT * 48].rearrange("p (k n) -> p k n", k=KT) for i in range(2)]
        gl = z[:, 0, 0:2, :].rearrange("p g t -> p (g t)")[:, 0:4 * GN].rearrange("p (j t n) -> p j t n", j=2, t=2)
        kct = u[0:DH, 0:2 * GN].rearrange("p (j n) -> p j n", j=2)
        kcf = u[0:DH, 2 * GN:3 * GN]

        raw_landed = [sem(f"raw_landed{i}") for i in range(SLOTS)]
        chunk_hi = sem("chunk_hi")
        chunk_lo = sem("chunk_lo")
        chunk_mm = sem("chunk_mm")
        pair_free = sem("pair_free")
        consts_in = sem("consts_in")
        consts_set = sem("consts_set")
        x_in_landed = sem("x_in_landed")
        x_turned = sem("x_turned")
        x_ready = sem("x_ready")
        sq_ready = sem("sq_ready")
        sq_sum = sem("sq_sum")
        ss_mm = sem("ss_mm")
        xh_ready = sem("xh_ready")
        xt_ready = sem("xt_ready")
        a_scaled = sem("a_scaled")
        std_ready = sem("std_ready")
        xn_ready = sem("xn_ready")
        silu_ready = sem("silu_ready")
        u_ready = sem("u_ready")
        down_mm = sem("down_mm")
        dve_step = sem("dve_step")
        pool_set = sem("pool_set")
        rel_mm = sem("rel_mm")
        rel_out = sem("rel_out")
        rel_stored = sem("rel_stored")
        ret_in = sem("ret_in")
        qk_ready = sem("qk_ready")
        v_ready = sem("v_ready")
        s_read = sem("s_read")
        osq_sum = sem("osq_sum")
        s_mm = sem("s_mm")
        a_ready = sem("a_ready")
        pv_mm = sem("pv_mm")
        osq_ready = sem("osq_ready")
        oss_mm = sem("oss_mm")
        ostd_ready = sem("ostd_ready")
        sig_ready = sem("sig_ready")
        sg_ready = sem("sg_ready")
        on_ready = sem("on_ready")
        hsq_ready = sem("hsq_ready")
        hss_mm = sem("hss_mm")
        hstd_ready = sem("hstd_ready")
        hn_ready = sem("hn_ready")
        uc_ready = sem("uc_ready")
        uc_used = sem("uc_used")
        gw_ready = sem("gw_ready")
        gate_mm = sem("gate_mm")
        gates_set = sem("gates_set")
        gelu_ready = sem("gelu_ready")
        w2_mm = sem("w2_mm")
        kcsq_ready = sem("kcsq_ready")
        kcss_mm = sem("kcss_mm")
        kcstd_ready = sem("kcstd_ready")
        cmp_ready = sem("cmp_ready")
        bias_landed = [sem("bias_landed0"), sem("bias_landed1")]
        qs_ready = sem("qs_ready")
        vst_ready = sem("vst_ready")
        sc_mm = sem("sc_mm")
        sc_read = sem("sc_read")
        exp_done = sem("exp_done")
        coef_ready = sem("coef_ready")
        p_scaled = sem("p_scaled")
        pt_mm = sem("pt_mm")
        pt_hi = sem("pt_hi")
        pt_ready = sem("pt_ready")
        apv_mm = sem("apv_mm")
        o_half = sem("o_half")
        o_ready = sem("o_ready")
        y_mm = sem("y_mm")
        y_ready = sem("y_ready")
        y_stored = sem("y_stored")

        def chunk(c0, i=None, step=0):
            if i is None:
                return c0, c0 % SLOTS, c0 // SLOTS
            return i * step + c0, c0 % SLOTS, i * (step // SLOTS) + c0 // SLOTS

        block = ctx.enter_context(nc.Block())

        @block.sync
        def _(sp):
            def load(ch):
                c, slot, turn = ch
                sp.dma_start(raw[:, slot, :], stream[c]).then_inc(raw_landed[slot], 16)

            for t in range(TT):
                sp.dma_start(xin[:, t, :], x_in[t * P:(t + 1) * P, :]).then_inc(x_in_landed, 16)
            sp.dma_start(csq[:, :], c_sq).then_inc(consts_in, 16)
            for c in range(SLOTS):
                load(chunk(c))
            sp.dma_start(gain[:, :, :], norm_g).then_inc(consts_in, 16)
            sp.dma_start(qkg[:, :], qk_gain).then_inc(consts_in, 16)
            sp.dma_start(relw[0:BUCKETS, :], rel).then_inc(consts_in, 16)
            sp.dma_start(onehot[:, :], c_rel).then_inc(consts_in, 16)

            def loads(c0, n):
                with sp.Fori(0, n // SLOTS) as i:
                    for k in range(SLOTS):
                        ch = chunk(c0 + k, i, SLOTS)
                        sp.wait_ge(chunk_lo, ch[0] - (SLOTS - 1))
                        load(ch)
                for c in range(c0 + n // SLOTS * SLOTS, c0 + n):
                    sp.wait_ge(chunk_lo, c - (SLOTS - 1))
                    load(chunk(c))

            sp.wait_ge(rel_out, 1)
            sp.dma_start(rel_rows, relo[:, :]).then_inc(rel_stored, 16)
            loads(SLOTS, C_RET - SLOTS)
            sp.wait_ge(chunk_mm, C_RET)
            sp.dma_start(rot[:, :, :], c_rot).then_inc(ret_in, 16)
            sp.dma_start(dec[:, :, :], c_dec).then_inc(ret_in, 16)
            loads(C_RET, C_NSA - C_RET)
            sp.wait_ge(chunk_mm, C_NSA)
            sp.dma_start(gwf[:, :, :], gate_w).then_inc(ret_in, 16)
            sp.dma_start(pos[:, :, :], cmp_pos).then_inc(ret_in, 16)
            sp.dma_start(w2[:, :, :, :], cmp_w2).then_inc(ret_in, 16)
            loads(C_NSA, C_NOUT + 2 * SLOTS - C_NSA)
            sp.wait_ge(rel_stored, 16)
            sp.wait_ge(cmp_ready, 2)
            sp.wait_ge(gates_set, 1)

            def bias(h, b):
                row = rel_rows[h]
                src = bass.AP(row.tensor, row.offset + 1, [[1, P], [1, T]])
                sp.dma_start(tn[:, b, :], src).then_inc(bias_landed[b], 16)

            bias(0, 0)
            bias(1, 1)
            with sp.Fori(1, NH // 2) as i:
                for b in range(2):
                    sp.wait_ge(sc_read, (i * 2 + (b - 1)) * NS)
                    bias(i * 2 + b, b)
            loads(C_NOUT + 2 * SLOTS, NCHUNK - C_NOUT - 2 * SLOTS)
            for t in range(TT):
                sp.wait_ge(y_ready, 8 * (t + 1))
                sp.dma_start(out[t * P:(t + 1) * P, :], xin[:, t, :]).then_inc(y_stored, 16)
            sp.wait_ge(y_stored, 16 * TT)

        @block.gpsimd
        def _(pool):
            def low(ch):
                c, slot, turn = ch
                pool.wait_ge(chunk_hi, c + 1)
                nc.gpsimd.tensor_tensor(wl[:, slot, :], raw[:, slot, :], wh[:, slot, :].bitcast(F32),
                                        ALU.subtract).then_inc(chunk_lo, 1)

            def lows(c0, c1):
                n = c1 - c0
                if n >= SLOTS:
                    with pool.Fori(0, n // SLOTS) as i:
                        for k in range(SLOTS):
                            low(chunk(c0 + k, i, SLOTS))
                for c in range(c0 + n // SLOTS * SLOTS, c1):
                    low(chunk(c))

            acc = std[:, 1, :]

            def sum_squares(m):
                add = nc.gpsimd.tensor_tensor
                pool.wait_ge(sq_ready, m * KT + 2)
                add(acc, sq[:, 0, :], sq[:, 1, :], ALU.add).then_inc(sq_sum, 1)
                for d in range(2, KT):
                    pool.wait_ge(sq_ready, m * KT + d + 1)
                    pool.wait_ge(sq_sum, m * (KT - 1) + d - 1)
                    add(acc, acc, sq[:, d % 2, :], ALU.add).then_inc(sq_sum, 1)

            nc.gpsimd.memset(pmark[:, :], 0.0).then_inc(pool_set, 1)
            pool.wait_ge(pool_set, 1)
            ahead = SLOTS - 1
            lows(0, ahead)
            sum_squares(0)
            lows(ahead, C_RET + ahead)
            sum_squares(1)
            low(chunk(C_RET + ahead))
            lows(C_RET + 4, C_RET + 16)
            def sum_outputs(h):
                pool.wait_ge(osq_ready, h * 4 + 4)
                for v in range(1, 4):
                    if v > 1:
                        pool.wait_ge(osq_sum, h * 3 + (v - 1))
                    nc.gpsimd.tensor_tensor(osq[0], osq[0], osq[v], ALU.add).then_inc(osq_sum, 1)

            with pool.Fori(0, RH - 1) as h:
                sum_outputs(h)
                for k in range(16):
                    low(chunk(C_RET + 16 + k, h, 16))
            sum_outputs(RH - 1)
            at = C_RET + 64
            for m, c0 in ((2, C_FFN[1]), (3, C_FFN[2]), (4, C_NSA)):
                lows(at, c0 + ahead)
                sum_squares(m)
                at = c0 + ahead
            split = C_NOUT + SLOTS
            lows(at, split)
            with pool.Fori(0, NH // 2) as i:
                for b in range(2):
                    pool.wait_ge(pool_set, i * 2 + b + 1)
                    pool.wait_ge(coef_ready, i * 2 + b + 1)
                    nc.gpsimd.tensor_tensor(pmark[:, :], pmark[:, :], pmark[:, :], ALU.mult).then_inc(pool_set, 1)
                    for br in range(3):
                        for ti in range(TT):
                            o, n = p_slice(br, ti)
                            k = ti * 3 + br
                            nc.gpsimd.tensor_scalar(pr[:, b, o:o + n], pr[:, b, o:o + n], coef[:, b, k:k + 1],
                                                    1.0, ALU.mult, ALU.mult).then_inc(p_scaled, 1)
            lows(split, C_FFN[3] + ahead)
            sum_squares(5)
            lows(C_FFN[3] + ahead, NCHUNK)

        @block.scalar
        def _(act):
            def high(ch, first=False):
                c, slot, turn = ch
                act.wait_ge(raw_landed[slot], turn * 16 + 16)
                if not first:
                    act.wait_ge(chunk_mm, c - (SLOTS - 1))
                nc.scalar.activation(wh[:, slot, :], raw[:, slot, :], ACT.Copy).then_inc(chunk_hi, 1)

            def after(c0, n=1, i=None, step=0):
                for c in range(c0, c0 + n):
                    if c + SLOTS < NCHUNK:
                        high(chunk(c + SLOTS, i, step))

            def square(m, d):
                if d >= 2:
                    act.wait_ge(sq_sum, m * (KT - 1) + max(1, d - 2))
                nc.scalar.activation(sq[:, d % 2, :], x[:, d, :], ACT.Square).then_inc(sq_ready, 1)

            def root(m):
                act.wait_ge(ss_mm, m + 1)
                nc.scalar.activation(std[:, 0, :], ps[:, 6, :], ACT.Sqrt, bias=eps[:, 0:1],
                                     scale=1.0 / D).then_inc(std_ready, 1)

            def norm_later(m):
                for d in range(KT):
                    act.wait_ge(x_ready, m * KT + d + 1)
                    nc.scalar.activation(xh[:, d, :], x[:, d, :], ACT.Copy, scale=gain[:, m, d:d + 1]).then_inc(xh_ready, 1)
                    square(m, d)

            def norm(m):
                for d in range(KT):
                    act.wait_ge(x_ready, m * KT + d + 1)
                    square(m, d)
                root(m)
                for d in range(KT):
                    act.wait_ge(xt_ready, (KT if m > 1 else 0) + d + 1)
                    nc.scalar.activation(xh[:, d, :], sq[:, d % 2, :], ACT.Copy).then_inc(xh_ready, 1)

            def ffn(m, last=False):
                c0, u0 = C_FFN[m], m * FT
                root((0, 2, 3, 5)[m])
                with act.Fori(0, FT // 2) as i:
                    for k in range(2):
                        after(c0 + 2 * k, 2, i, 4)
                        act.wait_ge(a_scaled, i * 2 + (u0 + k + 1))
                        nc.scalar.activation(uf[:, k, :], uf[:, k, :], ACT.Silu).then_inc(silu_ready, 1)
                (wide_last if last else wide)(c0 + UP, FT)

            def wide(c0, n):
                with act.Fori(0, n // 4) as i:
                    for k in range(4):
                        after(c0 + k, 1, i, 4)
                for c in range(c0 + n // 4 * 4, c0 + n):
                    after(c)

            def wide_last(c0, n):
                m = (n - SLOTS) // 4
                with act.Fori(0, m) as i:
                    for k in range(4):
                        high(chunk(c0 + k + SLOTS, i, 4))
                for c in range(c0 + 4 * m, c0 + n - SLOTS):
                    high(chunk(c + SLOTS))

            act.wait_ge(consts_set, 3)
            for c in range(SLOTS):
                high(chunk(c), first=True)
            act.wait_ge(consts_in, 16 * 5)
            norm_later(0)
            ffn(0)
            norm(1)

            def ret_qk(c0, i=None, step=0):
                after(c0, 4, i, step)

            def ret_main(h, c0, i=None, step=0):
                after(c0, 4, i, step)
                for k in range(2):
                    c = chunk(c0 + 4 + 2 * k, i, step)[0]
                    act.wait_ge(chunk_mm, c + 2)
                    for ab in range(2):
                        nc.scalar.activation(sg[:, 2 * k + ab, :], ps[:, 2 * k + ab, :],
                                             ACT.Sigmoid).then_inc(sig_ready, 1)
                    after(c0 + 4 + 2 * k, 2, i, step)
                act.wait_ge(pv_mm, h + 1)
                for v in range(4):
                    nc.scalar.activation(osq[v], ps[:, 4 + v, :], ACT.Square).then_inc(osq_ready, 1)

            def ret_std(h):
                act.wait_ge(oss_mm, h + 1)
                nc.scalar.activation(std[:, 0, :], ps[:, 4, :], ACT.Sqrt, bias=eps[:, 0:1],
                                     scale=1.0 / DV).then_inc(ostd_ready, 1)

            ret_qk(C_RET)
            with act.Fori(0, RH - 1) as h:
                ret_main(h, C_RET + 4, h, 16)
                after(C_RET + 12, 2, h, 16)
                ret_std(h)
                after(C_RET + 14, 6, h, 16)
            ret_main(RH - 1, C_RET + 52)
            ret_std(RH - 1)
            after(C_RET + 60, 4)
            norm_later(2)
            ffn(1)
            norm_later(3)
            ffn(2)
            norm(4)

            HN_BANK = (0, 0, 0, 2, 0, 2)

            def head_sq(n, c):
                act.wait_ge(chunk_mm, c + 2)
                if n >= 1:
                    act.wait_ge(hss_mm, n)
                for ab in range(2):
                    nc.scalar.activation(sq[:, ab, :], ps[:, HN_BANK[n] + ab, :], ACT.Square).then_inc(hsq_ready, 1)
                after(c, 2)

            def head_std(n):
                act.wait_ge(hss_mm, n + 1)
                if n >= 1:
                    act.wait_ge(hn_ready, n)
                b = 4 + 2 * (n % 2)
                nc.scalar.activation(std[:, :, :], ps[:, b:b + 2, :], ACT.Sqrt, bias=eps[:, 0:1],
                                     scale=1.0 / DH).then_inc(hstd_ready, 1)

            def gelu(j, c):
                after(c, 4)
                act.wait_ge(chunk_mm, c + 4)
                nc.scalar.activation(gl[:, j, :, :], ps[:, 2:4, 0:GN], ACT.Gelu_apprx_tanh).then_inc(gelu_ready, 1)

            c0 = C_NSA
            after(c0, 4)
            head_sq(0, c0 + 4)
            gelu(0, c0 + 6)
            head_std(0)
            head_sq(1, c0 + 10)
            gelu(1, c0 + 12)
            head_std(1)
            head_sq(2, c0 + 16)
            head_sq(3, c0 + 18)
            head_std(2)
            head_sq(4, c0 + 20)
            head_std(3)
            head_sq(5, c0 + 22)
            head_std(4)
            act.wait_ge(gate_mm, 1)
            g = ps[:, 0, 0:TT * 48].rearrange("p (i b h) -> p i b h", i=TT, b=3)
            for b, gb in ((SLC, 1), (WIN, 2), (CMPB, 0)):
                nc.scalar.activation(gates[:, :, :, b].rearrange("p h i -> p i h"), g[:, :, gb, :],
                                     ACT.Sigmoid).then_inc(sig_ready, 1)
            head_std(5)
            act.wait_ge(w2_mm, 1)
            nc.scalar.activation(kct[:, 0, :], ps[0:DH, 1, 0:GN], ACT.Square).then_inc(kcsq_ready, 1)
            after(c0 + 24, 4)
            act.wait_ge(kcss_mm, 1)
            nc.scalar.activation(kct[:, 1, :], ps[0:DH, 3, 0:GN], ACT.Sqrt, bias=eps[0:DH, 0:1],
                                 scale=1.0 / DH).then_inc(kcstd_ready, 1)

            def exp(h, b, k):
                o, n = p_slice(k % 3, k // 3)
                act.wait_ge(sc_read, h * NS + k + 1)
                nc.scalar.activation(pr[:, b, o:o + n], pr[:, b, o:o + n], ACT.Exp, bias=mn[:, b, k:k + 1],
                                     scale=-1.0, accum_out=rsum[:, b, k:k + 1]).then_inc(exp_done, 1)

            def pt_high(h, hh, k):
                t = hh * NTT + k
                act.wait_ge(pt_mm, h * NTT + k + 1)
                if not (isinstance(h, int) and h == 0 and k < 2):
                    act.wait_ge(apv_mm, h * NTT + k - 1)
                np_, n = (NCP, T) if k == 8 else (P, T - P * (k % 4))
                nc.scalar.activation(pth[0:np_, t % 2, 0:n], ps[0:np_, 3 + t % 3, 0:n], ACT.Copy).then_inc(pt_hi, 1)

            def o_copy(h, hh):
                s = DH * (hh % 2)
                act.wait_ge(apv_mm, (h + 1) * NTT)
                if not (isinstance(h, int) and h == 0):
                    act.wait_ge(o_ready, h)
                nc.scalar.activation(sq[s:s + DH, 0, :], ps[DH:P, 6 + hh % 2, :], ACT.Copy).then_inc(o_half, 1)

            def step_of(h, hh, more=True):
                for k in range(NS):
                    if more:
                        exp(h + 1, (hh + 1) % 2, k)
                    if k == O_AT and not (isinstance(h, int) and h == 0):
                        o_copy(h - 1, (hh + 1) % 2)
                    if k >= LAG:
                        pt_high(h, hh, k - LAG)

            for k in range(NS):
                exp(0, 0, k)
            for hh in range(HPG):
                step_of(hh, hh)
            with act.Fori(1, NG - 1) as g4:
                for hh in range(HPG):
                    step_of(g4 * HPG + hh, hh)
            for hh in range(HPG):
                step_of(NH - HPG + hh, hh, more=hh < HPG - 1)
            o_copy(NH - 1, HPG - 1)
            after(C_NOUT, 8)
            norm_later(5)
            ffn(3, last=True)

        @block.tensor
        def _(pe):
            mm = nc.tensor.matmul

            def tall(g, parity, chunks, moving, n=T, kpc=4, ready=None):
                last_k = kpc * len(chunks) - 1
                pe.wait_ge(pair_free, g - 1)
                for ci, (c, slot, turn) in enumerate(chunks):
                    pe.wait_ge(chunk_lo, c + 1)
                    for r in range(kpc):
                        k = ci * kpc + r
                        if ready is not None:
                            ready(k)
                        hi, lo = moving(k)
                        for ab in range(2):
                            col = r * 2 * P + ab * P
                            o = ps[:, 2 * parity + ab, 0:n]
                            w_h, w_l = wh[:, slot, col:col + P], wl[:, slot, col:col + P]
                            mm(o, w_h, hi, start=k == 0, stop=False)
                            mm(o, w_h, lo, start=False, stop=False)
                            last = mm(o, w_l, hi, start=False, stop=k == last_k)
                    last.then_inc(chunk_mm, 1)

            def from_x(k):
                return xh[:, k, :], xl[:, k, :]

            def natural(chunks, ready=None):
                for ci, (c, slot, turn) in enumerate(chunks):
                    pe.wait_ge(chunk_lo, c + 1)
                    for r in range(2):
                        k = 2 * ci + r
                        w_h, w_l = wh[:, slot, r * T:(r + 1) * T], wl[:, slot, r * T:(r + 1) * T]
                        for t in range(TT):
                            o = ps[:, 4 + t, :]
                            x_h, x_l = xh[:, k, t * P:(t + 1) * P], xl[:, k, t * P:(t + 1) * P]
                            mm(o, x_h, w_h, start=k == 0, stop=False)
                            mm(o, x_h, w_l, start=False, stop=False)
                            last = mm(o, x_l, w_h, start=False, stop=k == KT - 1)
                    last.then_inc(chunk_mm, 1)

            def wide_chunk(ch, f_h, f_l, order, start, stop):
                c, slot, turn = ch
                pe.wait_ge(chunk_lo, c + 1)
                for d in order:
                    w_h, w_l = wh[:, slot, d * P:(d + 1) * P], wl[:, slot, d * P:(d + 1) * P]
                    mm(ps[:, d, :], w_h, f_h, start=start, stop=False)
                    mm(ps[:, d, :], w_h, f_l, start=False, stop=False)
                    last = mm(ps[:, d, :], w_l, f_h, start=False, stop=stop)
                    if stop and d < KT - 1:
                        last.then_inc(down_mm, 1)
                last.then_inc(chunk_mm, 1)

            def norm(m):
                pe.wait_ge(sq_sum, (m + 1) * (KT - 1))
                mm(ps[:, 6, :], ones[:, :], std[:, 1, :], start=True, stop=True).then_inc(ss_mm, 1)

            def ffn(m):
                c0, g0, u0 = C_FFN[m], G_FFN[m], m * FT
                nm = (0, 2, 3, 5)[m]
                tall(g0, 0, [chunk(c0), chunk(c0 + 1)], from_x, ready=lambda kt: pe.wait_ge(xn_ready, nm * KT + kt + 1))
                norm(nm)
                tall(g0 + 1, 1, [chunk(c0 + 2), chunk(c0 + 3)], from_x)
                with pe.Fori(1, FT // 2) as i:
                    for k in range(2):
                        tall(i * 2 + (g0 + k), k, [chunk(c0 + 2 * k, i, 4), chunk(c0 + 2 * k + 1, i, 4)], from_x)
                cd = c0 + UP
                pe.wait_ge(u_ready, u0 + 1)
                first = list(range(4, 8)) + list(range(4))
                c, slot, turn = chunk(cd)
                pe.wait_ge(chunk_lo, c + 1)
                for d in first:
                    if d == 0:
                        pe.wait_ge(pair_free, g0 + FT)
                    w_h, w_l = wh[:, slot, d * P:(d + 1) * P], wl[:, slot, d * P:(d + 1) * P]
                    mm(ps[:, d, :], w_h, uh[:, 0, :], start=True, stop=False)
                    mm(ps[:, d, :], w_h, ul[:, 0, :], start=False, stop=False)
                    last = mm(ps[:, d, :], w_l, uh[:, 0, :], start=False, stop=False)
                last.then_inc(chunk_mm, 1)
                n = (FT - 2) // 4
                with pe.Fori(0, n) as i:
                    for k in range(4):
                        f = i * 4 + (1 + k)
                        pe.wait_ge(u_ready, f + (u0 + 1))
                        wide_chunk(chunk(cd + 1 + k, i, 4), uh[:, f, :], ul[:, f, :], range(KT), False, False)
                for f in range(1 + 4 * n, FT):
                    pe.wait_ge(u_ready, u0 + f + 1)
                    wide_chunk(chunk(cd + f), uh[:, f, :], ul[:, f, :], range(KT), False, f == FT - 1)

            pe.wait_ge(consts_in, 16 * 5)
            pe.wait_ge(consts_set, 3)
            pe.wait_ge(x_in_landed, 16 * TT)
            for d in range(KT):
                if d >= 4:
                    pe.wait_ge(pair_free, d // 2 - 1)
                for t in range(TT):
                    last = nc.tensor.transpose(ps[:, d % 4, t * P:(t + 1) * P], xin[:, t, d * P:(d + 1) * P], ident)
                last.then_inc(x_turned, 1)
            for k in range(2):
                last = mm(ps[0:NH, 4 + k, 0:REL // 2], relw[:, :], onehot[:, k * (REL // 2):(k + 1) * (REL // 2)],
                          start=True, stop=True)
            last.then_inc(rel_mm, 1)
            ffn(0)
            norm(1)

            def ret_qk_q(g, c0, i=None, step=0, ready=None):
                tall(g, 0, [chunk(c0, i, step), chunk(c0 + 1, i, step)], from_x, ready=ready)

            def ret_qk_k(g, c0, i=None, step=0):
                tall(g, 1, [chunk(c0, i, step), chunk(c0 + 1, i, step)], from_x)

            def ret_main(h, g0, c0, i=None, step=0):
                natural([chunk(c0 + k, i, step) for k in range(4)])
                pe.wait_ge(qk_ready, h * 2 + 2)
                pe.wait_ge(pair_free, g0)
                for j in range(TT):
                    n = T - j * P
                    for half in range(2):
                        k_h, k_l = qkh[:, 1, half, j * P:(j + 1) * P], qkl[:, 1, half, j * P:(j + 1) * P]
                        q_h, q_l = qkh[:, 0, half, j * P:], qkl[:, 0, half, j * P:]
                        mm(ps[:, j, 0:n], k_h, q_h, start=half == 0, stop=False)
                        mm(ps[:, j, 0:n], k_h, q_l, start=False, stop=False)
                        last = mm(ps[:, j, 0:n], k_l, q_h, start=False, stop=half == 1)
                    last.then_inc(s_mm, 1)
                for k in range(2):
                    pe.wait_ge(s_read, h * TT + (2 * k + 2))
                    tall(g0 + k, k, [chunk(c0 + 4 + 2 * k, i, step), chunk(c0 + 5 + 2 * k, i, step)], from_x)
                pe.wait_ge(v_ready, h + 1)
                pe.wait_ge(a_ready, h * TT + TT)
                for j in range(TT):
                    o0 = (0, 512, 896, 1152)[j]
                    n = T - j * P
                    for v in range(4):
                        v_h, v_l = vh[:, j, v * P:(v + 1) * P], vl[:, j, v * P:(v + 1) * P]
                        o = ps[:, 4 + v, j * P:]
                        mm(o, v_h, ah[:, o0:o0 + n], start=j == 0, stop=False)
                        mm(o, v_h, al[:, o0:o0 + n], start=False, stop=False)
                        last = mm(o, v_l, ah[:, o0:o0 + n], start=False, stop=j == TT - 1)
                last.then_inc(pv_mm, 1)

            def ret_ss(h):
                pe.wait_ge(on_ready, h + 1)
                pe.wait_ge(osq_sum, h * 3 + 3)
                mm(ps[:, 4, :], ones[:, :], osq[0], start=True, stop=True).then_inc(oss_mm, 1)

            def ret_out(h, g0, c0, i=None, step=0):
                pe.wait_ge(on_ready, h + 1)
                for k in range(4):
                    tall(g0 + k, k % 2, [chunk(c0 + k, i, step)], lambda v: (onh[:, v, :], onl[:, v, :]))

            ret_qk_q(G_RET, C_RET, ready=lambda kt: pe.wait_ge(xn_ready, KT + kt + 1))
            ret_qk_k(G_RET + 1, C_RET + 2)
            with pe.Fori(0, RH - 1) as h:
                g = h * 8 + (G_RET + 2)
                ret_main(h, g, C_RET + 4, h, 16)
                ret_qk_q(g + 2, C_RET + 12, h, 16)
                ret_ss(h)
                ret_qk_k(g + 3, C_RET + 14, h, 16)
                ret_out(h, g + 4, C_RET + 16, h, 16)
                pe.wait_ge(ostd_ready, h + 1)
            g = G_RET + 2 + 8 * (RH - 1)
            ret_main(RH - 1, g, C_RET + 52)
            ret_ss(RH - 1)
            ret_out(RH - 1, g + 2, C_RET + 60)
            ffn(1)
            ffn(2)
            norm(4)

            def pair(n, c, ready=None):
                tall(G_NSA + n, n % 2, [chunk(C_NSA + c), chunk(C_NSA + c + 1)], from_x, ready=ready)

            def head_ss(n):
                pe.wait_ge(hsq_ready, 2 * n + 2)
                if n >= 2:
                    pe.wait_ge(hstd_ready, n - 1)
                b = 4 + 2 * (n % 2)
                for ab in range(2):
                    last = mm(ps[:, b + ab, :], bones, sq[:, ab, :], start=True, stop=True)
                last.then_inc(hss_mm, 1)

            def compress(j, n, c):
                pe.wait_ge(uc_ready, j + 1)
                tall(G_NSA + n, n % 2, [chunk(C_NSA + c + k) for k in range(4)],
                     lambda l2: (uch[:, l2 * GN:(l2 + 1) * GN], ucl[:, l2 * GN:(l2 + 1) * GN]), n=GN)

            pair(0, 0, ready=lambda kt: pe.wait_ge(xn_ready, 4 * KT + kt + 1))
            pair(1, 2)
            pair(2, 4)
            compress(0, 3, 6)
            head_ss(0)
            pair(4, 10)
            compress(1, 5, 12)
            head_ss(1)
            pair(6, 16)
            pair(7, 18)
            head_ss(2)
            pair(8, 20)
            head_ss(3)
            pair(9, 22)
            head_ss(4)
            pe.wait_ge(gw_ready, 1)
            pe.wait_ge(pair_free, G_NSA + 9)
            for t in range(TT):
                for k in range(KT):
                    o = ps[:, 0, t * 48:(t + 1) * 48]
                    x_h, x_l = xh[:, k, t * P:(t + 1) * P], xl[:, k, t * P:(t + 1) * P]
                    mm(o, x_h, gwh[:, k, :], start=k == 0, stop=False)
                    mm(o, x_h, gwl[:, k, :], start=False, stop=False)
                    last = mm(o, x_l, gwh[:, k, :], start=False, stop=k == KT - 1)
            last.then_inc(gate_mm, 1)
            pe.wait_ge(gelu_ready, 2)
            for g in range(NG):
                for t in range(2):
                    mm(ps[0:NC, 1, P + g * DH:P + (g + 1) * DH], gl[:, 1, t, g * NC:(g + 1) * NC], w2[:, 1, t, :],
                       start=t == 0, stop=t == 1)
            for t in range(2):
                last = mm(ps[0:DH, 1, 0:GN], w2[:, 0, t, :], gl[:, 0, t, :], start=t == 0, stop=t == 1)
            last.then_inc(w2_mm, 1)
            head_ss(5)
            pe.wait_ge(hstd_ready, 6)
            natural([chunk(C_NSA + 24 + k) for k in range(4)])
            pe.wait_ge(kcsq_ready, 1)
            pe.wait_ge(pair_free, G_NSA + 10)
            mm(ps[0:DH, 3, 0:GN], ones[0:DH, 0:DH], kct[:, 0, :], start=True, stop=True).then_inc(kcss_mm, 1)

            def score(h, g, b, k):
                ti, br = k // 3, k % 3
                if not (isinstance(h, int) and h == 0 and k < 3):
                    pe.wait_ge(sc_read, h * NS + (k - 2))
                q = qs[:, b, ti * P:(ti + 1) * P]
                n = p_slice(br, ti)[1]
                if br == CMPB:
                    n += 1
                    m_h, m_l = kch[:, g, 0:n], kcl[:, g, 0:n]
                else:
                    m_h, m_l = kh[:, br, g, 0:n], kl[:, br, g, 0:n]
                o = ps[:, k % 3, 0:n]
                mm(o, q, m_h, start=True, stop=False)
                mm(o, q, m_l, start=False, stop=True).then_inc(sc_mm, 1)

            def turn(h, hh, k):
                t, b = hh * NTT + k, hh % 2
                if not (isinstance(h, int) and h == 0 and k < 3):
                    pe.wait_ge(pt_ready, h * NTT + (k - 2))
                for ti in range(0 if k == 8 else k % 4, TT):
                    po = p_slice(CMPB if k == 8 else k // 4, ti)[0]
                    if k == 8:
                        last = nc.tensor.transpose(ps[0:NCP, 3 + t % 3, ti * P:(ti + 1) * P],
                                                   pr[:, b, po:po + NCP], ident)
                    else:
                        j = k % 4
                        last = nc.tensor.transpose(ps[:, 3 + t % 3, (ti - j) * P:(ti - j + 1) * P],
                                                   pr[:, b, po + j * P:po + (j + 1) * P], ident)
                last.then_inc(pt_mm, 1)

            def values(h, hh, k):
                t, o = hh * NTT + k, ps[:, 6 + hh % 2, :]
                pe.wait_ge(pt_ready, h * NTT + k + 1)
                if k == 8:
                    mm(o, vcst[:, :], pth[0:NCP, t % 2, :], start=False, stop=False)
                    last = mm(o, vcst[:, :], ptl[0:NCP, t % 2, :], start=False, stop=True)
                else:
                    j, br = k % 4, k // 4
                    n = T - j * P
                    mm(o[:, j * P:], vst[:, j, br, :], pth[:, t % 2, 0:n], start=k == 0, stop=False)
                    last = mm(o[:, j * P:], vst[:, j, br, :], ptl[:, t % 2, 0:n], start=False, stop=False)
                last.then_inc(apv_mm, 1)

            def step_of(h, hh, g, more=True):
                if more:
                    pe.wait_ge(qs_ready, h + 2)
                for k in range(NS):
                    if more:
                        score(h + 1, g + (hh + 1) // HPG, (hh + 1) % 2, k)
                    t = k - LAG
                    if t >= 0:
                        if t % 4 == 0:
                            pe.wait_ge(p_scaled, h * NS + (t + 4))
                        turn(h, hh, t)
                        if t == 2:
                            if hh == 0:
                                pe.wait_ge(vst_ready, g + 1)
                            if not (isinstance(h, int) and h < 2):
                                pe.wait_ge(o_ready, h - 1)
                        if t >= 2:
                            values(h, hh, t - 2)
                values(h, hh, 7)
                values(h, hh, 8)

            pe.wait_ge(cmp_ready, 3)
            pe.wait_ge(qs_ready, 1)
            for k in range(NS):
                score(0, 0, 0, k)
            for hh in range(HPG):
                step_of(hh, hh, 0)
            with pe.Fori(1, NG - 1) as g4:
                for hh in range(HPG):
                    step_of(g4 * HPG + hh, hh, g4)
            for hh in range(HPG):
                step_of(NH - HPG + hh, hh, NG - 1, more=hh < HPG - 1)
            pe.wait_ge(sc_read, NH * NS)
            for f in range(8):
                pe.wait_ge(o_ready, NH if f == 0 else 2 * f + 2)
                wide_chunk(chunk(C_NOUT + f), xh[:, f, :], xl[:, f, :], range(KT), f == 0, f == 7)
            ffn(3)
            pe.wait_ge(x_ready, 7 * KT)
            for t in range(TT):
                for q in range(2):
                    n = 2 * t + q
                    if n >= 4:
                        pe.wait_ge(y_ready, 4 * (n - 3))
                    for r in range(4):
                        d = 4 * q + r
                        last = nc.tensor.transpose(ps[:, n % 4, r * P:(r + 1) * P], x[:, d, t * P:(t + 1) * P], ident)
                    last.then_inc(y_mm, 1)

        @block.vector
        def _(dve):
            V = nc.vector

            class Steps:
                n, i, per, start = 0, None, 0, 0

                def __call__(self, ins):
                    ins.then_inc(dve_step, 1)
                    self.n += 1
                    dve.wait_ge(dve_step, self.n if self.i is None else self.i * self.per + self.n)

                def loop(self, i, per, first=0):
                    self.i, self.per, self.start = i, per, self.n
                    self.n -= first * per

                def end(self, count, first=0):
                    assert self.n + first * self.per - self.start == self.per, (self.n + first * self.per - self.start, self.per)
                    self.i, self.n = None, self.start + self.per * count

            step = Steps()

            def split(hi, lo, src):
                step(V.tensor_copy(hi, src))
                return V.tensor_tensor(lo, src, hi.bitcast(F32), ALU.subtract)

            def invert(m):
                dve.wait_ge(std_ready, m + 1)
                step(V.reciprocal(std[:, 0, :], std[:, 0, :]))

            def norm(m):
                m0 = KT if m > 1 else 0
                invert(m)

                def low(d):
                    dve.wait_ge(xh_ready, m * KT + d + 1)
                    V.tensor_tensor(xl[:, d, :], sq[:, d % 2, :], xh[:, d, :].bitcast(F32),
                                    ALU.subtract).then_inc(xn_ready, 1)
                    dve.wait_ge(xn_ready, m * KT + d + 1)

                for d in range(KT):
                    V.scalar_tensor_tensor(sq[:, d % 2, :], x[:, d, :], gain[:, m, d:d + 1], std[:, 0, :],
                                           ALU.mult, ALU.mult).then_inc(xt_ready, 1)
                    if d:
                        low(d - 1)
                low(KT - 1)

            def gained_low(m, d):
                dve.wait_ge(xh_ready, m * KT + d + 1)
                V.scalar_tensor_tensor(xl[:, d, :], x[:, d, :], gain[:, m, d:d + 1], xh[:, d, :].bitcast(F32),
                                       ALU.mult, ALU.subtract).then_inc(xn_ready, 1)

            def residual(n, c_last, scale, m=None):
                for d in range(KT):
                    if d < KT - 1:
                        dve.wait_ge(down_mm, n * (KT - 1) + d + 1)
                    else:
                        dve.wait_ge(chunk_mm, c_last + 1)
                    V.scalar_tensor_tensor(x[:, d, :], ps[:, d, :], scale, x[:, d, :], ALU.mult,
                                           ALU.add).then_inc(x_ready, 1)
                    if m is not None and d:
                        gained_low(m, d - 1)
                if m is not None:
                    gained_low(m, KT - 1)

            def ffn(m, after=None):
                c0, u0 = C_FFN[m], m * FT
                invert((0, 2, 3, 5)[m])
                with dve.Fori(0, FT // 2) as i:
                    step.loop(i, 4)
                    for k in range(2):
                        f = i * 2 + k
                        dve.wait_ge(chunk_mm, i * 4 + (c0 + 2 * k + 2))
                        V.tensor_tensor(uf[:, k, :], ps[:, 2 * k, :], std[:, 0, :], ALU.mult).then_inc(a_scaled, 1)
                        V.tensor_tensor(bf[:, k, :], ps[:, 2 * k + 1, :], std[:, 0, :], ALU.mult).then_inc(pair_free, 1)
                        dve.wait_ge(pair_free, f + (G_FFN[m] + 1))
                        dve.wait_ge(silu_ready, f + (u0 + 1))
                        step(V.tensor_tensor(bf[:, k, :], uf[:, k, :], bf[:, k, :], ALU.mult))
                        split(uh[:, f, :], ul[:, f, :], bf[:, k, :]).then_inc(u_ready, 1)
                        dve.wait_ge(u_ready, f + (u0 + 1))
                    step.end(FT // 2)
                residual((0, 1, 2, 4)[m], C_FFN[m] + UP + DOWN - 1, 0.5, after)

            V.memset(ones[:, :], 1.0).then_inc(consts_set, 1)
            V.memset(eps[:, :], EPS).then_inc(consts_set, 1)
            V.memset(relw[BUCKETS:BUCKETS + 1, :], BIG).then_inc(consts_set, 1)
            dve.wait_ge(consts_in, 16 * 5)
            for d in range(KT):
                dve.wait_ge(x_turned, d + 1)
                V.tensor_copy(x[:, d, :], ps[:, d % 4, :]).then_inc(x_ready, 1)
                dve.wait_ge(x_ready, d + 1)
                if d % 2:
                    V.memset(mark[:, 0:1], 0.0).then_inc(pair_free, 1)
                if d:
                    gained_low(0, d - 1)
            gained_low(0, KT - 1)
            dve.wait_ge(rel_mm, 1)
            for k in range(2):
                step(V.tensor_copy(relo[:, k * (REL // 2):(k + 1) * (REL // 2)], ps[0:NH, 4 + k, 0:REL // 2]))
            step(V.tensor_scalar(qkg[:, 0:1], qkg[:, 0:1], -(DH ** -0.5), None, ALU.mult))
            V.memset(mark[:, 0:1], 0.0).then_inc(rel_out, 1)
            dve.wait_ge(rel_stored, 16)
            ffn(0)
            norm(1)

            def rotate(h, c_end, which):
                b = 2 * which
                dve.wait_ge(chunk_mm, c_end)
                V.tensor_tensor(rt[:, 0, :], ps[:, b, :], rot[:, 0, :], ALU.mult)
                V.tensor_tensor(rt[:, 1, :], ps[:, b + 1, :], rot[:, 1, :], ALU.mult)
                V.tensor_tensor(rt[:, 2, :], ps[:, b, :], rot[:, 1, :], ALU.mult)
                step(V.tensor_tensor(rt[:, 3, :], ps[:, b + 1, :], rot[:, 0, :], ALU.mult))
                V.tensor_tensor(qf[:, 0, :], rt[:, 0, :], rt[:, 1, :], ALU.subtract).then_inc(pair_free, 1)
                step(V.tensor_tensor(qf[:, 1, :], rt[:, 2, :], rt[:, 3, :], ALU.add))
                split(qkh[:, which, :, :], qkl[:, which, :, :], qf[:, :, :]).then_inc(qk_ready, 1)

            def ret_values(h, c_end):
                dve.wait_ge(chunk_mm, c_end)
                for t in range(TT):
                    step(V.tensor_copy(vh[:, t, :], ps[:, 4 + t, :]))
                    last = V.tensor_tensor(vl[:, t, :], ps[:, 4 + t, :], vh[:, t, :].bitcast(F32), ALU.subtract)
                last.then_inc(v_ready, 1)

            def ret_main(h, c0, g0, i=None, n=0):
                ret_values(h, chunk(c0, i, 16)[0] + 4)
                for j in range(TT):
                    o0, w = (0, 512, 896, 1152)[j], T - j * P
                    dve.wait_ge(s_mm, h * TT + (j + 1))
                    V.tensor_tensor(af[:, o0:o0 + w], ps[:, j, 0:w], dec[:, h, 0:w], ALU.mult).then_inc(s_read, 1)
                for j in range(TT):
                    o0, w = (0, 512, 896, 1152)[j], T - j * P
                    dve.wait_ge(s_read, h * TT + (j + 1))
                    split(ah[:, o0:o0 + w], al[:, o0:o0 + w], af[:, o0:o0 + w]).then_inc(a_ready, 1)
                for k in range(4):
                    dve.wait_ge(sig_ready, h * 4 + (k + 1))
                    ins = V.tensor_tensor(sg[:, k, :], sg[:, k, :], ps[:, k, :], ALU.mult)
                    if k % 2:
                        ins.then_inc(pair_free, 1)
                    else:
                        step(ins)

            def ret_outputs(h, g_done):
                dve.wait_ge(pair_free, g_done)
                for v in range(4):
                    dve.wait_ge(osq_ready, h * 4 + (v + 1))
                    step(V.tensor_tensor(onf[:, v, :], ps[:, 4 + v, :], sg[:, v, :], ALU.mult))
                    last = split(onh[:, v, :], onl[:, v, :], onf[:, v, :])
                last.then_inc(on_ready, 1)
                dve.wait_ge(on_ready, h + 1)

            def ret_invert(h):
                dve.wait_ge(ostd_ready, h + 1)
                step(V.reciprocal(std[:, 0, :], std[:, 0, :]))

            def ret_residual(c0, i=None, last=False):
                r = std[:, 0, :]
                twice = bass.AP(r.tensor, r.offset, [list(r.ap[0]), [0, 2], [1, T]])
                for k in range(4):
                    b = 2 * (k % 2)
                    dve.wait_ge(chunk_mm, chunk(c0 + k, i, 16)[0] + 1)
                    step(V.tensor_tensor(rt[:, b:b + 2, :], ps[:, b:b + 2, :], twice, ALU.mult))
                    ins = V.tensor_tensor(x[:, 2 * k:2 * k + 2, :], x[:, 2 * k:2 * k + 2, :], rt[:, b:b + 2, :], ALU.add)
                    if not last:
                        ins.then_inc(pair_free, 1)
                    else:
                        ins.then_inc(x_ready, 2)
                        dve.wait_ge(x_ready, 2 * KT + 2 * k + 2)
                        V.memset(mark[:, 0:1], 0.0).then_inc(pair_free, 1)
                        if k:
                            gained_low(2, 2 * k - 2)
                            gained_low(2, 2 * k - 1)
                if last:
                    gained_low(2, KT - 2)
                    gained_low(2, KT - 1)

            dve.wait_ge(ret_in, 32)
            rotate(0, C_RET + 2, 0)
            rotate(0, C_RET + 4, 1)
            with dve.Fori(0, RH - 1) as h:
                step.loop(h, 4 + 4 + 2 + 8 + 3 + 1 + 3 + 4)
                g = h * 8 + (G_RET + 2)
                ret_main(h, C_RET + 4, g, h)
                ret_outputs(h, g + 2)
                rotate(h + 1, h * 16 + (C_RET + 14), 0)
                ret_invert(h)
                rotate(h + 1, h * 16 + (C_RET + 16), 1)
                ret_residual(C_RET + 16, h)
                step.end(RH - 1)
            ret_main(RH - 1, C_RET + 52, 0)
            ret_outputs(RH - 1, G_RET + 4 + 8 * (RH - 1))
            ret_invert(RH - 1)
            ret_residual(C_RET + 60, last=True)
            ffn(1, after=3)
            ffn(2)
            norm(4)

            for j in range(2):
                dve.wait_ge(chunk_mm, C_NSA + 2 * j + 2)
                for g in range(NG):
                    for par in range(2):
                        s = DH * (g % 2)
                        src = ps[s:s + DH, 2 * j + g // 2, :].rearrange("d (t two) -> d t two", two=2)[:, :, par]
                        ins = V.tensor_copy(z[DH * par:DH * (par + 1), j, g, :], src)
                        if (g, par) != (NG - 1, 1):
                            step(ins)
                ins.then_inc(pair_free, 1)

            def head_copy(n):
                dve.wait_ge(hsq_ready, 2 * n + 2)
                b = (0, 0, 0, 2, 0, 2)[n]
                dst = kn[:, 2 * n:2 * n + 2, :] if n < 2 else qn[:, 2 * (n - 2):2 * (n - 2) + 2, :]
                step(V.tensor_copy(dst, ps[:, b:b + 2, :]))
                V.memset(mark[:, 0:1], 0.0).then_inc(pair_free, 1)
                dve.wait_ge(pair_free, G_NSA + (3, 5, 7, 8, 9, 10)[n])

            def head_norm(n):
                dst = kn[:, 2 * n:2 * n + 2, :] if n < 2 else qn[:, 2 * (n - 2):2 * (n - 2) + 2, :]
                dve.wait_ge(hstd_ready, n + 1)
                step(V.reciprocal(std[:, :, :], std[:, :, :]))
                col = 0 if n >= 2 else 2 + n
                V.scalar_tensor_tensor(dst, dst, qkg[:, col:col + 1], std[:, :, :], ALU.mult,
                                       ALU.mult).then_inc(hn_ready, 1)
                if n < 2:
                    dve.wait_ge(hn_ready, n + 1)
                    for g in range(NG):
                        s = DH * (g % 2)
                        src = kn[s:s + DH, 2 * n + g // 2, :]
                        for half in (DH - s, s):
                            step(V.tensor_copy(kh[half:half + DH, n, g, :], src))
                        for half in (0, DH):
                            step(V.tensor_tensor(kl[half:half + DH, n, g, :], src,
                                                 kh[s:s + DH, n, g, :].bitcast(F32), ALU.subtract))

            dve.wait_ge(ret_in, 80)
            step(V.tensor_copy(gwh[:, :, :], gwf[:, :, :]))
            V.tensor_tensor(gwl[:, :, :], gwf[:, :, :], gwh[:, :, :].bitcast(F32), ALU.subtract).then_inc(gw_ready, 1)
            def blocks(j):
                zz = z[:, j, :, :]
                src = bass.AP(zz.tensor, zz.offset, [list(zz.ap[0]), [1, LP], [T // 2, NG], [CMP_STRIDE // 2, NC]])
                pp = pos[:, j, :]
                add = bass.AP(pp.tensor, pp.offset, [list(pp.ap[0]), [1, LP], [0, NG], [0, NC]])
                dst = u[:, 0:LP * GN].rearrange("p (l g n) -> p l g n", l=LP, g=NG)
                step(V.tensor_tensor(dst, src, add, ALU.add))
                split(uch[:, :], ucl[:, :], u[:, 0:LP * GN]).then_inc(uc_ready, 1)

            def hidden_out(j):
                dve.wait_ge(gelu_ready, j + 1)
                V.memset(mark[:, 0:1], 0.0).then_inc(pair_free, 1)
                dve.wait_ge(pair_free, G_NSA + (4, 6)[j])

            blocks(0)
            dve.wait_ge(uc_ready, 1)
            head_copy(0)
            hidden_out(0)
            head_norm(0)
            blocks(1)
            dve.wait_ge(uc_ready, 2)
            head_copy(1)
            hidden_out(1)
            head_norm(1)
            head_copy(2)
            head_copy(3)
            head_norm(2)
            head_copy(4)
            head_norm(3)
            head_copy(5)
            head_norm(4)
            head_norm(5)
            dve.wait_ge(sig_ready, 16 + 3)
            gm = gates[:, :, 0, CMPB]
            V.tensor_scalar(gm, gm, rowmask, None, ALU.mult).then_inc(gates_set, 1)
            dve.wait_ge(hn_ready, 6)
            step(V.tensor_copy(qs[0:DH, 0, :], qn[0:DH, 0, :]))
            V.tensor_tensor(qs[DH:P, 0, :], qn[0:DH, 0, :], qs[0:DH, 0, :].bitcast(F32), ALU.subtract).then_inc(qs_ready, 1)
            step(V.tensor_copy(qs[DH:P, 1, :], qn[DH:P, 0, :]))
            V.tensor_tensor(qs[0:DH, 1, :], qn[DH:P, 0, :], qs[DH:P, 1, :].bitcast(F32), ALU.subtract).then_inc(qs_ready, 1)
            dve.wait_ge(chunk_mm, C_NSA + 28)
            for t in range(TT):
                step(V.tensor_copy(vf[:, t, :, :, :].rearrange("p b g d -> p (b g d)"), ps[:, 4 + t, :]))
            dve.wait_ge(w2_mm, 1)
            dve.wait_ge(kcstd_ready, 1)
            step(V.memset(vcf[:, :, :], 0.0))
            step(V.tensor_copy(vcf[0:NC, :, :], ps[0:NC, 1, P:P + NG * DH].rearrange("n (g d) -> n g d", g=NG)))
            step(V.memset(u[:, 3 * P * 4:3 * P * 4 + NG * NCP], 0.0))
            zero = u[:, 3 * P * 4:3 * P * 4 + NG * NCP].rearrange("p (g n) -> p g n", g=NG)
            step(V.tensor_copy(kch[:, :, :], zero))
            step(V.tensor_copy(kcl[:, :, :], zero))
            step(V.reciprocal(kct[:, 1, :], kct[:, 1, :]))
            step(V.scalar_tensor_tensor(kcf, ps[0:DH, 1, 0:GN], qkg[0:DH, 1:2], kct[:, 1, :], ALU.mult, ALU.mult))
            ksrc = kcf.rearrange("p (g n) -> p g n", g=NG)
            for half in (0, DH):
                step(V.tensor_copy(kch[half:half + DH, :, 0:NC], ksrc))
            for half in (0, DH):
                step(V.tensor_tensor(kcl[half:half + DH, :, 0:NC], ksrc, kch[0:DH, :, 0:NC].bitcast(F32), ALU.subtract))
            V.memset(mark[:, 0:1], 0.0).then_inc(cmp_ready, 1)
            for b in range(2):
                V.memset(pr[:, b, 2 * PB:PW], 0.0).then_inc(cmp_ready, 1)

            def stage_q(h, tile, hh, b):
                s = DH * (hh % 2)
                src = qn[s:s + DH, tile, :]
                step(V.tensor_copy(qs[s:s + DH, b, :], src))
                V.tensor_tensor(qs[DH - s:P - s, b, :], src, qs[s:s + DH, b, :].bitcast(F32),
                                ALU.subtract).then_inc(qs_ready, 1)

            def stage_v(g):
                src = vf[:, :, :, g, :].rearrange("p t b d -> p (t b) d")
                vv = vst[:, :, :, :].rearrange("p t b d -> p (t b) d")
                step(V.tensor_copy(vv[:, :, 0:DH], src))
                step(V.tensor_tensor(vv[:, :, DH:2 * DH], src, vv[:, :, 0:DH].bitcast(F32), ALU.subtract))
                step(V.tensor_copy(vcst[:, 0:DH], vcf[:, g, :]))
                V.tensor_tensor(vcst[:, DH:2 * DH], vcf[:, g, :], vcst[:, 0:DH].bitcast(F32),
                                ALU.subtract).then_inc(vst_ready, 1)

            def read_score(h, b, k):
                ti, br = k // 3, k % 3
                o, n = p_slice(br, ti)
                c, st = (ti * P + P - CMP_LEN, CMP_STRIDE) if br == CMPB else (ti * P + P - 1, 1)
                t = tn[:, b, c:c + 1]
                bias = bass.AP(t.tensor, t.offset, [list(t.ap[0]), [-st, n]])
                dve.wait_ge(sc_mm, h * NS + k + 1)
                V.memset(mark[:, k + 1:k + 2], 0.0)
                V.tensor_tensor_reduce(out=pr[:, b, o:o + n], in0=ps[:, k % 3, 0:n], in1=bias, scale=1.0,
                                       scalar=3e38, op0=ALU.add, op1=ALU.min,
                                       accum_out=mn[:, b, k:k + 1]).then_inc(sc_read, 1)

            def coefficients(h, b):
                dve.wait_ge(exp_done, (h + 1) * NS)
                step(V.reciprocal(coef[:, b, :], rsum[:, b, :]))
                V.tensor_tensor(coef[:, b, :], coef[:, b, :], gates[:, h, :, :].rearrange("p i b -> p (i b)"),
                                ALU.mult).then_inc(coef_ready, 1)

            def pt_low(h, hh, k):
                t = hh * NTT + k
                dve.wait_ge(pt_hi, h * NTT + k + 1)
                np_, n = (NCP, T) if k == 8 else (P, T - P * (k % 4))
                V.tensor_tensor(ptl[0:np_, t % 2, 0:n], ps[0:np_, 3 + t % 3, 0:n],
                                pth[0:np_, t % 2, 0:n].bitcast(F32), ALU.subtract).then_inc(pt_ready, 1)

            def o_out(h, tile, hh):
                s = DH * (hh % 2)
                dve.wait_ge(o_half, h + 1)
                step(V.tensor_tensor(sq[s:s + DH, 1, :], ps[0:DH, 6 + hh % 2, :], sq[s:s + DH, 0, :], ALU.add))
                split(xh[s:s + DH, tile, :], xl[s:s + DH, tile, :], sq[s:s + DH, 1, :]).then_inc(o_ready, 1)

            def step_of(h, hh, g, more=True):
                first = isinstance(h, int) and h == 0
                if more:
                    dve.wait_ge(bias_landed[(hh + 1) % 2], (g * 2 + (hh + 1) // 2) * 16 + 16)
                for k in range(NS):
                    if more:
                        read_score(h + 1, (hh + 1) % 2, k)
                    if k == O_AT:
                        if not first:
                            o_out(h - 1, g * 2 + (hh - 1) // 2, (hh + 1) % 2)
                        if hh == 0:
                            if not first:
                                dve.wait_ge(o_ready, h)
                            stage_v(g)
                    if k == O_AT + 1 and (more and not (hh == HPG - 2 and isinstance(g, int) and g == NG - 1)):
                        n = hh + 2
                        stage_q(h + 2, g * 2 + n // 2, n % 2, n % 2)
                    if k >= LAG:
                        pt_low(h, hh, k - LAG)
                if more:
                    coefficients(h + 1, (hh + 1) % 2)

            dve.wait_ge(cmp_ready, 3)
            dve.wait_ge(bias_landed[0], 16)
            for k in range(NS):
                read_score(0, 0, k)
            coefficients(0, 0)
            for hh in range(HPG):
                step_of(hh, hh, 0)
            with dve.Fori(1, NG - 1) as g4:
                step.loop(g4, 3 + 4 * HPG, 1)
                for hh in range(HPG):
                    step_of(g4 * HPG + hh, hh, g4)
                step.end(NG - 2, 1)
            for hh in range(HPG):
                step_of(NH - HPG + hh, hh, NG - 1, more=hh < HPG - 1)
            o_out(NH - 1, NH // 2 - 1, HPG - 1)
            residual(3, C_FFN[3] - 1, 1.0, 5)
            ffn(3)
            for t in range(TT):
                for q in range(2):
                    n = 2 * t + q
                    dve.wait_ge(y_mm, n + 1)
                    V.tensor_copy(xin[:, t, q * T:(q + 1) * T], ps[:, n % 4, :]).then_inc(y_ready, 4)


def constants():
    sq = np.zeros((P, 2 * P + 1), np.float32)
    sq[:, 0:P] = np.eye(P)
    sq[0:64, P:P + 64] = 1
    sq[64:P, P + 64:2 * P] = 1
    sq[:, 2 * P] = np.arange(P) >= CMP_LEN - 1
    half = DK // 2
    inv = np.float32(10000.0) ** (-np.arange(half, dtype=np.float32) / np.float32(half))
    ang = (np.arange(T, dtype=np.float32)[None, :] * inv[:, None]).astype(np.float32)
    rot = np.stack([np.cos(ang), np.sin(ang)], 1).astype(np.float32)
    lg = np.log(1.0 - 2.0 ** (-5.0 - np.arange(RH, dtype=np.float64)))
    diff = np.arange(T)[None, None, :] - np.arange(P)[:, None, None]
    dec = np.where(diff >= 0, np.exp(lg[None, :, None] * np.maximum(diff, 0)) * DK ** -0.5, 0.0).astype(np.float32)
    dist = np.arange(REL) - P
    n = np.maximum(dist, 0)
    nf = np.maximum(n, 16).astype(np.float32)
    large = 16 + (np.log(nf / np.float32(16)) / np.float32(np.log(8.0)) * np.float32(16)).astype(np.int32)
    bucket = np.where(n < 16, n, np.minimum(large, 31))
    onehot = np.zeros((BUCKETS + 1, REL), np.float32)
    onehot[bucket[dist >= 0], np.arange(REL)[dist >= 0]] = -1
    onehot[BUCKETS, dist < 0] = 1
    return sq, rot, dec, onehot


def tall_chunks(w):
    k, n = w.shape
    return w.reshape(k // T, 4, P, n // 256, 256).transpose(3, 0, 2, 1, 4).reshape(-1, P, CW)


def wide_chunks(w):
    return w.reshape(-1, P, CW)


def natural_chunks(w):
    return w.reshape(4, 2, P, T).transpose(0, 2, 1, 3).reshape(-1, P, CW)


def ffn_chunks(gu, down):
    gu = gu.reshape(D, 2, FT, P).transpose(0, 2, 1, 3).reshape(D, 2 * F)
    return [tall_chunks(gu), wide_chunks(down)]


def kernel(**inputs):
    import concourse.bacc as bacc
    from concourse.bass_utils import run_bass_kernel_spmd

    a = {k: np.ascontiguousarray(v) for k, v in inputs.items()}
    gu1, dn1, gu2, dn2 = a["ffn1_w_gu"], a["ffn1_w_down"], a["ffn2_w_gu"], a["ffn2_w_down"]
    win, wout = a["ret_w_in"][0], a["ret_w_out"][0]
    rq = [tall_chunks(win[:, DK * h:DK * (h + 1)]) for h in range(RH)]
    rk = [tall_chunks(win[:, D + DK * h:D + DK * (h + 1)]) for h in range(RH)]
    rv = [natural_chunks(win[:, 2 * D + DV * h:2 * D + DV * (h + 1)]) for h in range(RH)]
    rg = [tall_chunks(win[:, 4 * D + DV * h:4 * D + DV * (h + 1)]) for h in range(RH)]
    ro = [tall_chunks(wout[DV * h:DV * (h + 1)]) for h in range(RH)]
    nin = a["nsa_w_in"][0]
    kc, vc, ks, vs, kw, vw = [nin[:, D + 256 * i:D + 256 * (i + 1)] for i in range(6)]
    parts = ffn_chunks(gu1[0], dn1[0]) + [rq[0], rk[0]]
    for h in range(RH):
        parts += [rv[h], rg[h]] + ([rq[h + 1], rk[h + 1]] if h < RH - 1 else []) + [ro[h]]
    parts += ffn_chunks(gu2[0], dn2[0]) + ffn_chunks(gu1[1], dn1[1])
    w1 = a["nsa_cmp_w1"][0]
    parts += [tall_chunks(w) for w in (kc, vc, ks, w1[0], kw, w1[1], nin[:, 0:D])]
    parts += [natural_chunks(np.concatenate([vs, vw], 1))]
    parts += [wide_chunks(a["nsa_w_out"][0])] + ffn_chunks(gu2[1], dn2[1])
    stream = np.ascontiguousarray(np.concatenate(parts, 0))
    assert stream.shape == (NCHUNK, P, CW)
    norms = [a["ffn1_norm"][0], a["mix_norm"][0], a["ffn2_norm"][0], a["ffn1_norm"][1], a["mix_norm"][1], a["ffn2_norm"][1]]
    gains = [a["nsa_q_gain"][0], a["nsa_k_gain"][0, 0], a["nsa_k_gain"][0, 1], a["nsa_k_gain"][0, 2]]
    sq, rot, dec, onehot = constants()
    arrays = {
        "x_in": a["x"].reshape(T, D),
        "stream": stream,
        "norm_g": np.stack(norms).reshape(6, KT, P).transpose(2, 0, 1),
        "gate_w": nin[:, -48:].reshape(KT, P, 48).transpose(1, 0, 2),
        "cmp_w2": a["nsa_cmp_w2"][0].reshape(2, 2, P, DH).transpose(2, 0, 1, 3),
        "cmp_pos": a["nsa_cmp_pos"][0].reshape(2, LP, 2, DH).transpose(2, 3, 0, 1).reshape(P, 2, LP),
        "qk_gain": np.tile(np.stack(gains, 1), (2, 1)),
        "rel": a["rel_bias"],
        "c_sq": sq, "c_rot": rot, "c_dec": dec, "c_rel": onehot,
    }
    arrays = {k: np.ascontiguousarray(v) for k, v in arrays.items()}
    nc = bacc.Bacc("TRN2", target_bir_lowering=False, num_devices=1)
    args = {k: nc.dram_tensor(k, v.shape, mybir.dt.from_np(v.dtype), kind="ExternalInput").ap() for k, v in arrays.items()}
    rel_rows = nc.dram_tensor("rel_rows", (NH, REL), F32, kind="Internal").ap()
    out = nc.dram_tensor("out", (T, D), F32, kind="ExternalOutput").ap()
    trunk(nc, **args, rel_rows=rel_rows, out=out)
    r = run_bass_kernel_spmd(nc, [arrays], core_ids=[0])
    return r.results[0]["out"].reshape(1, T, D)
```

```python
from contextlib import ExitStack

import numpy as np
import concourse.bass as bass
from concourse import mybir

F32 = mybir.dt.float32
F32R = mybir.dt.float32r
ALU = mybir.AluOpType
ACT = mybir.ActivationFunctionType

P = 128
D = 1024
T = 512
KT = D // P
TT = T // P
F = 2816
FT = F // P
EPS = 1e-6
RH, DK, DV = 4, 256, 512
NH, NG, HPG, DH = 16, 4, 4, 64
CMP_LEN, CMP_STRIDE = 32, 16
NC = (T - CMP_LEN) // CMP_STRIDE + 1
NCP = NC + 1
GN = NG * NC
LP = CMP_LEN // 2
BUCKETS = 32
REL = 640
BIG = 1e30

SLOTS = 4
CW = 1024
UP, DOWN = 2 * FT, FT
C_FFN = [0, 0, 0, 0]
C_FFN[0] = 0
C_RET = C_FFN[0] + UP + DOWN
C_FFN[1] = C_RET + RH * 16
C_FFN[2] = C_FFN[1] + UP + DOWN
C_NSA = C_FFN[2] + UP + DOWN
C_NOUT = C_NSA + 28
C_FFN[3] = C_NOUT + 8
NCHUNK = C_FFN[3] + UP + DOWN
G_FFN = [4, 0, 0, 0]
G_RET = G_FFN[0] + FT
G_FFN[1] = G_RET + RH * 8
G_FFN[2] = G_FFN[1] + FT
G_NSA = G_FFN[2] + FT
G_FFN[3] = G_NSA + 10
NS, NTT = 12, 9
SLC, WIN, CMPB = 0, 1, 2
LAG = 1
V_LAG = 3
O_AT = 3
P_OFF = [0, 128, 384, 768]
PB = 1280
PW = 2 * PB + TT * NCP


def p_slice(b, i):
    if b == CMPB:
        return 2 * PB + i * NCP, 7 + 8 * i
    return b * PB + P_OFF[i], P * (i + 1)


def trunk(nc, x_in, stream, norm_g, gate_w, cmp_w2, cmp_pos, qk_gain, rel, c_sq, c_rot, c_dec, c_rel, rel_rows, out):
    ctx = ExitStack()
    with ctx:
        def sem(name):
            return ctx.enter_context(nc.semaphore(name))

        def sb(name, shape, dt=F32, scope=ctx):
            return scope.enter_context(nc.sbuf_tensor(name, shape, dt))

        x = sb("x", [P, KT, T])
        xh = sb("xh", [P, KT, T], F32R)
        xl = sb("xl", [P, KT, T], F32R)
        raw = sb("raw", [P, SLOTS, CW])
        wh = sb("wh", [P, SLOTS, CW], F32R)
        wl = sb("wl", [P, SLOTS, CW], F32R)
        sq = sb("sq", [P, 2, T])
        with ExitStack() as s:
            std = sb("std", [P, 2, T], F32, s)
        pt3 = sb("pt3", [P, 2, T], F32R)
        csq = sb("csq", [P, 2 * P + 1])
        ident = csq[:, 0:P]
        bones = csq[:, P:2 * P]
        rowmask = csq[:, 2 * P:2 * P + 1]
        ones = sb("ones", [P, P])
        eps = sb("eps", [P, 1])
        pmark = sb("pmark", [1, 2])
        mark = sb("mark", [1, 16])
        gain = sb("gain", [P, 6, KT])
        qkg = sb("qkg", [P, 4])

        with ExitStack() as s:
            uh = sb("uh", [P, FT, T], F32R, s)
            ul = sb("ul", [P, FT, T], F32R, s)
            uf = sb("uf", [P, 2, T], F32, s)
            bf = sb("bf", [P, 2, T], F32, s)
        with ExitStack() as s:
            rotq = sb("rotq", [P, 2, T], F32, s)
            rotk = sb("rotk", [P, 2, T], F32, s)
            rnt = sb("rnt", [P, T], F32, s)
            rn = rnt[:, :]
            sx = sb("sx", [P, 4, T], F32, s)
            dec = sb("dec", [P, RH, T], F32, s)
            rt = sb("rt", [P, 4, T], F32, s)
            qkh = sb("qkh", [P, 2, 2, T], F32R, s)
            qkl = sb("qkl", [P, 2, 2, T], F32R, s)
            vh = sb("vh", [P, TT, DV], F32R, s)
            vl = sb("vl", [P, TT, DV], F32R, s)
            sg = sb("sg", [P, 2, T], F32, s)
            af = sb("af", [P, PB], F32, s)
            qf = af[:, 0:2 * T].rearrange("p (a t) -> p a t", a=2)
            ah = sb("ah", [P, PB], F32R, s)
            al = sb("al", [P, PB], F32R, s)
            onf = rt
            onh = sb("onh", [P, 4, T], F32R, s)
            onl = sb("onl", [P, 4, T], F32R, s)
        with ExitStack() as s:
            qn = sb("qn", [P, KT, T], F32, s)
            kh = sb("kh", [P, 2, NG, T], F32R, s)
            kl = sb("kl", [P, 2, NG, T], F32R, s)
            vf = sb("vf", [P, TT, 2, NG, DH], F32, s)
            vst = sb("vst", [P, TT, 2, 2 * DH], F32R, s)
            rcol = sb("rcol", [P, TT], F32, s)
            gates = sb("gates", [P, NH, 3, TT], F32, s)
            kch = sb("kch", [P, NG, NCP], F32R, s)
            kcl = sb("kcl", [P, NG, NCP], F32R, s)
            vcf = sb("vcf", [NCP, NG, DH], F32, s)
            vcst = sb("vcst", [NCP, 2 * DH], F32R, s)
            qs = sb("qs", [P, 2, T], F32R, s)
            mn = sb("mn", [P, 2, NS], F32, s)
            rsum = sb("rsum", [P, 2, NS], F32, s)
            coef = sb("coef", [P, 2, NS], F32, s)
            with ExitStack() as s2:
                z = sb("z", [P, 2, NG, T // 2], F32, s2)
                u = sb("u", [P, 4 * T], F32, s2)
                uch = sb("uch", [P, LP * GN], F32R, s2)
                ucl = sb("ucl", [P, LP * GN], F32R, s2)
                pos = sb("pos", [P, 2, LP], F32, s2)
                w2 = sb("w2", [P, 2, 2, DH], F32, s2)
            with ExitStack() as s2:
                tn = sb("tn", [P, 2, T], F32, s2)
                pr = sb("pr", [P, 2, PW], F32, s2)
                pth2 = sb("pth", [P, 2, T], F32R, s2)
                ptl2 = sb("ptl", [P, 2, T], F32R, s2)
        pth = [pth2[:, 0, :], pth2[:, 1, :], pt3[:, 0, :]]
        ptl = [ptl2[:, 0, :], ptl2[:, 1, :], pt3[:, 1, :]]
        osq = [sq[:, 0, :], sq[:, 1, :], std[:, 0, :], std[:, 1, :]]
        hpair = [qn[:, a:a + 2, :] for a in (6, 4, 0, 2, 4, 6)]
        HN_FREE = (3, 5, 7, 8, 9, 10)
        nrn = vf[:, 1, :, :, :].rearrange("p b g d -> p (b g d)")
        with ExitStack() as s:
            xin = sb("xin", [P, TT, D], F32, s)
            relw = sb("relw", [BUCKETS + 1, NH], F32, s)
            onehot = sb("onehot", [BUCKETS + 1, REL], F32, s)
            relo = sb("relo", [NH, REL], F32, s)
        ps = ctx.enter_context(nc.psum_tensor("ps", [P, 8, T], F32))
        gwf = vf[:, 0, :, :, :].rearrange("p b g d -> p (b g d)")[:, 0:KT * 48].rearrange("p (k n) -> p k n", k=KT)
        gw2 = vst[:, :, :, :].rearrange("p t b d -> p (t b d)")[:, 0:2 * KT * 48]
        gwh, gwl = [gw2[:, i * KT * 48:(i + 1) * KT * 48].rearrange("p (k n) -> p k n", k=KT) for i in range(2)]
        gl = z[:, 0, 0:2, :].rearrange("p g t -> p (g t)")[:, 0:4 * GN].rearrange("p (j t n) -> p j t n", j=2, t=2)
        kct = u[0:DH, 0:2 * GN].rearrange("p (j n) -> p j n", j=2)
        kcf = u[0:DH, 2 * GN:3 * GN]

        raw_landed = [sem(f"raw_landed{i}") for i in range(SLOTS)]
        chunk_hi = sem("chunk_hi")
        chunk_lo = sem("chunk_lo")
        chunk_mm = sem("chunk_mm")
        r_ready = sem("r_ready")
        r_turned = sem("r_turned")
        rcol_ready = sem("rcol_ready")
        pair_free = sem("pair_free")
        consts_in = sem("consts_in")
        consts_set = sem("consts_set")
        x_in_landed = sem("x_in_landed")
        x_turned = sem("x_turned")
        x_ready = sem("x_ready")
        sq_ready = sem("sq_ready")
        sq_sum = sem("sq_sum")
        ss_mm = sem("ss_mm")
        xh_ready = sem("xh_ready")
        a_scaled = sem("a_scaled")
        std_ready = sem("std_ready")
        xn_ready = sem("xn_ready")
        silu_ready = sem("silu_ready")
        u_ready = sem("u_ready")
        down_mm = sem("down_mm")
        dve_step = sem("dve_step")
        pool_set = sem("pool_set")
        rel_mm = sem("rel_mm")
        rel_out = sem("rel_out")
        rel_stored = sem("rel_stored")
        ret_in = sem("ret_in")
        qk_ready = sem("qk_ready")
        v_ready = sem("v_ready")
        s_read = sem("s_read")
        osq_sum = sem("osq_sum")
        s_mm = sem("s_mm")
        a_ready = sem("a_ready")
        pv_mm = sem("pv_mm")
        osq_ready = sem("osq_ready")
        oss_mm = sem("oss_mm")
        ostd_ready = sem("ostd_ready")
        sig_ready = sem("sig_ready")
        sx_ready = sem("sx_ready")
        sg_ready = sem("sg_ready")
        on_ready = sem("on_ready")
        hsq_ready = sem("hsq_ready")
        hss_mm = sem("hss_mm")
        hstd_ready = sem("hstd_ready")
        hn_ready = sem("hn_ready")
        uc_ready = sem("uc_ready")
        uc_used = sem("uc_used")
        gw_ready = sem("gw_ready")
        gate_mm = sem("gate_mm")
        gates_set = sem("gates_set")
        gelu_ready = sem("gelu_ready")
        w2_mm = sem("w2_mm")
        kcsq_ready = sem("kcsq_ready")
        kcss_mm = sem("kcss_mm")
        kcstd_ready = sem("kcstd_ready")
        cmp_ready = sem("cmp_ready")
        bias_landed = [sem("bias_landed0"), sem("bias_landed1")]
        qs_ready = sem("qs_ready")
        vst_ready = sem("vst_ready")
        vst_half = sem("vst_half")
        sc_mm = sem("sc_mm")
        sc_read = sem("sc_read")
        exp_done = sem("exp_done")
        coef_ready = sem("coef_ready")
        p_scaled = sem("p_scaled")
        pt_mm = sem("pt_mm")
        pt_hi = sem("pt_hi")
        pt_ready = sem("pt_ready")
        apv_mm = sem("apv_mm")
        o_half = sem("o_half")
        o_ready = sem("o_ready")
        y_mm = sem("y_mm")
        y_ready = sem("y_ready")
        y_stored = sem("y_stored")

        def chunk(c0, i=None, step=0):
            if i is None:
                return c0, c0 % SLOTS, c0 // SLOTS
            return i * step + c0, c0 % SLOTS, i * (step // SLOTS) + c0 // SLOTS

        block = ctx.enter_context(nc.Block())

        @block.sync
        def _(sp):
            def load(ch):
                c, slot, turn = ch
                sp.dma_start(raw[:, slot, :], stream[c]).then_inc(raw_landed[slot], 16)

            for t in range(TT):
                sp.dma_start(xin[:, t, :], x_in[t * P:(t + 1) * P, :]).then_inc(x_in_landed, 16)
            sp.dma_start(csq[:, :], c_sq).then_inc(consts_in, 16)
            for c in range(SLOTS):
                load(chunk(c))
            sp.dma_start(gain[:, :, :], norm_g).then_inc(consts_in, 16)
            sp.dma_start(qkg[:, :], qk_gain).then_inc(consts_in, 16)
            sp.dma_start(relw[0:BUCKETS, :], rel).then_inc(consts_in, 16)
            sp.dma_start(onehot[:, :], c_rel).then_inc(consts_in, 16)

            def loads(c0, n):
                with sp.Fori(0, n // SLOTS) as i:
                    for k in range(SLOTS):
                        ch = chunk(c0 + k, i, SLOTS)
                        sp.wait_ge(chunk_lo, ch[0] - (SLOTS - 1))
                        load(ch)
                for c in range(c0 + n // SLOTS * SLOTS, c0 + n):
                    sp.wait_ge(chunk_lo, c - (SLOTS - 1))
                    load(chunk(c))

            sp.wait_ge(rel_out, 1)
            sp.dma_start(rel_rows, relo[:, :]).then_inc(rel_stored, 16)
            loads(SLOTS, C_RET - SLOTS)
            sp.wait_ge(chunk_mm, C_RET)
            sp.dma_start(rotq[:, :, :], c_rot).then_inc(ret_in, 16)
            sp.dma_start(dec[:, :, :], c_dec).then_inc(ret_in, 16)
            loads(C_RET, C_NSA - C_RET)
            sp.wait_ge(chunk_mm, C_NSA)
            sp.dma_start(gwf[:, :, :], gate_w).then_inc(ret_in, 16)
            sp.dma_start(pos[:, :, :], cmp_pos).then_inc(ret_in, 16)
            sp.dma_start(w2[:, :, :, :], cmp_w2).then_inc(ret_in, 16)
            loads(C_NSA, C_NOUT + 2 * SLOTS - C_NSA)
            sp.wait_ge(rel_stored, 16)
            sp.wait_ge(cmp_ready, 2)
            sp.wait_ge(gates_set, 1)

            def bias(h, b):
                row = rel_rows[h]
                src = bass.AP(row.tensor, row.offset + 1, [[1, P], [1, T]])
                sp.dma_start(tn[:, b, :], src).then_inc(bias_landed[b], 16)

            bias(0, 0)
            bias(1, 1)
            with sp.Fori(1, NH // 2) as i:
                for b in range(2):
                    sp.wait_ge(sc_read, (i * 2 + (b - 1)) * NS)
                    bias(i * 2 + b, b)
            loads(C_NOUT + 2 * SLOTS, NCHUNK - C_NOUT - 2 * SLOTS)
            for t in range(TT):
                sp.wait_ge(y_ready, 8 * (t + 1))
                sp.dma_start(out[t * P:(t + 1) * P, :], xin[:, t, :]).then_inc(y_stored, 16)
            sp.wait_ge(y_stored, 16 * TT)

        @block.gpsimd
        def _(pool):
            def low(ch):
                c, slot, turn = ch
                pool.wait_ge(chunk_hi, c + 1)
                nc.gpsimd.tensor_tensor(wl[:, slot, :], raw[:, slot, :], wh[:, slot, :].bitcast(F32),
                                        ALU.subtract).then_inc(chunk_lo, 1)

            def lows(c0, c1):
                n = c1 - c0
                if n >= SLOTS:
                    with pool.Fori(0, n // SLOTS) as i:
                        for k in range(SLOTS):
                            low(chunk(c0 + k, i, SLOTS))
                for c in range(c0 + n // SLOTS * SLOTS, c1):
                    low(chunk(c))

            acc = std[:, 1, :]

            def sum_squares(m):
                add = nc.gpsimd.tensor_tensor
                pool.wait_ge(sq_ready, m * KT + 2)
                add(acc, sq[:, 0, :], sq[:, 1, :], ALU.add).then_inc(sq_sum, 1)
                for d in range(2, KT):
                    pool.wait_ge(sq_ready, m * KT + d + 1)
                    pool.wait_ge(sq_sum, m * (KT - 1) + d - 1)
                    add(acc, acc, sq[:, d % 2, :], ALU.add).then_inc(sq_sum, 1)

            nc.gpsimd.memset(pmark[:, :], 0.0).then_inc(pool_set, 1)
            pool.wait_ge(pool_set, 1)
            ahead = SLOTS - 1
            lows(0, ahead)
            sum_squares(0)
            lows(ahead, C_RET + ahead)
            sum_squares(1)
            low(chunk(C_RET + ahead))
            lows(C_RET + 4, C_RET + 16)
            def sum_outputs(h):
                pool.wait_ge(osq_ready, h * 4 + 4)
                for v in range(1, 4):
                    if v > 1:
                        pool.wait_ge(osq_sum, h * 3 + (v - 1))
                    nc.gpsimd.tensor_tensor(osq[0], osq[0], osq[v], ALU.add).then_inc(osq_sum, 1)

            with pool.Fori(0, RH - 1) as h:
                sum_outputs(h)
                for k in range(16):
                    low(chunk(C_RET + 16 + k, h, 16))
            sum_outputs(RH - 1)
            at = C_RET + 64
            for m, c0 in ((2, C_FFN[1]), (3, C_FFN[2]), (4, C_NSA)):
                lows(at, c0 + ahead)
                sum_squares(m)
                at = c0 + ahead
            split = C_NOUT + SLOTS
            lows(at, split)
            def stage_v(g):
                src = vf[:, :, :, g, :].rearrange("p t b d -> p (t b) d")
                vv = vst[:, :, :, :].rearrange("p t b d -> p (t b) d")
                if not (isinstance(g, int) and g == 0):
                    pool.wait_ge(apv_mm, g * HPG * NTT)
                nc.gpsimd.tensor_copy(vv[:, :, 0:DH], src).then_inc(vst_half, 1)
                nc.gpsimd.tensor_copy(vcst[:, 0:DH], vcf[:, g, :]).then_inc(vst_half, 1)
                pool.wait_ge(vst_half, g * 3 + 2)
                nc.gpsimd.tensor_tensor(pmark[:, 1:2], pmark[:, 1:2], pmark[:, 1:2], ALU.mult).then_inc(vst_half, 1)
                nc.gpsimd.tensor_tensor(vv[:, :, DH:2 * DH], src, vv[:, :, 0:DH].bitcast(F32),
                                        ALU.subtract).then_inc(vst_ready, 1)
                nc.gpsimd.tensor_tensor(vcst[:, DH:2 * DH], vcf[:, g, :], vcst[:, 0:DH].bitcast(F32),
                                        ALU.subtract).then_inc(vst_ready, 1)

            pool.wait_ge(cmp_ready, 1)
            stage_v(0)
            def scale(h, hh, br):
                b = hh % 2
                pool.wait_ge(pool_set, h * 3 + (br + 1))
                pool.wait_ge(coef_ready, h * 3 + (br + 1))
                nc.gpsimd.tensor_tensor(pmark[:, 0:1], pmark[:, 0:1], pmark[:, 0:1], ALU.mult).then_inc(pool_set, 1)
                for ti in range(TT):
                    o, n = p_slice(br, ti)
                    k = br * TT + ti
                    nc.gpsimd.tensor_scalar(pr[:, b, o:o + n], pr[:, b, o:o + n], coef[:, b, k:k + 1],
                                            1.0, ALU.mult, ALU.mult).then_inc(p_scaled, 1)

            for hh in range(HPG):
                for br in range(3):
                    scale(hh, hh, br)
            with pool.Fori(1, NG) as g:
                for hh in range(HPG):
                    for br in range(3):
                        scale(g * HPG + hh, hh, br)
                        if (hh, br) == (0, WIN):
                            stage_v(g)
            lows(split, C_FFN[3] + ahead)
            sum_squares(5)
            lows(C_FFN[3] + ahead, NCHUNK)

        @block.scalar
        def _(act):
            def high(ch, first=False):
                c, slot, turn = ch
                act.wait_ge(raw_landed[slot], turn * 16 + 16)
                if not first:
                    act.wait_ge(chunk_mm, c - (SLOTS - 1))
                nc.scalar.activation(wh[:, slot, :], raw[:, slot, :], ACT.Copy).then_inc(chunk_hi, 1)

            def after(c0, n=1, i=None, step=0):
                for c in range(c0, c0 + n):
                    if c + SLOTS < NCHUNK:
                        high(chunk(c + SLOTS, i, step))

            def square(m, d):
                if d >= 2:
                    act.wait_ge(sq_sum, m * (KT - 1) + max(1, d - 2))
                nc.scalar.activation(sq[:, d % 2, :], x[:, d, :], ACT.Square).then_inc(sq_ready, 1)

            def root(m):
                act.wait_ge(ss_mm, m + 1)
                nc.scalar.activation(std[:, 0, :], ps[:, 6, :], ACT.Sqrt, bias=eps[:, 0:1],
                                     scale=1.0 / D).then_inc(std_ready, 1)

            def norm_later(m, tiles=range(KT)):
                for d in tiles:
                    act.wait_ge(x_ready, m * KT + d + 1)
                    nc.scalar.activation(xh[:, d, :], x[:, d, :], ACT.Copy, scale=gain[:, m, d:d + 1]).then_inc(xh_ready, 1)
                    square(m, d)

            def ffn(m, last=False):
                c0, u0 = C_FFN[m], m * FT
                root((0, 2, 3, 5)[m])
                with act.Fori(0, FT // 2) as i:
                    for k in range(2):
                        after(c0 + 2 * k, 2, i, 4)
                        act.wait_ge(a_scaled, i * 2 + (u0 + k + 1))
                        nc.scalar.activation(uf[:, k, :], uf[:, k, :], ACT.Silu).then_inc(silu_ready, 1)
                (wide_last if last else wide)(c0 + UP, FT)

            def wide(c0, n):
                with act.Fori(0, n // 4) as i:
                    for k in range(4):
                        after(c0 + k, 1, i, 4)
                for c in range(c0 + n // 4 * 4, c0 + n):
                    after(c)

            def wide_last(c0, n):
                m = (n - SLOTS) // 4
                with act.Fori(0, m) as i:
                    for k in range(4):
                        high(chunk(c0 + k + SLOTS, i, 4))
                for c in range(c0 + 4 * m, c0 + n - SLOTS):
                    high(chunk(c + SLOTS))

            act.wait_ge(consts_set, 3)
            for c in range(SLOTS):
                high(chunk(c), first=True)
            act.wait_ge(consts_in, 16 * 5)
            norm_later(0)
            ffn(0)
            norm_later(1)
            root(1)

            def ret_qk(c0, i=None, step=0):
                after(c0, 4, i, step)

            def ret_main(h, c0, i=None, step=0):
                after(c0, 4, i, step)
                after(c0 + 4, 4, i, step)
                for k in range(2):
                    act.wait_ge(sx_ready, h * 2 + (k + 1))
                    if k:
                        act.wait_ge(sg_ready, h * 2 + 1)
                    nc.scalar.activation(sg[:, :, :], sx[:, 2 * k:2 * k + 2, :],
                                         ACT.Sigmoid).then_inc(sig_ready, 1)
                act.wait_ge(pv_mm, h + 1)
                for v in range(4):
                    nc.scalar.activation(osq[v], ps[:, 4 + v, :], ACT.Square).then_inc(osq_ready, 1)

            def ret_std(h):
                act.wait_ge(oss_mm, h + 1)
                nc.scalar.activation(std[:, 0, :], ps[:, 4, :], ACT.Sqrt, bias=eps[:, 0:1],
                                     scale=1.0 / DV).then_inc(ostd_ready, 1)

            ret_qk(C_RET)
            with act.Fori(0, RH - 1) as h:
                ret_main(h, C_RET + 4, h, 16)
                after(C_RET + 12, 2, h, 16)
                ret_std(h)
                after(C_RET + 14, 6, h, 16)
            ret_main(RH - 1, C_RET + 52)
            ret_std(RH - 1)
            for k in range(4):
                after(C_RET + 60 + k)
                if k:
                    norm_later(2, range(2 * k - 2, 2 * k))
            norm_later(2, range(KT - 2, KT))
            ffn(1)
            norm_later(3)
            ffn(2)
            norm_later(4)
            root(4)

            def head_sq(n, c):
                after(c, 2)
                act.wait_ge(pair_free, G_NSA + HN_FREE[n])
                if n >= 1:
                    act.wait_ge(hss_mm, n)
                nc.scalar.activation(sq[:, :, :], hpair[n], ACT.Square).then_inc(hsq_ready, 1)

            def head_std(n):
                act.wait_ge(hss_mm, n + 1)
                if n >= 1:
                    act.wait_ge(hn_ready, n)
                b = 4 + 2 * (n % 2)
                nc.scalar.activation(std[:, :, :], ps[:, b:b + 2, :], ACT.Sqrt, bias=eps[:, 0:1],
                                     scale=1.0 / DH).then_inc(hstd_ready, 1)

            def gelu(j, c):
                after(c, 4)
                act.wait_ge(chunk_mm, c + 4)
                nc.scalar.activation(gl[:, j, :, :], ps[:, 2:4, 0:GN], ACT.Gelu_apprx_tanh).then_inc(gelu_ready, 1)

            c0 = C_NSA
            after(c0, 4)
            head_sq(0, c0 + 4)
            gelu(0, c0 + 6)
            head_std(0)
            head_sq(1, c0 + 10)
            gelu(1, c0 + 12)
            head_std(1)
            head_sq(2, c0 + 16)
            head_sq(3, c0 + 18)
            head_std(2)
            head_sq(4, c0 + 20)
            head_std(3)
            head_sq(5, c0 + 22)
            head_std(4)
            act.wait_ge(gate_mm, 1)
            act.wait_ge(rcol_ready, 1)
            for i in range(TT):
                g = ps[:, 0, i * 48:(i + 1) * 48].rearrange("p (b h) -> p b h", b=3)
                nc.scalar.activation(gates[:, :, :, i].rearrange("p h b -> p b h"), g, ACT.Sigmoid,
                                     scale=rcol[:, i:i + 1]).then_inc(sig_ready, 1)
            head_std(5)
            act.wait_ge(w2_mm, 1)
            nc.scalar.activation(kct[:, 0, :], ps[0:DH, 1, 0:GN], ACT.Square).then_inc(kcsq_ready, 1)
            after(c0 + 24, 4)
            act.wait_ge(kcss_mm, 1)
            nc.scalar.activation(kct[:, 1, :], ps[0:DH, 3, 0:GN], ACT.Sqrt, bias=eps[0:DH, 0:1],
                                 scale=1.0 / DH).then_inc(kcstd_ready, 1)

            def exp(h, b, k):
                o, n = p_slice(k // TT, k % TT)
                act.wait_ge(sc_read, h * NS + k + 1)
                nc.scalar.activation(pr[:, b, o:o + n], pr[:, b, o:o + n], ACT.Exp, bias=mn[:, b, k:k + 1],
                                     scale=-1.0, accum_out=rsum[:, b, k:k + 1]).then_inc(exp_done, 1)

            def pt_high(h, hh, k):
                act.wait_ge(pt_mm, h * NTT + k + 1)
                if not (isinstance(h, int) and h == 0 and k < 3):
                    act.wait_ge(apv_mm, h * NTT + k - 2)
                np_, n = (NCP, T) if k == 8 else (P, T - P * (k % 4))
                nc.scalar.activation(pth[k % 3][0:np_, 0:n], ps[0:np_, 3 + k % 3, 0:n], ACT.Copy).then_inc(pt_hi, 1)

            def o_copy(h, hh):
                s = DH * (hh % 2)
                act.wait_ge(apv_mm, (h + 1) * NTT)
                if not (isinstance(h, int) and h == 0):
                    act.wait_ge(o_ready, h)
                nc.scalar.activation(sq[s:s + DH, 0, :], ps[DH:P, 6 + hh % 2, :], ACT.Copy).then_inc(o_half, 1)

            def step_of(h, hh, more=True):
                for k in range(NS):
                    if LAG <= k < LAG + NTT:
                        pt_high(h, hh, k - LAG)
                    if k == O_AT and not (isinstance(h, int) and h == 0):
                        o_copy(h - 1, (hh + 1) % 2)
                    if more:
                        exp(h + 1, (hh + 1) % 2, k)

            for k in range(NS):
                exp(0, 0, k)
            for hh in range(HPG):
                step_of(hh, hh)
            with act.Fori(1, NG - 1) as g4:
                for hh in range(HPG):
                    step_of(g4 * HPG + hh, hh)
            for hh in range(HPG):
                step_of(NH - HPG + hh, hh, more=hh < HPG - 1)
            o_copy(NH - 1, HPG - 1)
            after(C_NOUT, 8)
            norm_later(5)
            ffn(3, last=True)

        @block.tensor
        def _(pe):
            mm = nc.tensor.matmul

            def tall(g, parity, chunks, moving, n=T, kpc=4, ready=None):
                last_k = kpc * len(chunks) - 1
                pe.wait_ge(pair_free, g - 1)
                for ci, (c, slot, turn) in enumerate(chunks):
                    pe.wait_ge(chunk_lo, c + 1)
                    for r in range(kpc):
                        k = ci * kpc + r
                        if ready is not None:
                            ready(k)
                        hi, lo = moving(k)
                        for ab in range(2):
                            col = r * 2 * P + ab * P
                            o = ps[:, 2 * parity + ab, 0:n]
                            w_h, w_l = wh[:, slot, col:col + P], wl[:, slot, col:col + P]
                            mm(o, w_h, hi, start=k == 0, stop=False)
                            mm(o, w_h, lo, start=False, stop=False)
                            last = mm(o, w_l, hi, start=False, stop=k == last_k)
                    last.then_inc(chunk_mm, 1)

            def from_x(k):
                return xh[:, k, :], xl[:, k, :]

            def natural(chunks, ready=None):
                for ci, (c, slot, turn) in enumerate(chunks):
                    pe.wait_ge(chunk_lo, c + 1)
                    for r in range(2):
                        k = 2 * ci + r
                        w_h, w_l = wh[:, slot, r * T:(r + 1) * T], wl[:, slot, r * T:(r + 1) * T]
                        for t in range(TT):
                            o = ps[:, 4 + t, :]
                            x_h, x_l = xh[:, k, t * P:(t + 1) * P], xl[:, k, t * P:(t + 1) * P]
                            mm(o, x_h, w_h, start=k == 0, stop=False)
                            mm(o, x_h, w_l, start=False, stop=False)
                            last = mm(o, x_l, w_h, start=False, stop=k == KT - 1)
                    last.then_inc(chunk_mm, 1)

            def wide_chunk(ch, f_h, f_l, order, start, stop):
                c, slot, turn = ch
                pe.wait_ge(chunk_lo, c + 1)
                for d in order:
                    w_h, w_l = wh[:, slot, d * P:(d + 1) * P], wl[:, slot, d * P:(d + 1) * P]
                    mm(ps[:, d, :], w_h, f_h, start=start, stop=False)
                    mm(ps[:, d, :], w_h, f_l, start=False, stop=False)
                    last = mm(ps[:, d, :], w_l, f_h, start=False, stop=stop)
                    if stop and d < KT - 1:
                        last.then_inc(down_mm, 1)
                last.then_inc(chunk_mm, 1)

            def norm(m):
                pe.wait_ge(sq_sum, (m + 1) * (KT - 1))
                mm(ps[:, 6, :], ones[:, :], std[:, 1, :], start=True, stop=True).then_inc(ss_mm, 1)

            def ffn(m):
                c0, g0, u0 = C_FFN[m], G_FFN[m], m * FT
                nm = (0, 2, 3, 5)[m]
                tall(g0, 0, [chunk(c0), chunk(c0 + 1)], from_x, ready=lambda kt: pe.wait_ge(xn_ready, nm * KT + kt + 1))
                norm(nm)
                tall(g0 + 1, 1, [chunk(c0 + 2), chunk(c0 + 3)], from_x)
                with pe.Fori(1, FT // 2) as i:
                    for k in range(2):
                        tall(i * 2 + (g0 + k), k, [chunk(c0 + 2 * k, i, 4), chunk(c0 + 2 * k + 1, i, 4)], from_x)
                cd = c0 + UP
                pe.wait_ge(u_ready, u0 + 1)
                first = list(range(4, 8)) + list(range(4))
                c, slot, turn = chunk(cd)
                pe.wait_ge(chunk_lo, c + 1)
                for d in first:
                    if d == 0:
                        pe.wait_ge(pair_free, g0 + FT)
                    w_h, w_l = wh[:, slot, d * P:(d + 1) * P], wl[:, slot, d * P:(d + 1) * P]
                    mm(ps[:, d, :], w_h, uh[:, 0, :], start=True, stop=False)
                    mm(ps[:, d, :], w_h, ul[:, 0, :], start=False, stop=False)
                    last = mm(ps[:, d, :], w_l, uh[:, 0, :], start=False, stop=False)
                last.then_inc(chunk_mm, 1)
                n = (FT - 2) // 4
                with pe.Fori(0, n) as i:
                    for k in range(4):
                        f = i * 4 + (1 + k)
                        pe.wait_ge(u_ready, f + (u0 + 1))
                        wide_chunk(chunk(cd + 1 + k, i, 4), uh[:, f, :], ul[:, f, :], range(KT), False, False)
                for f in range(1 + 4 * n, FT):
                    pe.wait_ge(u_ready, u0 + f + 1)
                    wide_chunk(chunk(cd + f), uh[:, f, :], ul[:, f, :], range(KT), False, f == FT - 1)

            pe.wait_ge(consts_in, 16 * 5)
            pe.wait_ge(consts_set, 3)
            pe.wait_ge(x_in_landed, 16 * TT)
            for d in range(KT):
                if d >= 4:
                    pe.wait_ge(pair_free, d // 2 - 1)
                for t in range(TT):
                    last = nc.tensor.transpose(ps[:, d % 4, t * P:(t + 1) * P], xin[:, t, d * P:(d + 1) * P], ident)
                last.then_inc(x_turned, 1)
            for k in range(2):
                last = mm(ps[0:NH, 4 + k, 0:REL // 2], relw[:, :], onehot[:, k * (REL // 2):(k + 1) * (REL // 2)],
                          start=True, stop=True)
            last.then_inc(rel_mm, 1)
            ffn(0)

            def ret_qk_q(g, c0, i=None, step=0, ready=None):
                tall(g, 0, [chunk(c0, i, step), chunk(c0 + 1, i, step)], from_x, ready=ready)

            def ret_qk_k(g, c0, i=None, step=0):
                tall(g, 1, [chunk(c0, i, step), chunk(c0 + 1, i, step)], from_x)

            def ret_main(h, g0, c0, i=None, step=0):
                natural([chunk(c0 + k, i, step) for k in range(4)])
                pe.wait_ge(qk_ready, h * 2 + 2)
                pe.wait_ge(pair_free, g0)
                for j in range(TT):
                    n = T - j * P
                    for half in range(2):
                        k_h, k_l = qkh[:, 1, half, j * P:(j + 1) * P], qkl[:, 1, half, j * P:(j + 1) * P]
                        q_h, q_l = qkh[:, 0, half, j * P:], qkl[:, 0, half, j * P:]
                        mm(ps[:, j, 0:n], k_h, q_h, start=half == 0, stop=False)
                        mm(ps[:, j, 0:n], k_h, q_l, start=False, stop=False)
                        last = mm(ps[:, j, 0:n], k_l, q_h, start=False, stop=half == 1)
                    last.then_inc(s_mm, 1)
                for k in range(2):
                    pe.wait_ge(s_read, h * TT + (2 * k + 2))
                    tall(g0 + k, k, [chunk(c0 + 4 + 2 * k, i, step), chunk(c0 + 5 + 2 * k, i, step)], from_x)
                pe.wait_ge(v_ready, h + 1)
                pe.wait_ge(a_ready, h * TT + TT)
                for j in range(TT):
                    o0 = (0, 512, 896, 1152)[j]
                    n = T - j * P
                    for v in range(4):
                        v_h, v_l = vh[:, j, v * P:(v + 1) * P], vl[:, j, v * P:(v + 1) * P]
                        o = ps[:, 4 + v, j * P:]
                        mm(o, v_h, ah[:, o0:o0 + n], start=j == 0, stop=False)
                        mm(o, v_h, al[:, o0:o0 + n], start=False, stop=False)
                        last = mm(o, v_l, ah[:, o0:o0 + n], start=False, stop=j == TT - 1)
                last.then_inc(pv_mm, 1)

            def ret_ss(h):
                pe.wait_ge(on_ready, h * 4 + 4)
                pe.wait_ge(osq_sum, h * 3 + 3)
                mm(ps[:, 4, :], ones[:, :], osq[0], start=True, stop=True).then_inc(oss_mm, 1)

            def ret_out(h, g0, c0, i=None, step=0, ks=range(4), ready=None):
                for k in ks:
                    tall(g0 + k, k % 2, [chunk(c0 + k, i, step)], lambda v: (onh[:, v, :], onl[:, v, :]), ready=ready)

            ret_qk_q(G_RET, C_RET, ready=lambda kt: pe.wait_ge(xn_ready, KT + kt + 1))
            norm(1)
            ret_qk_k(G_RET + 1, C_RET + 2)
            pe.wait_ge(std_ready, 2)
            with pe.Fori(0, RH - 1) as h:
                g = h * 8 + (G_RET + 2)
                ret_main(h, g, C_RET + 4, h, 16)
                ret_qk_q(g + 2, C_RET + 12, h, 16)
                ret_ss(h)
                ret_qk_k(g + 3, C_RET + 14, h, 16)
                ret_out(h, g + 4, C_RET + 16, h, 16)
                pe.wait_ge(ostd_ready, h + 1)
            g = G_RET + 2 + 8 * (RH - 1)
            ret_main(RH - 1, g, C_RET + 52)
            ret_out(RH - 1, g + 2, C_RET + 60, ks=[0], ready=lambda v: pe.wait_ge(on_ready, (RH - 1) * 4 + v + 1))
            ret_ss(RH - 1)
            ret_out(RH - 1, g + 2, C_RET + 60, ks=[1, 2, 3])
            ffn(1)
            ffn(2)

            def pair(n, c, ready=None):
                tall(G_NSA + n, n % 2, [chunk(C_NSA + c), chunk(C_NSA + c + 1)], from_x, ready=ready)

            def head_ss(n):
                pe.wait_ge(hsq_ready, n + 1)
                if n >= 2:
                    pe.wait_ge(hstd_ready, n - 1)
                b = 4 + 2 * (n % 2)
                for ab in range(2):
                    last = mm(ps[:, b + ab, :], bones, sq[:, ab, :], start=True, stop=True)
                last.then_inc(hss_mm, 1)

            def compress(j, n, c):
                pe.wait_ge(uc_ready, j + 1)
                tall(G_NSA + n, n % 2, [chunk(C_NSA + c + k) for k in range(4)],
                     lambda l2: (uch[:, l2 * GN:(l2 + 1) * GN], ucl[:, l2 * GN:(l2 + 1) * GN]), n=GN)

            pair(0, 0, ready=lambda kt: pe.wait_ge(xn_ready, 4 * KT + kt + 1))
            norm(4)
            pair(1, 2)
            pe.wait_ge(r_ready, 1)
            for t in range(TT):
                last = nc.tensor.transpose(ps[:, 7, t * P:(t + 1) * P], nrn[:, t * P:(t + 1) * P], ident)
            last.then_inc(r_turned, 1)
            pair(2, 4)
            compress(0, 3, 6)
            head_ss(0)
            pair(4, 10)
            compress(1, 5, 12)
            pe.wait_ge(rcol_ready, 1)
            head_ss(1)
            pair(6, 16)
            pair(7, 18)
            head_ss(2)
            pair(8, 20)
            head_ss(3)
            pair(9, 22)
            head_ss(4)
            pe.wait_ge(gw_ready, 1)
            pe.wait_ge(pair_free, G_NSA + 9)
            for t in range(TT):
                for k in range(KT):
                    o = ps[:, 0, t * 48:(t + 1) * 48]
                    x_h, x_l = xh[:, k, t * P:(t + 1) * P], xl[:, k, t * P:(t + 1) * P]
                    mm(o, x_h, gwh[:, k, :], start=k == 0, stop=False)
                    mm(o, x_h, gwl[:, k, :], start=False, stop=False)
                    last = mm(o, x_l, gwh[:, k, :], start=False, stop=k == KT - 1)
            last.then_inc(gate_mm, 1)
            pe.wait_ge(gelu_ready, 2)
            for g in range(NG):
                for t in range(2):
                    mm(ps[0:NC, 1, P + g * DH:P + (g + 1) * DH], gl[:, 1, t, g * NC:(g + 1) * NC], w2[:, 1, t, :],
                       start=t == 0, stop=t == 1)
            for t in range(2):
                last = mm(ps[0:DH, 1, 0:GN], w2[:, 0, t, :], gl[:, 0, t, :], start=t == 0, stop=t == 1)
            last.then_inc(w2_mm, 1)
            head_ss(5)
            pe.wait_ge(hstd_ready, 6)
            natural([chunk(C_NSA + 24 + k) for k in range(4)])
            pe.wait_ge(kcsq_ready, 1)
            pe.wait_ge(pair_free, G_NSA + 10)
            mm(ps[0:DH, 3, 0:GN], ones[0:DH, 0:DH], kct[:, 0, :], start=True, stop=True).then_inc(kcss_mm, 1)

            def score(h, g, b, k):
                br, ti = k // TT, k % TT
                if not (isinstance(h, int) and h == 0 and k < 3):
                    pe.wait_ge(sc_read, h * NS + (k - 2))
                q = qs[:, b, ti * P:(ti + 1) * P]
                n = p_slice(br, ti)[1]
                if br == CMPB:
                    n += 1
                    m_h, m_l = kch[:, g, 0:n], kcl[:, g, 0:n]
                else:
                    m_h, m_l = kh[:, br, g, 0:n], kl[:, br, g, 0:n]
                o = ps[:, k % 3, 0:n]
                mm(o, q, m_h, start=True, stop=False)
                mm(o, q, m_l, start=False, stop=True).then_inc(sc_mm, 1)

            def turn(h, hh, k):
                b = hh % 2
                if not (isinstance(h, int) and h == 0 and k < 3):
                    pe.wait_ge(pt_ready, h * NTT + (k - 2))
                for ti in range(0 if k == 8 else k % 4, TT):
                    po = p_slice(CMPB if k == 8 else k // 4, ti)[0]
                    if k == 8:
                        last = nc.tensor.transpose(ps[0:NCP, 3 + k % 3, ti * P:(ti + 1) * P],
                                                   pr[:, b, po:po + NCP], ident)
                    else:
                        j = k % 4
                        last = nc.tensor.transpose(ps[:, 3 + k % 3, (ti - j) * P:(ti - j + 1) * P],
                                                   pr[:, b, po + j * P:po + (j + 1) * P], ident)
                last.then_inc(pt_mm, 1)

            def values(h, hh, k):
                o, t_h, t_l = ps[:, 6 + hh % 2, :], pth[k % 3], ptl[k % 3]
                pe.wait_ge(pt_ready, h * NTT + k + 1)
                if k == 8:
                    mm(o, vcst[:, :], t_h[0:NCP, :], start=False, stop=False)
                    last = mm(o, vcst[:, :], t_l[0:NCP, :], start=False, stop=True)
                else:
                    j, br = k % 4, k // 4
                    n = T - j * P
                    mm(o[:, j * P:], vst[:, j, br, :], t_h[:, 0:n], start=k == 0, stop=False)
                    last = mm(o[:, j * P:], vst[:, j, br, :], t_l[:, 0:n], start=False, stop=False)
                last.then_inc(apv_mm, 1)

            def step_of(h, hh, g, more=True):
                if more:
                    pe.wait_ge(qs_ready, h + 2)
                for k in range(NS):
                    if more:
                        score(h + 1, g + (hh + 1) // HPG, (hh + 1) % 2, k)
                    t = k - LAG
                    if 0 <= t < NTT:
                        if t % 4 == 0:
                            pe.wait_ge(p_scaled, h * NS + (t + 4))
                        turn(h, hh, t)
                    if t == V_LAG:
                        if hh == 0:
                            pe.wait_ge(vst_ready, g * 2 + 2)
                        if not (isinstance(h, int) and h < 2):
                            pe.wait_ge(o_ready, h - 1)
                    if 0 <= t - V_LAG < NTT:
                        values(h, hh, t - V_LAG)
                for t in range(NS - LAG - V_LAG, NTT):
                    values(h, hh, t)

            pe.wait_ge(cmp_ready, 3)
            pe.wait_ge(qs_ready, 1)
            for k in range(NS):
                score(0, 0, 0, k)
            for hh in range(HPG):
                step_of(hh, hh, 0)
            with pe.Fori(1, NG - 1) as g4:
                for hh in range(HPG):
                    step_of(g4 * HPG + hh, hh, g4)
            for hh in range(HPG):
                step_of(NH - HPG + hh, hh, NG - 1, more=hh < HPG - 1)
            pe.wait_ge(sc_read, NH * NS)
            for f in range(8):
                pe.wait_ge(o_ready, NH if f == 0 else 2 * f + 2)
                wide_chunk(chunk(C_NOUT + f), xh[:, f, :], xl[:, f, :], range(KT), f == 0, f == 7)
            ffn(3)
            pe.wait_ge(x_ready, 7 * KT)
            for t in range(TT):
                for q in range(2):
                    n = 2 * t + q
                    if n >= 4:
                        pe.wait_ge(y_ready, 4 * (n - 3))
                    for r in range(4):
                        d = 4 * q + r
                        last = nc.tensor.transpose(ps[:, n % 4, r * P:(r + 1) * P], x[:, d, t * P:(t + 1) * P], ident)
                    last.then_inc(y_mm, 1)

        @block.vector
        def _(dve):
            V = nc.vector

            class Steps:
                n, i, per, start = 0, None, 0, 0

                def __call__(self, ins):
                    self.add(ins)
                    self.wait()

                def add(self, ins):
                    ins.then_inc(dve_step, 1)
                    self.n += 1

                def wait(self, but=0):
                    n = self.n - but
                    dve.wait_ge(dve_step, n if self.i is None else self.i * self.per + n)

                def loop(self, i, per, first=0):
                    self.i, self.per, self.start = i, per, self.n
                    self.n -= first * per

                def end(self, count, first=0):
                    assert self.n + first * self.per - self.start == self.per, (self.n + first * self.per - self.start, self.per)
                    self.i, self.n = None, self.start + self.per * count

            step = Steps()

            def split(hi, lo, src):
                step(V.tensor_copy(hi, src))
                return V.tensor_tensor(lo, src, hi.bitcast(F32), ALU.subtract)

            def invert(m):
                dve.wait_ge(std_ready, m + 1)
                step(V.reciprocal(std[:, 0, :], std[:, 0, :]))

            def gained_low(m, d):
                dve.wait_ge(xh_ready, m * KT + d + 1)
                V.scalar_tensor_tensor(xl[:, d, :], x[:, d, :], gain[:, m, d:d + 1], xh[:, d, :].bitcast(F32),
                                       ALU.mult, ALU.subtract).then_inc(xn_ready, 1)

            def residual(n, c_last, scale, m=None):
                for d in range(KT):
                    if d < KT - 1:
                        dve.wait_ge(down_mm, n * (KT - 1) + d + 1)
                    else:
                        dve.wait_ge(chunk_mm, c_last + 1)
                    V.scalar_tensor_tensor(x[:, d, :], ps[:, d, :], scale, x[:, d, :], ALU.mult,
                                           ALU.add).then_inc(x_ready, 1)
                    if m is not None and d:
                        gained_low(m, d - 1)
                if m is not None:
                    gained_low(m, KT - 1)

            def ffn(m, after=None):
                c0, u0 = C_FFN[m], m * FT
                invert((0, 2, 3, 5)[m])
                with dve.Fori(0, FT // 2) as i:
                    step.loop(i, 4)
                    for k in range(2):
                        f = i * 2 + k
                        dve.wait_ge(chunk_mm, i * 4 + (c0 + 2 * k + 2))
                        V.tensor_tensor(uf[:, k, :], ps[:, 2 * k, :], std[:, 0, :], ALU.mult).then_inc(a_scaled, 1)
                        V.tensor_tensor(bf[:, k, :], ps[:, 2 * k + 1, :], std[:, 0, :], ALU.mult).then_inc(pair_free, 1)
                        dve.wait_ge(pair_free, f + (G_FFN[m] + 1))
                        dve.wait_ge(silu_ready, f + (u0 + 1))
                        step(V.tensor_tensor(bf[:, k, :], uf[:, k, :], bf[:, k, :], ALU.mult))
                        split(uh[:, f, :], ul[:, f, :], bf[:, k, :]).then_inc(u_ready, 1)
                        dve.wait_ge(u_ready, f + (u0 + 1))
                    step.end(FT // 2)
                residual((0, 1, 2, 4)[m], C_FFN[m] + UP + DOWN - 1, 0.5, after)

            V.memset(ones[:, :], 1.0).then_inc(consts_set, 1)
            V.memset(eps[:, :], EPS).then_inc(consts_set, 1)
            V.memset(relw[BUCKETS:BUCKETS + 1, :], BIG).then_inc(consts_set, 1)
            dve.wait_ge(consts_in, 16 * 5)
            for d in range(KT):
                dve.wait_ge(x_turned, d + 1)
                V.tensor_copy(x[:, d, :], ps[:, d % 4, :]).then_inc(x_ready, 1)
                dve.wait_ge(x_ready, d + 1)
                if d % 2:
                    V.memset(mark[:, 0:1], 0.0).then_inc(pair_free, 1)
                if d:
                    gained_low(0, d - 1)
            gained_low(0, KT - 1)
            dve.wait_ge(rel_mm, 1)
            for k in range(2):
                step(V.tensor_copy(relo[:, k * (REL // 2):(k + 1) * (REL // 2)], ps[0:NH, 4 + k, 0:REL // 2]))
            step(V.tensor_scalar(qkg[:, 0:1], qkg[:, 0:1], -(DH ** -0.5), None, ALU.mult))
            V.memset(mark[:, 0:1], 0.0).then_inc(rel_out, 1)
            dve.wait_ge(rel_stored, 16)
            ffn(0, after=1)

            def twice(r):
                return bass.AP(r.tensor, r.offset, [list(r.ap[0]), [0, 2], [1, T]])

            def rotate(h, c_end, which):
                b = 2 * which
                rot = (rotq, rotk)[which]
                dve.wait_ge(chunk_mm, c_end)
                V.tensor_tensor(rt[:, 0, :], ps[:, b, :], rot[:, 0, :], ALU.mult)
                V.tensor_tensor(rt[:, 1, :], ps[:, b + 1, :], rot[:, 1, :], ALU.mult)
                V.tensor_tensor(rt[:, 2, :], ps[:, b, :], rot[:, 1, :], ALU.mult)
                step(V.tensor_tensor(rt[:, 3, :], ps[:, b + 1, :], rot[:, 0, :], ALU.mult))
                V.tensor_tensor(qf[:, 0, :], rt[:, 0, :], rt[:, 1, :], ALU.subtract).then_inc(pair_free, 1)
                step(V.tensor_tensor(qf[:, 1, :], rt[:, 2, :], rt[:, 3, :], ALU.add))
                split(qkh[:, which, :, :], qkl[:, which, :, :], qf).then_inc(qk_ready, 1)

            def ret_values(t):
                step(V.tensor_copy(vh[:, t, :], ps[:, 4 + t, :]))
                return V.tensor_tensor(vl[:, t, :], ps[:, 4 + t, :], vh[:, t, :].bitcast(F32), ALU.subtract)

            def ret_main(h, c0, g0, i=None, n=0):
                dve.wait_ge(chunk_mm, chunk(c0, i, 16)[0] + 4)
                ret_values(0)
                for j in range(TT):
                    o0, w = (0, 512, 896, 1152)[j], T - j * P
                    dve.wait_ge(s_mm, h * TT + (j + 1))
                    V.tensor_tensor(af[:, o0:o0 + w], ps[:, j, 0:w], dec[:, h, 0:w], ALU.mult).then_inc(s_read, 1)
                for t in range(1, TT):
                    last = ret_values(t)
                last.then_inc(v_ready, 1)
                for j in range(TT):
                    o0, w = (0, 512, 896, 1152)[j], T - j * P
                    dve.wait_ge(s_read, h * TT + (j + 1))
                    split(ah[:, o0:o0 + w], al[:, o0:o0 + w], af[:, o0:o0 + w]).then_inc(a_ready, 1)
                for k in range(2):
                    b = 2 * k
                    dve.wait_ge(chunk_mm, chunk(c0, i, 16)[0] + (6 + b))
                    V.tensor_tensor(sx[:, b:b + 2, :], ps[:, b:b + 2, :], twice(rn), ALU.mult).then_inc(pair_free, 1)
                    dve.wait_ge(pair_free, g0 + (k + 1))
                    V.memset(mark[:, 0:1], 0.0).then_inc(sx_ready, 1)
                    dve.wait_ge(sig_ready, h * 2 + (k + 1))
                    V.tensor_tensor(sx[:, b:b + 2, :], sx[:, b:b + 2, :], sg[:, :, :], ALU.mult).then_inc(sg_ready, 1)

            def ret_outputs(h):
                dve.wait_ge(sg_ready, h * 2 + 2)
                for v in range(4 + 2):
                    if v < 4:
                        dve.wait_ge(osq_ready, h * 4 + (v + 1))
                        step.add(V.tensor_tensor(onf[:, v, :], ps[:, 4 + v, :], sx[:, v, :], ALU.mult))
                    if 0 <= v - 1 < 4:
                        step.wait(1 if v < 4 else 0)
                        step.add(V.tensor_copy(onh[:, v - 1, :], onf[:, v - 1, :]))
                    if v - 2 >= 0:
                        step.wait((2, 2, 1, 0)[v - 2])
                        V.tensor_tensor(onl[:, v - 2, :], onf[:, v - 2, :], onh[:, v - 2, :].bitcast(F32),
                                        ALU.subtract).then_inc(on_ready, 1)
                dve.wait_ge(on_ready, h * 4 + 4)

            def ret_invert(h):
                dve.wait_ge(ostd_ready, h + 1)
                step(V.reciprocal(std[:, 0, :], std[:, 0, :]))

            def ret_residual(c0, i=None, last=False):
                for k in range(4):
                    b = 2 * (k % 2)
                    dve.wait_ge(chunk_mm, chunk(c0 + k, i, 16)[0] + 1)
                    step(V.tensor_tensor(rt[:, b:b + 2, :], ps[:, b:b + 2, :], twice(std[:, 0, :]), ALU.mult))
                    ins = V.tensor_tensor(x[:, 2 * k:2 * k + 2, :], x[:, 2 * k:2 * k + 2, :], rt[:, b:b + 2, :], ALU.add)
                    if not last:
                        ins.then_inc(pair_free, 1)
                    else:
                        ins.then_inc(x_ready, 2)
                        V.memset(mark[:, 0:1], 0.0).then_inc(pair_free, 1)
                        dve.wait_ge(x_ready, 2 * KT + 2 * k + 2)
                        if k:
                            gained_low(2, 2 * k - 2)
                            gained_low(2, 2 * k - 1)
                if last:
                    gained_low(2, KT - 2)
                    gained_low(2, KT - 1)

            dve.wait_ge(ret_in, 32)
            dve.wait_ge(std_ready, 2)
            step(V.reciprocal(rn, std[:, 0, :]))
            step(V.tensor_tensor(rotq[:, :, :], rotq[:, :, :], twice(rn), ALU.mult))
            step(V.tensor_tensor(rotk[:, :, :], rotq[:, :, :], twice(rn), ALU.mult))
            rotate(0, C_RET + 2, 0)
            rotate(0, C_RET + 4, 1)
            with dve.Fori(0, RH - 1) as h:
                step.loop(h, 4 + 4 + 8 + 3 + 1 + 3 + 4)
                g = h * 8 + (G_RET + 2)
                ret_main(h, C_RET + 4, g, h)
                ret_outputs(h)
                rotate(h + 1, h * 16 + (C_RET + 14), 0)
                ret_invert(h)
                rotate(h + 1, h * 16 + (C_RET + 16), 1)
                ret_residual(C_RET + 16, h)
                step.end(RH - 1)
            ret_main(RH - 1, C_RET + 52, G_RET + 2 + 8 * (RH - 1))
            ret_outputs(RH - 1)
            ret_invert(RH - 1)
            ret_residual(C_RET + 60, last=True)
            ffn(1, after=3)
            ffn(2, after=4)

            def inputs(j):
                dve.wait_ge(chunk_mm, C_NSA + 2 * j + 2)
                for g in range(NG):
                    for par in range(2):
                        s = DH * (g % 2)

                        def half(a):
                            return a[s:s + DH, :].rearrange("d (t two) -> d t two", two=2)[:, :, par]

                        ins = V.tensor_tensor(z[DH * par:DH * (par + 1), j, g, :], half(ps[:, 2 * j + g // 2, :]),
                                              half(nrn), ALU.mult)
                        if (g, par) != (NG - 1, 1):
                            step.add(ins)
                ins.then_inc(pair_free, 1)
                dve.wait_ge(pair_free, G_NSA + j + 1)

            def blocks(j):
                zz = z[:, j, :, :]
                src = bass.AP(zz.tensor, zz.offset, [list(zz.ap[0]), [1, LP], [T // 2, NG], [CMP_STRIDE // 2, NC]])
                pp = pos[:, j, :]
                add = bass.AP(pp.tensor, pp.offset, [list(pp.ap[0]), [1, LP], [0, NG], [0, NC]])
                dst = u[:, 0:LP * GN].rearrange("p (l g n) -> p l g n", l=LP, g=NG)
                step(V.tensor_tensor(dst, src, add, ALU.add))
                split(uch[:, :], ucl[:, :], u[:, 0:LP * GN]).then_inc(uc_ready, 1)

            def hidden_out(j):
                dve.wait_ge(gelu_ready, j + 1)
                V.memset(mark[:, 0:1], 0.0).then_inc(pair_free, 1)
                dve.wait_ge(pair_free, G_NSA + (4, 6)[j])

            def head_copy(n):
                b = (0, 0, 0, 2, 0, 2)[n]
                dve.wait_ge(chunk_mm, C_NSA + (6, 12, 18, 20, 22, 24)[n])
                V.tensor_tensor(hpair[n], ps[:, b:b + 2, :], twice(nrn), ALU.mult).then_inc(pair_free, 1)

            def head_norm(n):
                dve.wait_ge(hstd_ready, n + 1)
                step(V.reciprocal(std[:, :, :], std[:, :, :]))
                col = 0 if n >= 2 else 2 + n
                V.scalar_tensor_tensor(hpair[n], hpair[n], qkg[:, col:col + 1], std[:, :, :], ALU.mult,
                                       ALU.mult).then_inc(hn_ready, 1)
                dve.wait_ge(hn_ready, n + 1)

            def keys(n):
                src = [hpair[n][DH * (g % 2):DH * (g % 2) + DH, g // 2, :] for g in range(NG)]
                for g in range(NG):
                    for half in (0, DH):
                        step.add(V.tensor_copy(kh[half:half + DH, n, g, :], src[g]))
                step.wait()
                for g in range(NG):
                    s = DH * (g % 2)
                    for half in (0, DH):
                        step.add(V.tensor_tensor(kl[half:half + DH, n, g, :], src[g],
                                                 kh[s:s + DH, n, g, :].bitcast(F32), ALU.subtract))
                step.wait()

            dve.wait_ge(ret_in, 80)
            step(V.tensor_copy(gwh[:, :, :], gwf[:, :, :]))
            V.tensor_tensor(gwl[:, :, :], gwf[:, :, :], gwh[:, :, :].bitcast(F32), ALU.subtract).then_inc(gw_ready, 1)
            dve.wait_ge(std_ready, 5)
            V.reciprocal(nrn, std[:, 0, :]).then_inc(r_ready, 1)
            dve.wait_ge(r_ready, 1)
            inputs(0)
            blocks(0)
            inputs(1)
            head_copy(0)
            dve.wait_ge(r_turned, 1)
            V.tensor_copy(rcol[:, :], ps[:, 7, :].rearrange("p (i q) -> p i q", i=TT)[:, :, 0]).then_inc(rcol_ready, 1)
            hidden_out(0)
            blocks(1)
            head_norm(0)
            head_copy(1)
            hidden_out(1)
            keys(0)
            head_norm(1)
            head_copy(2)
            head_copy(3)
            keys(1)
            head_norm(2)
            head_copy(4)
            head_norm(3)
            head_copy(5)
            head_norm(4)
            head_norm(5)
            dve.wait_ge(sig_ready, 2 * RH + 4)
            gm = gates[:, :, CMPB, 0]
            V.tensor_scalar(gm, gm, rowmask, None, ALU.mult).then_inc(gates_set, 1)
            dve.wait_ge(hn_ready, 6)
            step(V.tensor_copy(qs[0:DH, 0, :], qn[0:DH, 0, :]))
            V.tensor_tensor(qs[DH:P, 0, :], qn[0:DH, 0, :], qs[0:DH, 0, :].bitcast(F32), ALU.subtract).then_inc(qs_ready, 1)
            step(V.tensor_copy(qs[DH:P, 1, :], qn[DH:P, 0, :]))
            V.tensor_tensor(qs[0:DH, 1, :], qn[DH:P, 0, :], qs[DH:P, 1, :].bitcast(F32), ALU.subtract).then_inc(qs_ready, 1)
            dve.wait_ge(chunk_mm, C_NSA + 28)
            for t in range(TT):
                step(V.tensor_scalar(vf[:, t, :, :, :].rearrange("p b g d -> p (b g d)"), ps[:, 4 + t, :],
                                     rcol[:, t:t + 1], None, ALU.mult))
            dve.wait_ge(w2_mm, 1)
            dve.wait_ge(kcstd_ready, 1)
            step(V.memset(vcf[:, :, :], 0.0))
            step(V.tensor_copy(vcf[0:NC, :, :], ps[0:NC, 1, P:P + NG * DH].rearrange("n (g d) -> n g d", g=NG)))
            step(V.memset(u[:, 3 * P * 4:3 * P * 4 + NG * NCP], 0.0))
            zero = u[:, 3 * P * 4:3 * P * 4 + NG * NCP].rearrange("p (g n) -> p g n", g=NG)
            step(V.tensor_copy(kch[:, :, :], zero))
            step(V.tensor_copy(kcl[:, :, :], zero))
            step(V.reciprocal(kct[:, 1, :], kct[:, 1, :]))
            step(V.scalar_tensor_tensor(kcf, ps[0:DH, 1, 0:GN], qkg[0:DH, 1:2], kct[:, 1, :], ALU.mult, ALU.mult))
            ksrc = kcf.rearrange("p (g n) -> p g n", g=NG)
            for half in (0, DH):
                step(V.tensor_copy(kch[half:half + DH, :, 0:NC], ksrc))
            for half in (0, DH):
                step(V.tensor_tensor(kcl[half:half + DH, :, 0:NC], ksrc, kch[0:DH, :, 0:NC].bitcast(F32), ALU.subtract))
            V.memset(mark[:, 0:1], 0.0).then_inc(cmp_ready, 1)
            for b in range(2):
                V.memset(pr[:, b, 2 * PB:PW], 0.0).then_inc(cmp_ready, 1)

            def stage_q(h, tile, hh, b, half):
                s = DH * (hh % 2)
                src = qn[s:s + DH, tile, :]
                if half == 0:
                    step.add(V.tensor_copy(qs[s:s + DH, b, :], src))
                else:
                    step.wait()
                    V.tensor_tensor(qs[DH - s:P - s, b, :], src, qs[s:s + DH, b, :].bitcast(F32),
                                    ALU.subtract).then_inc(qs_ready, 1)

            def read_score(h, b, k):
                br, ti = k // TT, k % TT
                o, n = p_slice(br, ti)
                c, st = (ti * P + P - CMP_LEN, CMP_STRIDE) if br == CMPB else (ti * P + P - 1, 1)
                t = tn[:, b, c:c + 1]
                bias = bass.AP(t.tensor, t.offset, [list(t.ap[0]), [-st, n]])
                dve.wait_ge(sc_mm, h * NS + k + 1)
                V.memset(mark[:, k + 1:k + 2], 0.0)
                V.tensor_tensor_reduce(out=pr[:, b, o:o + n], in0=ps[:, k % 3, 0:n], in1=bias, scale=1.0,
                                       scalar=3e38, op0=ALU.add, op1=ALU.min,
                                       accum_out=mn[:, b, k:k + 1]).then_inc(sc_read, 1)

            def coefficients(h, b, br, half):
                k = br * TT
                if half == 0:
                    dve.wait_ge(exp_done, h * NS + (k + TT))
                    step.add(V.reciprocal(coef[:, b, k:k + TT], rsum[:, b, k:k + TT]))
                else:
                    step.wait()
                    V.tensor_tensor(coef[:, b, k:k + TT], coef[:, b, k:k + TT], gates[:, h, br, :],
                                    ALU.mult).then_inc(coef_ready, 1)

            def pt_low(h, hh, k):
                dve.wait_ge(pt_hi, h * NTT + k + 1)
                np_, n = (NCP, T) if k == 8 else (P, T - P * (k % 4))
                V.tensor_tensor(ptl[k % 3][0:np_, 0:n], ps[0:np_, 3 + k % 3, 0:n],
                                pth[k % 3][0:np_, 0:n].bitcast(F32), ALU.subtract).then_inc(pt_ready, 1)

            def o_out(h, tile, hh, part):
                s = DH * (hh % 2)
                o = sq[s:s + DH, 1, :]
                if part == 0:
                    dve.wait_ge(o_half, h + 1)
                    step.add(V.tensor_tensor(o, ps[0:DH, 6 + hh % 2, :], sq[s:s + DH, 0, :], ALU.add))
                elif part == 1:
                    step.wait()
                    step.add(V.tensor_copy(xh[s:s + DH, tile, :], o))
                else:
                    step.wait()
                    V.tensor_tensor(xl[s:s + DH, tile, :], o, xh[s:s + DH, tile, :].bitcast(F32),
                                    ALU.subtract).then_inc(o_ready, 1)

            def step_of(h, hh, g, more=True):
                first = isinstance(h, int) and h == 0
                last_q = not more or (hh == HPG - 2 and isinstance(g, int) and g == NG - 1)
                if more:
                    dve.wait_ge(bias_landed[(hh + 1) % 2], (g * 2 + (hh + 1) // 2) * 16 + 16)
                for k in range(NS):
                    if more:
                        read_score(h + 1, (hh + 1) % 2, k)
                    if LAG <= k < LAG + NTT:
                        pt_low(h, hh, k - LAG)
                    if k in (1, 2):
                        coefficients(h, hh % 2, CMPB, k - 1)
                    if more and k in (5, 6):
                        coefficients(h + 1, (hh + 1) % 2, SLC, k - 5)
                    if more and k in (9, 10):
                        coefficients(h + 1, (hh + 1) % 2, WIN, k - 9)
                    if k - O_AT in (0, 1, 2) and not first:
                        o_out(h - 1, g * 2 + (hh - 1) // 2, (hh + 1) % 2, k - O_AT)
                    if k in (7, 8) and not last_q:
                        n = hh + 2
                        stage_q(h + 2, g * 2 + n // 2, n % 2, n % 2, k - 7)

            dve.wait_ge(cmp_ready, 3)
            dve.wait_ge(bias_landed[0], 16)
            for k in range(NS):
                read_score(0, 0, k)
            for br in (SLC, WIN):
                for half in range(2):
                    coefficients(0, 0, br, half)
            for hh in range(HPG):
                step_of(hh, hh, 0)
            with dve.Fori(1, NG - 1) as g4:
                step.loop(g4, 6 * HPG, 1)
                for hh in range(HPG):
                    step_of(g4 * HPG + hh, hh, g4)
                step.end(NG - 2, 1)
            for hh in range(HPG):
                step_of(NH - HPG + hh, hh, NG - 1, more=hh < HPG - 1)
            for part in range(3):
                o_out(NH - 1, NH // 2 - 1, HPG - 1, part)
            residual(3, C_FFN[3] - 1, 1.0, 5)
            ffn(3)
            for t in range(TT):
                for q in range(2):
                    n = 2 * t + q
                    dve.wait_ge(y_mm, n + 1)
                    V.tensor_copy(xin[:, t, q * T:(q + 1) * T], ps[:, n % 4, :]).then_inc(y_ready, 4)


def constants():
    sq = np.zeros((P, 2 * P + 1), np.float32)
    sq[:, 0:P] = np.eye(P)
    sq[0:64, P:P + 64] = 1
    sq[64:P, P + 64:2 * P] = 1
    sq[:, 2 * P] = np.arange(P) >= CMP_LEN - 1
    half = DK // 2
    inv = np.float32(10000.0) ** (-np.arange(half, dtype=np.float32) / np.float32(half))
    ang = (np.arange(T, dtype=np.float32)[None, :] * inv[:, None]).astype(np.float32)
    rot = np.stack([np.cos(ang), np.sin(ang)], 1).astype(np.float32)
    lg = np.log(1.0 - 2.0 ** (-5.0 - np.arange(RH, dtype=np.float64)))
    diff = np.arange(T)[None, None, :] - np.arange(P)[:, None, None]
    dec = np.where(diff >= 0, np.exp(lg[None, :, None] * np.maximum(diff, 0)) * DK ** -0.5, 0.0).astype(np.float32)
    dist = np.arange(REL) - P
    n = np.maximum(dist, 0)
    nf = np.maximum(n, 16).astype(np.float32)
    large = 16 + (np.log(nf / np.float32(16)) / np.float32(np.log(8.0)) * np.float32(16)).astype(np.int32)
    bucket = np.where(n < 16, n, np.minimum(large, 31))
    onehot = np.zeros((BUCKETS + 1, REL), np.float32)
    onehot[bucket[dist >= 0], np.arange(REL)[dist >= 0]] = -1
    onehot[BUCKETS, dist < 0] = 1
    return sq, rot, dec, onehot


def tall_chunks(w):
    k, n = w.shape
    return w.reshape(k // T, 4, P, n // 256, 256).transpose(3, 0, 2, 1, 4).reshape(-1, P, CW)


def wide_chunks(w):
    return w.reshape(-1, P, CW)


def natural_chunks(w):
    return w.reshape(4, 2, P, T).transpose(0, 2, 1, 3).reshape(-1, P, CW)


def ffn_chunks(gu, down):
    gu = gu.reshape(D, 2, FT, P).transpose(0, 2, 1, 3).reshape(D, 2 * F)
    return [tall_chunks(gu), wide_chunks(down)]


def kernel(**inputs):
    import concourse.bacc as bacc
    from concourse.bass_utils import run_bass_kernel_spmd

    a = {k: np.ascontiguousarray(v) for k, v in inputs.items()}
    gu1, dn1, gu2, dn2 = a["ffn1_w_gu"], a["ffn1_w_down"], a["ffn2_w_gu"], a["ffn2_w_down"]
    win, wout = a["ret_w_in"][0], a["ret_w_out"][0]
    rq = [tall_chunks(win[:, DK * h:DK * (h + 1)]) for h in range(RH)]
    rk = [tall_chunks(win[:, D + DK * h:D + DK * (h + 1)]) for h in range(RH)]
    rv = [natural_chunks(win[:, 2 * D + DV * h:2 * D + DV * (h + 1)]) for h in range(RH)]
    rg = [tall_chunks(win[:, 4 * D + DV * h:4 * D + DV * (h + 1)]) for h in range(RH)]
    ro = [tall_chunks(wout[DV * h:DV * (h + 1)]) for h in range(RH)]
    nin = a["nsa_w_in"][0]
    kc, vc, ks, vs, kw, vw = [nin[:, D + 256 * i:D + 256 * (i + 1)] for i in range(6)]
    parts = ffn_chunks(gu1[0], dn1[0]) + [rq[0], rk[0]]
    for h in range(RH):
        parts += [rv[h], rg[h]] + ([rq[h + 1], rk[h + 1]] if h < RH - 1 else []) + [ro[h]]
    parts += ffn_chunks(gu2[0], dn2[0]) + ffn_chunks(gu1[1], dn1[1])
    w1 = a["nsa_cmp_w1"][0]
    parts += [tall_chunks(w) for w in (kc, vc, ks, w1[0], kw, w1[1], nin[:, 0:D])]
    parts += [natural_chunks(np.concatenate([vs, vw], 1))]
    parts += [wide_chunks(a["nsa_w_out"][0])] + ffn_chunks(gu2[1], dn2[1])
    stream = np.ascontiguousarray(np.concatenate(parts, 0))
    assert stream.shape == (NCHUNK, P, CW)
    norms = [a["ffn1_norm"][0], a["mix_norm"][0], a["ffn2_norm"][0], a["ffn1_norm"][1], a["mix_norm"][1], a["ffn2_norm"][1]]
    gains = [a["nsa_q_gain"][0], a["nsa_k_gain"][0, 0], a["nsa_k_gain"][0, 1], a["nsa_k_gain"][0, 2]]
    sq, rot, dec, onehot = constants()
    arrays = {
        "x_in": a["x"].reshape(T, D),
        "stream": stream,
        "norm_g": np.stack(norms).reshape(6, KT, P).transpose(2, 0, 1),
        "gate_w": nin[:, -48:].reshape(D, 3, NH)[:, [1, 2, 0]].reshape(KT, P, 48).transpose(1, 0, 2),
        "cmp_w2": a["nsa_cmp_w2"][0].reshape(2, 2, P, DH).transpose(2, 0, 1, 3),
        "cmp_pos": a["nsa_cmp_pos"][0].reshape(2, LP, 2, DH).transpose(2, 3, 0, 1).reshape(P, 2, LP),
        "qk_gain": np.tile(np.stack(gains, 1), (2, 1)),
        "rel": a["rel_bias"],
        "c_sq": sq, "c_rot": rot, "c_dec": dec, "c_rel": onehot,
    }
    arrays = {k: np.ascontiguousarray(v) for k, v in arrays.items()}
    nc = bacc.Bacc("TRN2", target_bir_lowering=False, num_devices=1)
    args = {k: nc.dram_tensor(k, v.shape, mybir.dt.from_np(v.dtype), kind="ExternalInput").ap() for k, v in arrays.items()}
    rel_rows = nc.dram_tensor("rel_rows", (NH, REL), F32, kind="Internal").ap()
    out = nc.dram_tensor("out", (T, D), F32, kind="ExternalOutput").ap()
    trunk(nc, **args, rel_rows=rel_rows, out=out)
    r = run_bass_kernel_spmd(nc, [arrays], core_ids=[0])
    return r.results[0]["out"].reshape(1, T, D)
```

```python
from contextlib import ExitStack

import numpy as np
import concourse.bass as bass
from concourse import mybir

F32 = mybir.dt.float32
F32R = mybir.dt.float32r
ALU = mybir.AluOpType
ACT = mybir.ActivationFunctionType

P = 128
D = 1024
T = 512
KT = D // P
TT = T // P
F = 2816
FT = F // P
EPS = 1e-6
RH, DK, DV = 4, 256, 512
NH, NG, HPG, DH = 16, 4, 4, 64
CMP_LEN, CMP_STRIDE = 32, 16
NC = (T - CMP_LEN) // CMP_STRIDE + 1
NCP = NC + 1
GN = NG * NC
LP = CMP_LEN // 2
BUCKETS = 32
REL = 640
BIG = 1e30

SLOTS = 4
CW = 1024
UP, DOWN = 2 * FT, FT
C_FFN = [0, 0, 0, 0]
C_FFN[0] = 0
C_RET = C_FFN[0] + UP + DOWN
C_FFN[1] = C_RET + RH * 16
C_FFN[2] = C_FFN[1] + UP + DOWN
C_NSA = C_FFN[2] + UP + DOWN
C_NOUT = C_NSA + 28
C_FFN[3] = C_NOUT + 8
NCHUNK = C_FFN[3] + UP + DOWN
G_FFN = [2, 0, 0, 0]
G_RET = G_FFN[0] + FT
G_FFN[1] = G_RET + RH * 8
G_FFN[2] = G_FFN[1] + FT
G_NSA = G_FFN[2] + FT
G_FFN[3] = G_NSA + 10
NS, NTT = 12, 9
SLC, WIN, CMPB = 0, 1, 2
LAG = 1
V_LAG = 3
V_LEFT = NS - LAG - V_LAG
O_AT = 3
P_OFF = [0, 128, 384, 768]
PB = 1280
PW = 2 * PB + TT * NCP


def p_slice(b, i):
    if b == CMPB:
        return 2 * PB + i * NCP, 7 + 8 * i
    return b * PB + P_OFF[i], P * (i + 1)


def trunk(nc, x_in, stream, norm_g, gate_w, cmp_w2, cmp_pos, qk_gain, rel, c_sq, c_rot, c_dec, c_rel, rel_rows, out):
    ctx = ExitStack()
    with ctx:
        def sem(name):
            return ctx.enter_context(nc.semaphore(name))

        def sb(name, shape, dt=F32, scope=ctx):
            return scope.enter_context(nc.sbuf_tensor(name, shape, dt))

        x = sb("x", [P, KT, T])
        xh = sb("xh", [P, KT, T], F32R)
        xl = sb("xl", [P, KT, T], F32R)
        raw = sb("raw", [P, SLOTS, CW])
        wh = sb("wh", [P, SLOTS, CW], F32R)
        wl = sb("wl", [P, SLOTS, CW], F32R)
        sq = sb("sq", [P, 2, T])
        with ExitStack() as s:
            std = sb("std", [P, 2, T], F32, s)
        pt3 = sb("pt3", [P, 2, T], F32R)
        csq = sb("csq", [P, 2 * P + 1])
        ident = csq[:, 0:P]
        bones = csq[:, P:2 * P]
        rowmask = csq[:, 2 * P:2 * P + 1]
        ones = sb("ones", [P, P])
        eps = sb("eps", [P, 1])
        amark = sb("amark", [P, 1])
        pmark = sb("pmark", [1, 2])
        mark = sb("mark", [1, 16])
        gain = sb("gain", [P, 6, KT])
        qkg = sb("qkg", [P, 4])

        with ExitStack() as s:
            uh = sb("uh", [P, FT, T], F32R, s)
            ul = sb("ul", [P, FT, T], F32R, s)
            uf = sb("uf", [P, 2, T], F32, s)
            bf = sb("bf", [P, 2, T], F32, s)
        with ExitStack() as s:
            rotq = sb("rotq", [P, 2, T], F32, s)
            rotk = sb("rotk", [P, 2, T], F32, s)
            rnt = sb("rnt", [P, T], F32, s)
            rn = rnt[:, :]
            sx = sb("sx", [P, 4, T], F32, s)
            dec = sb("dec", [P, RH, T], F32, s)
            rt = sb("rt", [P, 4, T], F32, s)
            qkh = sb("qkh", [P, 2, 2, T], F32R, s)
            qkl = sb("qkl", [P, 2, 2, T], F32R, s)
            vh = sb("vh", [P, TT, DV], F32R, s)
            vl = sb("vl", [P, TT, DV], F32R, s)
            sg = sb("sg", [P, 2, T], F32, s)
            af = sb("af", [P, PB], F32, s)
            qf = af[:, 0:2 * T].rearrange("p (a t) -> p a t", a=2)
            ah = sb("ah", [P, PB], F32R, s)
            al = sb("al", [P, PB], F32R, s)
            onf = rt
            onh = sb("onh", [P, 4, T], F32R, s)
            onl = sb("onl", [P, 4, T], F32R, s)
        with ExitStack() as s:
            qn = sb("qn", [P, KT, T], F32, s)
            kh = sb("kh", [P, 2, NG, T], F32R, s)
            kl = sb("kl", [P, 2, NG, T], F32R, s)
            vf = sb("vf", [P, TT, 2, NG, DH], F32, s)
            vst = sb("vst", [P, TT, 2, 2 * DH], F32R, s)
            rcol = sb("rcol", [P, TT], F32, s)
            gates = sb("gates", [P, NH, 3, TT], F32, s)
            kch = sb("kch", [P, NG, NCP], F32R, s)
            kcl = sb("kcl", [P, NG, NCP], F32R, s)
            vcf = sb("vcf", [NCP, NG, DH], F32, s)
            vcst = sb("vcst", [NCP, 2 * DH], F32R, s)
            qs = sb("qs", [P, 2, T], F32R, s)
            mn = sb("mn", [P, 2, NS], F32, s)
            rsum = sb("rsum", [P, 2, NS], F32, s)
            coef = sb("coef", [P, 2, NS], F32, s)
            with ExitStack() as s2:
                z = sb("z", [P, 2, NG, T // 2], F32, s2)
                u = sb("u", [P, 4 * T], F32, s2)
                uch = sb("uch", [P, LP * GN], F32R, s2)
                ucl = sb("ucl", [P, LP * GN], F32R, s2)
                pos = sb("pos", [P, 2, LP], F32, s2)
                w2 = sb("w2", [P, 2, 2, DH], F32, s2)
            with ExitStack() as s2:
                tn = sb("tn", [P, 2, T], F32, s2)
                pr = sb("pr", [P, 2, PW], F32, s2)
                pth2 = sb("pth", [P, 2, T], F32R, s2)
                ptl2 = sb("ptl", [P, 2, T], F32R, s2)
        pth = [pth2[:, 0, :], pth2[:, 1, :], pt3[:, 0, :]]
        ptl = [ptl2[:, 0, :], ptl2[:, 1, :], pt3[:, 1, :]]
        osq = [sq[:, 0, :], sq[:, 1, :], std[:, 0, :], std[:, 1, :]]
        hpair = [qn[:, a:a + 2, :] for a in (6, 4, 0, 2, 4, 6)]
        HSS_BANK = (4, 6, 4, 6, 4, 2)
        HN_FREE = (3, 5, 7, 8, 9, 10)
        nrn = vf[:, 1, :, :, :].rearrange("p b g d -> p (b g d)")
        with ExitStack() as s:
            xin = sb("xin", [P, TT, D], F32, s)
            relw = sb("relw", [BUCKETS + 1, NH], F32, s)
            onehot = sb("onehot", [BUCKETS + 1, REL], F32, s)
            relo = sb("relo", [NH, REL], F32, s)
        ps = ctx.enter_context(nc.psum_tensor("ps", [P, 8, T], F32))
        gwf = vf[:, 0, :, :, :].rearrange("p b g d -> p (b g d)")[:, 0:KT * 48].rearrange("p (k n) -> p k n", k=KT)
        gw2 = vst[:, :, :, :].rearrange("p t b d -> p (t b d)")[:, 0:2 * KT * 48]
        gwh, gwl = [gw2[:, i * KT * 48:(i + 1) * KT * 48].rearrange("p (k n) -> p k n", k=KT) for i in range(2)]
        gl = z[:, 0, 0:2, :].rearrange("p g t -> p (g t)")[:, 0:4 * GN].rearrange("p (j t n) -> p j t n", j=2, t=2)
        gt = z[0:3 * NH, 1, 0:2, :].rearrange("p g t -> p (g t)")
        kct = u[0:DH, 0:2 * GN].rearrange("p (j n) -> p j n", j=2)
        kcf = u[0:DH, 2 * GN:3 * GN]

        raw_landed = [sem(f"raw_landed{i}") for i in range(SLOTS)]
        chunk_hi = sem("chunk_hi")
        chunk_lo = sem("chunk_lo")
        chunk_mm = sem("chunk_mm")
        r_ready = sem("r_ready")
        r_turned = sem("r_turned")
        rcol_ready = sem("rcol_ready")
        pair_free = sem("pair_free")
        consts_in = sem("consts_in")
        consts_set = sem("consts_set")
        rel_in = sem("rel_in")
        csq_in = sem("csq_in")
        x_in_landed = [sem(f"x_in_landed{t}") for t in range(TT)]
        x_turned = sem("x_turned")
        x_ready = sem("x_ready")
        sq_ready = sem("sq_ready")
        sq_sum = sem("sq_sum")
        ss_mm = sem("ss_mm")
        xh_ready = sem("xh_ready")
        a_scaled = sem("a_scaled")
        std_ready = sem("std_ready")
        xn_ready = sem("xn_ready")
        silu_ready = sem("silu_ready")
        u_ready = sem("u_ready")
        down_mm = sem("down_mm")
        act_step = sem("act_step")
        dve_step = sem("dve_step")
        pool_set = sem("pool_set")
        rel_mm = sem("rel_mm")
        rel_out = sem("rel_out")
        rel_stored = sem("rel_stored")
        ret_in = sem("ret_in")
        qk_ready = sem("qk_ready")
        v_ready = sem("v_ready")
        s_read = sem("s_read")
        osq_sum = sem("osq_sum")
        s_mm = sem("s_mm")
        a_ready = sem("a_ready")
        pv_mm = sem("pv_mm")
        osq_ready = sem("osq_ready")
        oss_mm = sem("oss_mm")
        ostd_ready = sem("ostd_ready")
        sig_ready = sem("sig_ready")
        sx_ready = sem("sx_ready")
        sg_ready = sem("sg_ready")
        on_ready = sem("on_ready")
        hsq_ready = sem("hsq_ready")
        hss_mm = sem("hss_mm")
        hstd_ready = sem("hstd_ready")
        hn_ready = sem("hn_ready")
        uc_ready = sem("uc_ready")
        gw_ready = sem("gw_ready")
        gate_mm = sem("gate_mm")
        gt_ready = sem("gt_ready")
        gate_turned = sem("gate_turned")
        gates_set = sem("gates_set")
        gelu_ready = sem("gelu_ready")
        w2_mm = sem("w2_mm")
        kcsq_ready = sem("kcsq_ready")
        kcss_mm = sem("kcss_mm")
        kcstd_ready = sem("kcstd_ready")
        cmp_ready = sem("cmp_ready")
        bias_landed = [sem("bias_landed0"), sem("bias_landed1")]
        qs_ready = sem("qs_ready")
        vf_ready = sem("vf_ready")
        vst_ready = sem("vst_ready")
        vst_half = sem("vst_half")
        sc_mm = sem("sc_mm")
        sc_read = sem("sc_read")
        exp_done = sem("exp_done")
        coef_ready = sem("coef_ready")
        p_scaled = sem("p_scaled")
        pt_mm = sem("pt_mm")
        pt_hi = sem("pt_hi")
        pt_ready = sem("pt_ready")
        apv_mm = sem("apv_mm")
        o_half = sem("o_half")
        o_ready = sem("o_ready")
        y_mm = sem("y_mm")
        y_even = sem("y_even")
        y_rest = sem("y_rest")
        y_stored = sem("y_stored")

        def chunk(c0, i=None, step=0):
            if i is None:
                return c0, c0 % SLOTS, c0 // SLOTS
            return i * step + c0, c0 % SLOTS, i * (step // SLOTS) + c0 // SLOTS

        block = ctx.enter_context(nc.Block())

        @block.sync
        def _(sp):
            def load(ch):
                c, slot, turn = ch
                sp.dma_start(raw[:, slot, :], stream[c]).then_inc(raw_landed[slot], 16)

            sp.dma_start(relw[0:BUCKETS, :], rel).then_inc(rel_in, 16)
            sp.dma_start(onehot[:, :], c_rel).then_inc(rel_in, 16)
            sp.dma_start(csq[:, :], c_sq).then_inc(csq_in, 16)
            for t in range(TT):
                sp.dma_start(xin[:, t, :], x_in[t * P:(t + 1) * P, :]).then_inc(x_in_landed[t], 16)
            sp.dma_start(gain[:, :, :], norm_g).then_inc(consts_in, 16)
            sp.dma_start(qkg[:, :], qk_gain).then_inc(consts_in, 16)
            for c in range(SLOTS):
                load(chunk(c))

            def loads(c0, n):
                with sp.Fori(0, n // SLOTS) as i:
                    for k in range(SLOTS):
                        ch = chunk(c0 + k, i, SLOTS)
                        sp.wait_ge(chunk_lo, ch[0] - (SLOTS - 1))
                        load(ch)
                for c in range(c0 + n // SLOTS * SLOTS, c0 + n):
                    sp.wait_ge(chunk_lo, c - (SLOTS - 1))
                    load(chunk(c))

            sp.wait_ge(rel_out, 1)
            sp.dma_start(rel_rows, relo[:, :]).then_inc(rel_stored, 16)
            loads(SLOTS, C_RET)
            sp.wait_ge(chunk_mm, C_RET)
            sp.dma_start(rotq[:, :, :], c_rot).then_inc(ret_in, 16)
            sp.dma_start(dec[:, :, :], c_dec).then_inc(ret_in, 16)
            loads(C_RET + SLOTS, C_NSA - C_RET)
            sp.wait_ge(chunk_mm, C_NSA)
            sp.dma_start(gwf[:, :, :], gate_w).then_inc(ret_in, 16)
            sp.dma_start(pos[:, :, :], cmp_pos).then_inc(ret_in, 16)
            sp.dma_start(w2[:, :, :, :], cmp_w2).then_inc(ret_in, 16)
            loads(C_NSA + SLOTS, C_NOUT - C_NSA - SLOTS)
            sp.wait_ge(rel_stored, 16)
            sp.wait_ge(cmp_ready, 2)
            sp.wait_ge(gates_set, 1)

            def bias(h, b):
                row = rel_rows[h]
                src = bass.AP(row.tensor, row.offset + 1, [[1, P], [1, T]])
                sp.dma_start(tn[:, b, :], src).then_inc(bias_landed[b], 16)

            bias(0, 0)
            bias(1, 1)
            loads(C_NOUT, SLOTS)
            with sp.Fori(1, NH // 2) as i:
                for b in range(2):
                    sp.wait_ge(sc_read, (i * 2 + (b - 1)) * NS)
                    bias(i * 2 + b, b)
            loads(C_NOUT + SLOTS, NCHUNK - C_NOUT - SLOTS)
            for n in range(2 * TT):
                q, t = n // 4, n % 4
                if q and t % 2 == 0:
                    sp.wait_ge(y_even, t // 2 + 1)
                else:
                    sp.wait_ge(y_rest, n + 1 if q == 0 else 5 + t // 2)
                sp.dma_start(out[t * P:(t + 1) * P, q * T:(q + 1) * T], xin[:, t, q * T:(q + 1) * T]).then_inc(y_stored, 16)
            sp.wait_ge(y_stored, 16 * 2 * TT)

        @block.gpsimd
        def _(pool):
            def low(ch):
                c, slot, turn = ch
                pool.wait_ge(chunk_hi, c + 1)
                nc.gpsimd.tensor_tensor(wl[:, slot, :], raw[:, slot, :], wh[:, slot, :].bitcast(F32),
                                        ALU.subtract).then_inc(chunk_lo, 1)

            def lows(c0, c1):
                n = c1 - c0
                if n >= SLOTS:
                    with pool.Fori(0, n // SLOTS) as i:
                        for k in range(SLOTS):
                            low(chunk(c0 + k, i, SLOTS))
                for c in range(c0 + n // SLOTS * SLOTS, c1):
                    low(chunk(c))

            acc = std[:, 1, :]

            def sum_squares(m):
                add = nc.gpsimd.tensor_tensor
                pool.wait_ge(sq_ready, m * KT + 2)
                add(acc, sq[:, 0, :], sq[:, 1, :], ALU.add).then_inc(sq_sum, 1)
                for d in range(2, KT):
                    pool.wait_ge(sq_ready, m * KT + d + 1)
                    pool.wait_ge(sq_sum, m * (KT - 1) + d - 1)
                    add(acc, acc, sq[:, d % 2, :], ALU.add).then_inc(sq_sum, 1)

            nc.gpsimd.memset(pmark[:, :], 0.0).then_inc(pool_set, 1)
            pool.wait_ge(pool_set, 1)
            ahead = SLOTS - 1
            lows(0, ahead)
            sum_squares(0)
            lows(ahead, C_RET + ahead)
            sum_squares(1)
            low(chunk(C_RET + ahead))
            lows(C_RET + 4, C_RET + 16)
            def sum_outputs(h):
                pool.wait_ge(osq_ready, h * 4 + 4)
                for v in range(1, 4):
                    if v > 1:
                        pool.wait_ge(osq_sum, h * 3 + (v - 1))
                    nc.gpsimd.tensor_tensor(osq[0], osq[0], osq[v], ALU.add).then_inc(osq_sum, 1)

            with pool.Fori(0, RH - 1) as h:
                sum_outputs(h)
                for k in range(16):
                    low(chunk(C_RET + 16 + k, h, 16))
            sum_outputs(RH - 1)
            at = C_RET + 64
            for m, c0 in ((2, C_FFN[1]), (3, C_FFN[2]), (4, C_NSA)):
                lows(at, c0 + ahead)
                sum_squares(m)
                at = c0 + ahead
            lows(at, C_NOUT)
            def stage_v(g, br):
                if br == CMPB:
                    src, v_h, v_l = vcf[:, g, :], vcst[:, 0:DH], vcst[:, DH:2 * DH]
                else:
                    src, v_h, v_l = vf[:, :, br, g, :], vst[:, :, br, 0:DH], vst[:, :, br, DH:2 * DH]
                if not (isinstance(g, int) and g == 0):
                    pool.wait_ge(apv_mm, g * HPG * NTT - (NTT - min(4 * br + 4, NTT)))
                nc.gpsimd.tensor_copy(v_h, src).then_inc(vst_half, 1)
                pool.wait_ge(vst_half, g * 6 + (2 * br + 1))
                nc.gpsimd.tensor_tensor(pmark[:, 1:2], pmark[:, 1:2], pmark[:, 1:2], ALU.mult).then_inc(vst_half, 1)
                nc.gpsimd.tensor_tensor(v_l, src, v_h.bitcast(F32), ALU.subtract).then_inc(vst_ready, 1)

            def scale(h, hh, br):
                b = hh % 2
                pool.wait_ge(pool_set, h * 3 + (br + 1))
                pool.wait_ge(coef_ready, h * 3 + (br + 1))
                nc.gpsimd.tensor_tensor(pmark[:, 0:1], pmark[:, 0:1], pmark[:, 0:1], ALU.mult).then_inc(pool_set, 1)
                for ti in range(TT):
                    o, n = p_slice(br, ti)
                    k = br * TT + ti
                    nc.gpsimd.tensor_scalar(pr[:, b, o:o + n], pr[:, b, o:o + n], coef[:, b, k:k + 1],
                                            1.0, ALU.mult, ALU.mult).then_inc(p_scaled, 1)

            for hh in range(HPG):
                for br in range(3):
                    scale(hh, hh, br)
                    if (hh, br) == (0, WIN):
                        pool.wait_ge(cmp_ready, 1)
                        pool.wait_ge(vf_ready, TT)
                        for b in range(3):
                            stage_v(0, b)
            with pool.Fori(1, NG) as g:
                for hh in range(HPG):
                    for br in range(3):
                        scale(g * HPG + hh, hh, br)
                        if hh == 0:
                            stage_v(g, br)
            lows(C_NOUT, C_FFN[3] + ahead)
            sum_squares(5)
            lows(C_FFN[3] + ahead, NCHUNK)

        @block.scalar
        def _(act):
            def high(ch, first=False):
                c, slot, turn = ch
                act.wait_ge(raw_landed[slot], turn * 16 + 16)
                if not first:
                    act.wait_ge(chunk_mm, c - (SLOTS - 1))
                nc.scalar.activation(wh[:, slot, :], raw[:, slot, :], ACT.Copy).then_inc(chunk_hi, 1)

            def after(c0, n=1, i=None, step=0):
                for c in range(c0, c0 + n):
                    if c + SLOTS < NCHUNK:
                        high(chunk(c + SLOTS, i, step))

            def square(m, d):
                if d >= 2:
                    act.wait_ge(sq_sum, m * (KT - 1) + max(1, d - 2))
                nc.scalar.activation(sq[:, d % 2, :], x[:, d, :], ACT.Square).then_inc(sq_ready, 1)

            def root(m):
                act.wait_ge(ss_mm, m + 1)
                nc.scalar.activation(std[:, 0, :], ps[:, 6, :], ACT.Sqrt, bias=eps[:, 0:1],
                                     scale=1.0 / D).then_inc(std_ready, 1)

            def norm_later(m, tiles=range(KT)):
                for d in tiles:
                    act.wait_ge(x_ready, m * KT + d + 1)
                    nc.scalar.activation(xh[:, d, :], x[:, d, :], ACT.Copy, scale=gain[:, m, d:d + 1]).then_inc(xh_ready, 1)
                    square(m, d)

            def ffn(m, following=None):
                c0, u0 = C_FFN[m], m * FT
                root((0, 2, 3, 5)[m])
                with act.Fori(0, FT // 2) as i:
                    for k in range(2):
                        after(c0 + 2 * k, 2, i, 4)
                        act.wait_ge(a_scaled, i * 2 + (u0 + k + 1))
                        nc.scalar.activation(uf[:, k, :], uf[:, k, :], ACT.Silu).then_inc(silu_ready, 1)
                if following is None:
                    wide_last(c0 + UP, FT)
                else:
                    wide(c0 + UP, FT - 1)
                    norm_later(following)
                    after(c0 + UP + FT - 1)

            def wide(c0, n):
                with act.Fori(0, n // 4) as i:
                    for k in range(4):
                        after(c0 + k, 1, i, 4)
                for c in range(c0 + n // 4 * 4, c0 + n):
                    after(c)

            def wide_last(c0, n):
                m = (n - SLOTS) // 4
                with act.Fori(0, m) as i:
                    for k in range(4):
                        high(chunk(c0 + k + SLOTS, i, 4))
                for c in range(c0 + 4 * m, c0 + n - SLOTS):
                    high(chunk(c + SLOTS))

            act.wait_ge(consts_set, 3)
            nc.scalar.activation(amark[:, :], eps[:, :], ACT.Copy).then_inc(act_step, 1)
            act.wait_ge(act_step, 1)
            act.wait_ge(consts_in, 16 * 2)
            for c in range(SLOTS):
                high(chunk(c), first=True)
                norm_later(0, ([0], [1], [2, 3], [4, 5, 6, 7])[c])
            ffn(0, following=1)
            root(1)

            def ret_qk(c0, i=None, step=0):
                after(c0, 4, i, step)

            def ret_main(h, c0, i=None, step=0):
                after(c0, 4, i, step)
                after(c0 + 4, 4, i, step)
                for k in range(2):
                    act.wait_ge(sx_ready, h * 2 + (k + 1))
                    if k:
                        act.wait_ge(sg_ready, h * 2 + 1)
                    nc.scalar.activation(sg[:, :, :], sx[:, 2 * k:2 * k + 2, :],
                                         ACT.Sigmoid).then_inc(sig_ready, 1)
                act.wait_ge(pv_mm, h + 1)
                for v in range(4):
                    nc.scalar.activation(osq[v], ps[:, 4 + v, :], ACT.Square).then_inc(osq_ready, 1)

            def ret_std(h):
                act.wait_ge(oss_mm, h + 1)
                nc.scalar.activation(std[:, 0, :], ps[:, 4, :], ACT.Sqrt, bias=eps[:, 0:1],
                                     scale=1.0 / DV).then_inc(ostd_ready, 1)

            ret_qk(C_RET)
            with act.Fori(0, RH - 1) as h:
                ret_main(h, C_RET + 4, h, 16)
                after(C_RET + 12, 2, h, 16)
                ret_std(h)
                after(C_RET + 14, 6, h, 16)
            ret_main(RH - 1, C_RET + 52)
            ret_std(RH - 1)
            after(C_RET + 60)
            for k in range(1, 3):
                after(C_RET + 60 + k)
                norm_later(2, range(2 * k - 2, 2 * k))
            norm_later(2, range(KT // 2, KT))
            after(C_RET + 63)
            ffn(1, following=3)
            ffn(2, following=4)
            root(4)

            def head_sq(n, c):
                after(c, 2)
                act.wait_ge(pair_free, G_NSA + HN_FREE[n])
                if n >= 1:
                    act.wait_ge(hss_mm, n)
                nc.scalar.activation(sq[:, :, :], hpair[n], ACT.Square).then_inc(hsq_ready, 1)

            def head_std(n):
                act.wait_ge(hss_mm, n + 1)
                if n >= 1:
                    act.wait_ge(hn_ready, n)
                b = HSS_BANK[n]
                nc.scalar.activation(std[:, :, :], ps[:, b:b + 2, :], ACT.Sqrt, bias=eps[:, 0:1],
                                     scale=1.0 / DH).then_inc(hstd_ready, 1)

            def gelu(j, c):
                after(c, 4)
                act.wait_ge(chunk_mm, c + 4)
                nc.scalar.activation(gl[:, j, :, :], ps[:, 2:4, 0:GN], ACT.Gelu_apprx_tanh).then_inc(gelu_ready, 1)

            c0 = C_NSA
            after(c0, 4)
            head_sq(0, c0 + 4)
            gelu(0, c0 + 6)
            head_std(0)
            head_sq(1, c0 + 10)
            gelu(1, c0 + 12)
            head_std(1)
            head_sq(2, c0 + 16)
            head_sq(3, c0 + 18)
            head_std(2)
            head_sq(4, c0 + 20)
            head_std(3)
            head_sq(5, c0 + 22)
            head_std(4)
            act.wait_ge(gate_mm, 1)
            nc.scalar.activation(gt, ps[0:3 * NH, 0, :], ACT.Copy).then_inc(gt_ready, 1)
            head_std(5)
            act.wait_ge(w2_mm, 1)
            nc.scalar.activation(kct[:, 0, :], ps[0:DH, 1, 0:GN], ACT.Square).then_inc(kcsq_ready, 1)
            act.wait_ge(kcss_mm, 1)
            nc.scalar.activation(kct[:, 1, :], ps[0:DH, 1, 3 * P:3 * P + GN], ACT.Sqrt, bias=eps[0:DH, 0:1],
                                 scale=1.0 / DH).then_inc(kcstd_ready, 1)
            act.wait_ge(gate_turned, 1)
            act.wait_ge(rcol_ready, 1)
            for i in range(TT):
                g = ps[:, 0, i * 48:(i + 1) * 48].rearrange("p (b h) -> p b h", b=3)
                nc.scalar.activation(gates[:, :, :, i].rearrange("p h b -> p b h"), g, ACT.Sigmoid,
                                     scale=rcol[:, i:i + 1]).then_inc(sig_ready, 1)
            nc.scalar.activation(amark[:, :], eps[:, :], ACT.Exp).then_inc(act_step, 1)

            def exp(h, b, k):
                o, n = p_slice(k // TT, k % TT)
                act.wait_ge(sc_read, h * NS + k + 1)
                nc.scalar.activation(pr[:, b, o:o + n], pr[:, b, o:o + n], ACT.Exp, bias=mn[:, b, k:k + 1],
                                     scale=-1.0, accum_out=rsum[:, b, k:k + 1]).then_inc(exp_done, 1)

            def pt_high(h, hh, k):
                act.wait_ge(pt_mm, h * NTT + k + 1)
                if not (isinstance(h, int) and h == 0 and k < 3):
                    act.wait_ge(apv_mm, h * NTT + k - 2)
                np_, n = (NCP, T) if k == 8 else (P, T - P * (k % 4))
                nc.scalar.activation(pth[k % 3][0:np_, 0:n], ps[0:np_, 3 + k % 3, 0:n], ACT.Copy).then_inc(pt_hi, 1)

            def o_high(h, tile, hh):
                s = DH * (hh % 2)
                act.wait_ge(apv_mm, (h + 1) * NTT)
                nc.scalar.activation(xh[s:s + DH, tile, :], ps[0:DH, 6 + hh % 2, :], ACT.Copy).then_inc(o_half, 1)

            def step_of(h, hh, g, more=True):
                for k in range(NS):
                    if LAG <= k < LAG + NTT:
                        pt_high(h, hh, k - LAG)
                    if k == O_AT and not (isinstance(h, int) and h == 0):
                        o_high(h - 1, g * 2 + (hh - 1) // 2, (hh + 1) % 2)
                    if more:
                        exp(h + 1, (hh + 1) % 2, k)
                    elif k in (2, 4, 6, 8):
                        high(chunk(C_NOUT + k // 2 - 1))

            for k in range(NS):
                exp(0, 0, k)
            act.wait_ge(chunk_mm, C_NOUT)
            for t in range(TT):
                nc.scalar.activation(vf[:, t, :, :, :].rearrange("p b g d -> p (b g d)"), ps[:, 4 + t, :], ACT.Copy,
                                     scale=rcol[:, t:t + 1]).then_inc(vf_ready, 1)
            for hh in range(HPG):
                step_of(hh, hh, 0)
            with act.Fori(1, NG - 1) as g4:
                for hh in range(HPG):
                    step_of(g4 * HPG + hh, hh, g4)
            for hh in range(HPG):
                step_of(NH - HPG + hh, hh, NG - 1, more=hh < HPG - 1)
            o_high(NH - 1, NH // 2 - 1, HPG - 1)
            after(C_NOUT, 7)
            norm_later(5)
            after(C_NOUT + 7)
            ffn(3)
            for n in (0, 1, 2, 3, 5, 7):
                act.wait_ge(y_mm, n + 1)
                q, t = n // 4, n % 4
                nc.scalar.activation(xin[:, t, q * T:(q + 1) * T], ps[:, n, :], ACT.Copy).then_inc(y_rest, 1)

        @block.tensor
        def _(pe):
            mm = nc.tensor.matmul

            def tall(g, parity, chunks, moving, n=T, kpc=4, ready=None):
                last_k = kpc * len(chunks) - 1
                pe.wait_ge(pair_free, g - 1)
                for ci, (c, slot, turn) in enumerate(chunks):
                    pe.wait_ge(chunk_lo, c + 1)
                    for r in range(kpc):
                        k = ci * kpc + r
                        if ready is not None:
                            ready(k)
                        hi, lo = moving(k)
                        for ab in range(2):
                            col = r * 2 * P + ab * P
                            o = ps[:, 2 * parity + ab, 0:n]
                            w_h, w_l = wh[:, slot, col:col + P], wl[:, slot, col:col + P]
                            mm(o, w_h, hi, start=k == 0, stop=False)
                            mm(o, w_h, lo, start=False, stop=False)
                            last = mm(o, w_l, hi, start=False, stop=k == last_k)
                    last.then_inc(chunk_mm, 1)

            def from_x(k):
                return xh[:, k, :], xl[:, k, :]

            def natural(chunks, first=0):
                for ci, (c, slot, turn) in enumerate(chunks, first):
                    pe.wait_ge(chunk_lo, c + 1)
                    for r in range(2):
                        k = 2 * ci + r
                        w_h, w_l = wh[:, slot, r * T:(r + 1) * T], wl[:, slot, r * T:(r + 1) * T]
                        for t in range(TT):
                            o = ps[:, 4 + t, :]
                            x_h, x_l = xh[:, k, t * P:(t + 1) * P], xl[:, k, t * P:(t + 1) * P]
                            mm(o, x_h, w_h, start=k == 0, stop=False)
                            mm(o, x_h, w_l, start=False, stop=False)
                            last = mm(o, x_l, w_h, start=False, stop=k == KT - 1)
                    last.then_inc(chunk_mm, 1)

            def wide_chunk(ch, f_h, f_l, order, start, stop):
                c, slot, turn = ch
                pe.wait_ge(chunk_lo, c + 1)
                for d in order:
                    w_h, w_l = wh[:, slot, d * P:(d + 1) * P], wl[:, slot, d * P:(d + 1) * P]
                    mm(ps[:, d, :], w_h, f_h, start=start, stop=False)
                    mm(ps[:, d, :], w_h, f_l, start=False, stop=False)
                    last = mm(ps[:, d, :], w_l, f_h, start=False, stop=stop)
                    if stop and d < KT - 1:
                        last.then_inc(down_mm, 1)
                last.then_inc(chunk_mm, 1)

            def norm(m):
                pe.wait_ge(sq_sum, (m + 1) * (KT - 1))
                mm(ps[:, 6, :], ones[:, :], std[:, 1, :], start=True, stop=True).then_inc(ss_mm, 1)

            def ffn(m):
                c0, g0, u0 = C_FFN[m], G_FFN[m], m * FT
                nm = (0, 2, 3, 5)[m]
                tall(g0, 0, [chunk(c0), chunk(c0 + 1)], from_x, ready=lambda kt: pe.wait_ge(xn_ready, nm * KT + kt + 1))
                norm(nm)
                tall(g0 + 1, 1, [chunk(c0 + 2), chunk(c0 + 3)], from_x)
                with pe.Fori(1, FT // 2) as i:
                    for k in range(2):
                        tall(i * 2 + (g0 + k), k, [chunk(c0 + 2 * k, i, 4), chunk(c0 + 2 * k + 1, i, 4)], from_x)
                cd = c0 + UP
                pe.wait_ge(u_ready, u0 + 1)
                first = list(range(4, 8)) + list(range(4))
                c, slot, turn = chunk(cd)
                pe.wait_ge(chunk_lo, c + 1)
                for d in first:
                    if d == 0:
                        pe.wait_ge(pair_free, g0 + FT)
                    w_h, w_l = wh[:, slot, d * P:(d + 1) * P], wl[:, slot, d * P:(d + 1) * P]
                    mm(ps[:, d, :], w_h, uh[:, 0, :], start=True, stop=False)
                    mm(ps[:, d, :], w_h, ul[:, 0, :], start=False, stop=False)
                    last = mm(ps[:, d, :], w_l, uh[:, 0, :], start=False, stop=False)
                last.then_inc(chunk_mm, 1)
                n = (FT - 2) // 4
                with pe.Fori(0, n) as i:
                    for k in range(4):
                        f = i * 4 + (1 + k)
                        pe.wait_ge(u_ready, f + (u0 + 1))
                        wide_chunk(chunk(cd + 1 + k, i, 4), uh[:, f, :], ul[:, f, :], range(KT), False, False)
                for f in range(1 + 4 * n, FT):
                    pe.wait_ge(u_ready, u0 + f + 1)
                    wide_chunk(chunk(cd + f), uh[:, f, :], ul[:, f, :], range(KT), False, f == FT - 1)

            pe.wait_ge(rel_in, 32)
            pe.wait_ge(consts_set, 3)
            for k in range(2):
                last = mm(ps[0:NH, 6 + k, 0:REL // 2], relw[:, :], onehot[:, k * (REL // 2):(k + 1) * (REL // 2)],
                          start=True, stop=True)
            last.then_inc(rel_mm, 1)
            pe.wait_ge(csq_in, 16)
            for t in range(TT):
                pe.wait_ge(x_in_landed[t], 16)
                for d in range(KT):
                    if t == 0 and d == 6:
                        pe.wait_ge(rel_out, 1)
                    last = nc.tensor.transpose(ps[:, d, t * P:(t + 1) * P], xin[:, t, d * P:(d + 1) * P], ident)
                    if t == TT - 1:
                        last.then_inc(x_turned, 1)
            ffn(0)

            def ret_qk_q(g, c0, i=None, step=0, ready=None):
                tall(g, 0, [chunk(c0, i, step), chunk(c0 + 1, i, step)], from_x, ready=ready)

            def ret_qk_k(g, c0, i=None, step=0):
                tall(g, 1, [chunk(c0, i, step), chunk(c0 + 1, i, step)], from_x)

            def ret_main(h, g0, c0, i=None, step=0):
                natural([chunk(c0 + k, i, step) for k in range(4)])
                pe.wait_ge(qk_ready, h * 2 + 2)
                pe.wait_ge(pair_free, g0)
                for j in range(TT):
                    n = T - j * P
                    for half in range(2):
                        k_h, k_l = qkh[:, 1, half, j * P:(j + 1) * P], qkl[:, 1, half, j * P:(j + 1) * P]
                        q_h, q_l = qkh[:, 0, half, j * P:], qkl[:, 0, half, j * P:]
                        mm(ps[:, j, 0:n], k_h, q_h, start=half == 0, stop=False)
                        mm(ps[:, j, 0:n], k_h, q_l, start=False, stop=False)
                        last = mm(ps[:, j, 0:n], k_l, q_h, start=False, stop=half == 1)
                    last.then_inc(s_mm, 1)
                for k in range(2):
                    pe.wait_ge(s_read, h * TT + (2 * k + 2))
                    tall(g0 + k, k, [chunk(c0 + 4 + 2 * k, i, step), chunk(c0 + 5 + 2 * k, i, step)], from_x)
                pe.wait_ge(v_ready, h + 1)
                pe.wait_ge(a_ready, h * TT + TT)
                for j in range(TT):
                    o0 = (0, 512, 896, 1152)[j]
                    n = T - j * P
                    for v in range(4):
                        v_h, v_l = vh[:, j, v * P:(v + 1) * P], vl[:, j, v * P:(v + 1) * P]
                        o = ps[:, 4 + v, j * P:]
                        mm(o, v_h, ah[:, o0:o0 + n], start=j == 0, stop=False)
                        mm(o, v_h, al[:, o0:o0 + n], start=False, stop=False)
                        last = mm(o, v_l, ah[:, o0:o0 + n], start=False, stop=j == TT - 1)
                last.then_inc(pv_mm, 1)

            def ret_ss(h):
                pe.wait_ge(on_ready, h * 4 + 4)
                pe.wait_ge(osq_sum, h * 3 + 3)
                mm(ps[:, 4, :], ones[:, :], osq[0], start=True, stop=True).then_inc(oss_mm, 1)

            def ret_out(h, g0, c0, i=None, step=0, ks=range(4), ready=None):
                for k in ks:
                    tall(g0 + k, k % 2, [chunk(c0 + k, i, step)], lambda v: (onh[:, v, :], onl[:, v, :]), ready=ready)

            ret_qk_q(G_RET, C_RET, ready=lambda kt: pe.wait_ge(xn_ready, KT + kt + 1))
            norm(1)
            ret_qk_k(G_RET + 1, C_RET + 2)
            pe.wait_ge(std_ready, 2)
            with pe.Fori(0, RH - 1) as h:
                g = h * 8 + (G_RET + 2)
                ret_main(h, g, C_RET + 4, h, 16)
                ret_qk_q(g + 2, C_RET + 12, h, 16)
                ret_ss(h)
                ret_qk_k(g + 3, C_RET + 14, h, 16)
                ret_out(h, g + 4, C_RET + 16, h, 16)
                pe.wait_ge(ostd_ready, h + 1)
            g = G_RET + 2 + 8 * (RH - 1)
            ret_main(RH - 1, g, C_RET + 52)
            ret_out(RH - 1, g + 2, C_RET + 60, ks=[0], ready=lambda v: pe.wait_ge(on_ready, (RH - 1) * 4 + v + 1))
            ret_ss(RH - 1)
            ret_out(RH - 1, g + 2, C_RET + 60, ks=[1, 2, 3])
            ffn(1)
            ffn(2)

            def pair(n, c, ready=None):
                tall(G_NSA + n, n % 2, [chunk(C_NSA + c), chunk(C_NSA + c + 1)], from_x, ready=ready)

            def head_ss(n):
                pe.wait_ge(hsq_ready, n + 1)
                if n >= 2:
                    pe.wait_ge(hstd_ready, n - 1)
                b = HSS_BANK[n]
                for ab in range(2):
                    last = mm(ps[:, b + ab, :], bones, sq[:, ab, :], start=True, stop=True)
                last.then_inc(hss_mm, 1)

            def compress(j, n, c):
                pe.wait_ge(uc_ready, j + 1)
                tall(G_NSA + n, n % 2, [chunk(C_NSA + c + k) for k in range(4)],
                     lambda l2: (uch[:, l2 * GN:(l2 + 1) * GN], ucl[:, l2 * GN:(l2 + 1) * GN]), n=GN)

            pair(0, 0, ready=lambda kt: pe.wait_ge(xn_ready, 4 * KT + kt + 1))
            norm(4)
            pair(1, 2)
            pe.wait_ge(r_ready, 1)
            for t in range(TT):
                last = nc.tensor.transpose(ps[:, 7, t * P:(t + 1) * P], nrn[:, t * P:(t + 1) * P], ident)
            last.then_inc(r_turned, 1)
            pair(2, 4)
            compress(0, 3, 6)
            head_ss(0)
            pair(4, 10)
            compress(1, 5, 12)
            pe.wait_ge(rcol_ready, 1)
            head_ss(1)
            pair(6, 16)
            pair(7, 18)
            head_ss(2)
            pair(8, 20)
            head_ss(3)
            pair(9, 22)
            head_ss(4)
            pe.wait_ge(gw_ready, 1)
            pe.wait_ge(pair_free, G_NSA + 9)
            for k in range(KT):
                o = ps[0:3 * NH, 0, :]
                mm(o, gwh[:, k, :], xh[:, k, :], start=k == 0, stop=False)
                mm(o, gwh[:, k, :], xl[:, k, :], start=False, stop=False)
                last = mm(o, gwl[:, k, :], xh[:, k, :], start=False, stop=k == KT - 1)
            last.then_inc(gate_mm, 1)
            pe.wait_ge(gelu_ready, 2)
            for g in range(NG):
                for t in range(2):
                    mm(ps[0:NC, 1, P + g * DH:P + (g + 1) * DH], gl[:, 1, t, g * NC:(g + 1) * NC], w2[:, 1, t, :],
                       start=t == 0, stop=t == 1)
            for t in range(2):
                last = mm(ps[0:DH, 1, 0:GN], w2[:, 0, t, :], gl[:, 0, t, :], start=t == 0, stop=t == 1)
            last.then_inc(w2_mm, 1)
            head_ss(5)
            pe.wait_ge(gt_ready, 1)
            for t in range(TT):
                last = nc.tensor.transpose(ps[:, 0, t * 48:(t + 1) * 48], gt[:, t * P:(t + 1) * P],
                                           ident[0:3 * NH, 0:3 * NH])
            last.then_inc(gate_turned, 1)
            pe.wait_ge(hstd_ready, 5)
            pe.wait_ge(kcsq_ready, 1)
            pe.wait_ge(pair_free, G_NSA + 10)
            mm(ps[0:DH, 1, 3 * P:3 * P + GN], ones[0:DH, 0:DH], kct[:, 0, :], start=True, stop=True).then_inc(kcss_mm, 1)
            natural([chunk(C_NSA + 24 + k) for k in range(3)])

            def score(h, g, b, k):
                br, ti = k // TT, k % TT
                if not (isinstance(h, int) and h == 0 and k < 3):
                    pe.wait_ge(sc_read, h * NS + (k - 2))
                q = qs[:, b, ti * P:(ti + 1) * P]
                n = p_slice(br, ti)[1]
                if br == CMPB:
                    n += 1
                    m_h, m_l = kch[:, g, 0:n], kcl[:, g, 0:n]
                else:
                    m_h, m_l = kh[:, br, g, 0:n], kl[:, br, g, 0:n]
                o = ps[:, k % 3, 0:n]
                mm(o, q, m_h, start=True, stop=False)
                mm(o, q, m_l, start=False, stop=True).then_inc(sc_mm, 1)

            def turn(h, hh, k):
                b = hh % 2
                if not (isinstance(h, int) and h == 0 and k < 3):
                    pe.wait_ge(pt_ready, h * NTT + (k - 2))
                for ti in range(0 if k == 8 else k % 4, TT):
                    po = p_slice(CMPB if k == 8 else k // 4, ti)[0]
                    if k == 8:
                        last = nc.tensor.transpose(ps[0:NCP, 3 + k % 3, ti * P:(ti + 1) * P],
                                                   pr[:, b, po:po + NCP], ident)
                    else:
                        j = k % 4
                        last = nc.tensor.transpose(ps[:, 3 + k % 3, (ti - j) * P:(ti - j + 1) * P],
                                                   pr[:, b, po + j * P:po + (j + 1) * P], ident)
                last.then_inc(pt_mm, 1)

            def values(h, hh, k, g):
                o, t_h, t_l = ps[0:DH, 6 + hh % 2, :], pth[k % 3], ptl[k % 3]
                pe.wait_ge(pt_ready, h * NTT + k + 1)
                if hh == 0 and k % 4 == 0:
                    pe.wait_ge(vst_ready, g * 3 + (k // 4 + 1))
                if k == 8:
                    np_, c, v = NCP, 0, vcst
                else:
                    np_, c, v = P, (k % 4) * P, vst[:, k % 4, k // 4, :]
                p_h, p_l = t_h[0:np_, 0:T - c], t_l[0:np_, 0:T - c]
                mm(o[:, c:], v[:, 0:DH], p_h, start=k == 0, stop=False)
                mm(o[:, c:], v[:, 0:DH], p_l, start=False, stop=False)
                last = mm(o[:, c:], v[:, DH:2 * DH], p_h, start=False, stop=k == 8)
                last.then_inc(apv_mm, 1)

            def step_of(h, hh, g, more=True):
                if more:
                    pe.wait_ge(qs_ready, h + 2)
                for k in range(NS):
                    if more:
                        score(h + 1, g + (hh + 1) // HPG, (hh + 1) % 2, k)
                    t = k - LAG
                    if 0 <= t < NTT:
                        if t % 4 == 0:
                            pe.wait_ge(p_scaled, h * NS + (t + 4))
                        turn(h, hh, t)
                    if t == 0 and not (isinstance(h, int) and h == 0):
                        for v in range(V_LEFT, NTT):
                            values(h - 1, (hh + 3) % HPG, v, g)
                    if t == V_LAG and not (isinstance(h, int) and h < 2):
                        pe.wait_ge(o_ready, h - 1)
                    if 0 <= t - V_LAG < NTT:
                        values(h, hh, t - V_LAG, g)

            pe.wait_ge(cmp_ready, 3)
            pe.wait_ge(qs_ready, 1)
            for k in range(NS):
                score(0, 0, 0, k)
            natural([chunk(C_NSA + 27)], first=3)
            pe.wait_ge(vf_ready, TT)
            for hh in range(HPG):
                step_of(hh, hh, 0)
            with pe.Fori(1, NG - 1) as g4:
                for hh in range(HPG):
                    step_of(g4 * HPG + hh, hh, g4)
            for hh in range(HPG):
                step_of(NH - HPG + hh, hh, NG - 1, more=hh < HPG - 1)
            for v in range(V_LEFT, NTT):
                values(NH - 1, HPG - 1, v, NG - 1)
            pe.wait_ge(sc_read, NH * NS)
            for f in range(8):
                pe.wait_ge(o_ready, NH if f == 0 else 2 * f + 2)
                wide_chunk(chunk(C_NOUT + f), xh[:, f, :], xl[:, f, :], range(KT), f == 0, f == 7)
            ffn(3)
            def turn_back(t, ds):
                for d in ds:
                    last = nc.tensor.transpose(ps[:, 4 * (d // 4) + t, d % 4 * P:(d % 4 + 1) * P],
                                               x[:, d, t * P:(t + 1) * P], ident)
                return last

            pe.wait_ge(x_ready, 7 * KT - 4)
            for t in range(TT):
                turn_back(t, range(4)).then_inc(y_mm, 1)
            pe.wait_ge(x_ready, 7 * KT - 1)
            for t in range(3):
                turn_back(t, range(4, 7))
            pe.wait_ge(x_ready, 7 * KT)
            for t in range(3):
                turn_back(t, [7]).then_inc(y_mm, 1)
            turn_back(3, range(4, 8)).then_inc(y_mm, 1)

        @block.vector
        def _(dve):
            V = nc.vector

            class Steps:
                n, i, per, start = 0, None, 0, 0

                def __call__(self, ins):
                    self.add(ins)
                    self.wait()

                def add(self, ins):
                    ins.then_inc(dve_step, 1)
                    self.n += 1

                def wait(self, but=0):
                    n = self.n - but
                    dve.wait_ge(dve_step, n if self.i is None else self.i * self.per + n)

                def loop(self, i, per, first=0):
                    self.i, self.per, self.start = i, per, self.n
                    self.n -= first * per

                def end(self, count, first=0):
                    assert self.n + first * self.per - self.start == self.per, (self.n + first * self.per - self.start, self.per)
                    self.i, self.n = None, self.start + self.per * count

            step = Steps()

            def split(hi, lo, src):
                step(V.tensor_copy(hi, src))
                return V.tensor_tensor(lo, src, hi.bitcast(F32), ALU.subtract)

            def invert(m):
                dve.wait_ge(std_ready, m + 1)
                step(V.reciprocal(std[:, 0, :], std[:, 0, :]))

            def gained_low(m, d):
                dve.wait_ge(xh_ready, m * KT + d + 1)
                V.scalar_tensor_tensor(xl[:, d, :], x[:, d, :], gain[:, m, d:d + 1], xh[:, d, :].bitcast(F32),
                                       ALU.mult, ALU.subtract).then_inc(xn_ready, 1)

            def residual(n, c_last, scale, m=None):
                for d in range(KT):
                    if d < KT - 1:
                        dve.wait_ge(down_mm, n * (KT - 1) + d + 1)
                    else:
                        dve.wait_ge(chunk_mm, c_last + 1)
                    V.scalar_tensor_tensor(x[:, d, :], ps[:, d, :], scale, x[:, d, :], ALU.mult,
                                           ALU.add).then_inc(x_ready, 1)
                    if m is not None and d:
                        gained_low(m, d - 1)
                if m is not None:
                    gained_low(m, KT - 1)

            def ffn(m, after=None):
                c0, u0 = C_FFN[m], m * FT
                invert((0, 2, 3, 5)[m])
                with dve.Fori(0, FT // 2) as i:
                    step.loop(i, 4)
                    for k in range(2):
                        f = i * 2 + k
                        dve.wait_ge(chunk_mm, i * 4 + (c0 + 2 * k + 2))
                        V.tensor_tensor(uf[:, k, :], ps[:, 2 * k, :], std[:, 0, :], ALU.mult).then_inc(a_scaled, 1)
                        V.tensor_tensor(bf[:, k, :], ps[:, 2 * k + 1, :], std[:, 0, :], ALU.mult).then_inc(pair_free, 1)
                        dve.wait_ge(pair_free, f + (G_FFN[m] + 1))
                        dve.wait_ge(silu_ready, f + (u0 + 1))
                        step(V.tensor_tensor(bf[:, k, :], uf[:, k, :], bf[:, k, :], ALU.mult))
                        split(uh[:, f, :], ul[:, f, :], bf[:, k, :]).then_inc(u_ready, 1)
                        dve.wait_ge(u_ready, f + (u0 + 1))
                    step.end(FT // 2)
                residual((0, 1, 2, 4)[m], C_FFN[m] + UP + DOWN - 1, 0.5, after)

            V.memset(ones[:, :], 1.0).then_inc(consts_set, 1)
            V.memset(eps[:, :], EPS).then_inc(consts_set, 1)
            V.memset(relw[BUCKETS:BUCKETS + 1, :], BIG).then_inc(consts_set, 1)
            dve.wait_ge(rel_mm, 1)
            for k in range(2):
                step(V.tensor_copy(relo[:, k * (REL // 2):(k + 1) * (REL // 2)], ps[0:NH, 6 + k, 0:REL // 2]))
            V.memset(mark[:, 0:1], 0.0).then_inc(rel_out, 1)
            dve.wait_ge(consts_in, 16 * 2)
            for d in range(KT):
                dve.wait_ge(x_turned, d + 1)
                V.tensor_copy(x[:, d, :], ps[:, d, :]).then_inc(x_ready, 1)
                dve.wait_ge(x_ready, d + 1)
                if d in (1, 3):
                    V.memset(mark[:, 0:1], 0.0).then_inc(pair_free, 1)
                if d:
                    gained_low(0, d - 1)
            gained_low(0, KT - 1)
            step(V.tensor_scalar(qkg[:, 0:1], qkg[:, 0:1], -(DH ** -0.5), None, ALU.mult))
            dve.wait_ge(rel_stored, 16)
            ffn(0, after=1)

            def twice(r):
                return bass.AP(r.tensor, r.offset, [list(r.ap[0]), [0, 2], [1, T]])

            def rotate(h, c_end, which):
                b = 2 * which
                rot = (rotq, rotk)[which]
                dve.wait_ge(chunk_mm, c_end)
                V.tensor_tensor(rt[:, 0, :], ps[:, b, :], rot[:, 0, :], ALU.mult)
                V.tensor_tensor(rt[:, 1, :], ps[:, b + 1, :], rot[:, 1, :], ALU.mult)
                V.tensor_tensor(rt[:, 2, :], ps[:, b, :], rot[:, 1, :], ALU.mult)
                step(V.tensor_tensor(rt[:, 3, :], ps[:, b + 1, :], rot[:, 0, :], ALU.mult))
                V.tensor_tensor(qf[:, 0, :], rt[:, 0, :], rt[:, 1, :], ALU.subtract).then_inc(pair_free, 1)
                step(V.tensor_tensor(qf[:, 1, :], rt[:, 2, :], rt[:, 3, :], ALU.add))
                split(qkh[:, which, :, :], qkl[:, which, :, :], qf).then_inc(qk_ready, 1)

            def ret_values(t):
                step(V.tensor_copy(vh[:, t, :], ps[:, 4 + t, :]))
                return V.tensor_tensor(vl[:, t, :], ps[:, 4 + t, :], vh[:, t, :].bitcast(F32), ALU.subtract)

            def ret_main(h, c0, g0, i=None, n=0):
                dve.wait_ge(chunk_mm, chunk(c0, i, 16)[0] + 4)
                ret_values(0)
                for j in range(TT):
                    o0, w = (0, 512, 896, 1152)[j], T - j * P
                    dve.wait_ge(s_mm, h * TT + (j + 1))
                    V.tensor_tensor(af[:, o0:o0 + w], ps[:, j, 0:w], dec[:, h, 0:w], ALU.mult).then_inc(s_read, 1)
                for t in range(1, TT):
                    last = ret_values(t)
                last.then_inc(v_ready, 1)
                for j in range(TT):
                    o0, w = (0, 512, 896, 1152)[j], T - j * P
                    dve.wait_ge(s_read, h * TT + (j + 1))
                    split(ah[:, o0:o0 + w], al[:, o0:o0 + w], af[:, o0:o0 + w]).then_inc(a_ready, 1)
                for k in range(2):
                    b = 2 * k
                    dve.wait_ge(chunk_mm, chunk(c0, i, 16)[0] + (6 + b))
                    V.tensor_tensor(sx[:, b:b + 2, :], ps[:, b:b + 2, :], twice(rn), ALU.mult).then_inc(pair_free, 1)
                    dve.wait_ge(pair_free, g0 + (k + 1))
                    V.memset(mark[:, 0:1], 0.0).then_inc(sx_ready, 1)
                    dve.wait_ge(sig_ready, h * 2 + (k + 1))
                    V.tensor_tensor(sx[:, b:b + 2, :], sx[:, b:b + 2, :], sg[:, :, :], ALU.mult).then_inc(sg_ready, 1)

            def ret_outputs(h):
                dve.wait_ge(sg_ready, h * 2 + 2)
                for v in range(4 + 2):
                    if v < 4:
                        dve.wait_ge(osq_ready, h * 4 + (v + 1))
                        step.add(V.tensor_tensor(onf[:, v, :], ps[:, 4 + v, :], sx[:, v, :], ALU.mult))
                    if 0 <= v - 1 < 4:
                        step.wait(1 if v < 4 else 0)
                        step.add(V.tensor_copy(onh[:, v - 1, :], onf[:, v - 1, :]))
                    if v - 2 >= 0:
                        step.wait((2, 2, 1, 0)[v - 2])
                        V.tensor_tensor(onl[:, v - 2, :], onf[:, v - 2, :], onh[:, v - 2, :].bitcast(F32),
                                        ALU.subtract).then_inc(on_ready, 1)
                dve.wait_ge(on_ready, h * 4 + 4)

            def ret_invert(h):
                dve.wait_ge(ostd_ready, h + 1)
                step(V.reciprocal(std[:, 0, :], std[:, 0, :]))

            def ret_residual(c0, i=None, last=False):
                for k in range(4):
                    b = 2 * (k % 2)
                    dve.wait_ge(chunk_mm, chunk(c0 + k, i, 16)[0] + 1)
                    step(V.tensor_tensor(rt[:, b:b + 2, :], ps[:, b:b + 2, :], twice(std[:, 0, :]), ALU.mult))
                    ins = V.tensor_tensor(x[:, 2 * k:2 * k + 2, :], x[:, 2 * k:2 * k + 2, :], rt[:, b:b + 2, :], ALU.add)
                    if not last:
                        ins.then_inc(pair_free, 1)
                    else:
                        ins.then_inc(x_ready, 2)
                        V.memset(mark[:, 0:1], 0.0).then_inc(pair_free, 1)
                        dve.wait_ge(x_ready, 2 * KT + 2 * k + 2)
                        if k:
                            gained_low(2, 2 * k - 2)
                            gained_low(2, 2 * k - 1)
                if last:
                    gained_low(2, KT - 2)
                    gained_low(2, KT - 1)

            dve.wait_ge(ret_in, 32)
            dve.wait_ge(std_ready, 2)
            step(V.reciprocal(rn, std[:, 0, :]))
            step(V.tensor_tensor(rotq[:, :, :], rotq[:, :, :], twice(rn), ALU.mult))
            step(V.tensor_tensor(rotk[:, :, :], rotq[:, :, :], twice(rn), ALU.mult))
            rotate(0, C_RET + 2, 0)
            rotate(0, C_RET + 4, 1)
            with dve.Fori(0, RH - 1) as h:
                step.loop(h, 4 + 4 + 8 + 3 + 1 + 3 + 4)
                g = h * 8 + (G_RET + 2)
                ret_main(h, C_RET + 4, g, h)
                ret_outputs(h)
                rotate(h + 1, h * 16 + (C_RET + 14), 0)
                ret_invert(h)
                rotate(h + 1, h * 16 + (C_RET + 16), 1)
                ret_residual(C_RET + 16, h)
                step.end(RH - 1)
            ret_main(RH - 1, C_RET + 52, G_RET + 2 + 8 * (RH - 1))
            ret_outputs(RH - 1)
            ret_invert(RH - 1)
            ret_residual(C_RET + 60, last=True)
            ffn(1, after=3)
            ffn(2, after=4)

            def inputs(j):
                dve.wait_ge(chunk_mm, C_NSA + 2 * j + 2)
                for g in range(NG):
                    for par in range(2):
                        s = DH * (g % 2)

                        def half(a):
                            return a[s:s + DH, :].rearrange("d (t two) -> d t two", two=2)[:, :, par]

                        ins = V.tensor_tensor(z[DH * par:DH * (par + 1), j, g, :], half(ps[:, 2 * j + g // 2, :]),
                                              half(nrn), ALU.mult)
                        if (g, par) != (NG - 1, 1):
                            step.add(ins)
                ins.then_inc(pair_free, 1)
                dve.wait_ge(pair_free, G_NSA + j + 1)

            def blocks(j):
                zz = z[:, j, :, :]
                src = bass.AP(zz.tensor, zz.offset, [list(zz.ap[0]), [1, LP], [T // 2, NG], [CMP_STRIDE // 2, NC]])
                pp = pos[:, j, :]
                add = bass.AP(pp.tensor, pp.offset, [list(pp.ap[0]), [1, LP], [0, NG], [0, NC]])
                dst = u[:, 0:LP * GN].rearrange("p (l g n) -> p l g n", l=LP, g=NG)
                step(V.tensor_tensor(dst, src, add, ALU.add))
                split(uch[:, :], ucl[:, :], u[:, 0:LP * GN]).then_inc(uc_ready, 1)

            def hidden_out(j):
                dve.wait_ge(gelu_ready, j + 1)
                V.memset(mark[:, 0:1], 0.0).then_inc(pair_free, 1)
                dve.wait_ge(pair_free, G_NSA + (4, 6)[j])

            def head_copy(n):
                b = (0, 0, 0, 2, 0, 2)[n]
                dve.wait_ge(chunk_mm, C_NSA + (6, 12, 18, 20, 22, 24)[n])
                V.tensor_tensor(hpair[n], ps[:, b:b + 2, :], twice(nrn), ALU.mult).then_inc(pair_free, 1)

            def head_norm(n):
                dve.wait_ge(hstd_ready, n + 1)
                step(V.reciprocal(std[:, :, :], std[:, :, :]))
                col = 0 if n >= 2 else 2 + n
                V.scalar_tensor_tensor(hpair[n], hpair[n], qkg[:, col:col + 1], std[:, :, :], ALU.mult,
                                       ALU.mult).then_inc(hn_ready, 1)
                dve.wait_ge(hn_ready, n + 1)

            def keys(n):
                src = [hpair[n][DH * (g % 2):DH * (g % 2) + DH, g // 2, :] for g in range(NG)]
                for g in range(NG):
                    for half in (0, DH):
                        step.add(V.tensor_copy(kh[half:half + DH, n, g, :], src[g]))
                step.wait()
                for g in range(NG):
                    s = DH * (g % 2)
                    for half in (0, DH):
                        step.add(V.tensor_tensor(kl[half:half + DH, n, g, :], src[g],
                                                 kh[s:s + DH, n, g, :].bitcast(F32), ALU.subtract))
                step.wait()

            dve.wait_ge(ret_in, 80)
            step(V.tensor_copy(gwh[:, :, :], gwf[:, :, :]))
            V.tensor_tensor(gwl[:, :, :], gwf[:, :, :], gwh[:, :, :].bitcast(F32), ALU.subtract).then_inc(gw_ready, 1)
            dve.wait_ge(std_ready, 5)
            V.reciprocal(nrn, std[:, 0, :]).then_inc(r_ready, 1)
            dve.wait_ge(r_ready, 1)
            inputs(0)
            blocks(0)
            inputs(1)
            head_copy(0)
            dve.wait_ge(r_turned, 1)
            V.tensor_copy(rcol[:, :], ps[:, 7, :].rearrange("p (i q) -> p i q", i=TT)[:, :, 0]).then_inc(rcol_ready, 1)
            hidden_out(0)
            blocks(1)
            head_norm(0)
            head_copy(1)
            hidden_out(1)
            keys(0)
            head_norm(1)
            head_copy(2)
            head_copy(3)
            keys(1)
            head_norm(2)
            head_copy(4)
            head_norm(3)
            head_copy(5)
            head_norm(4)
            head_norm(5)
            dve.wait_ge(sig_ready, 2 * RH + 4)
            gm = gates[:, :, CMPB, 0]
            V.tensor_scalar(gm, gm, rowmask, None, ALU.mult).then_inc(gates_set, 1)
            dve.wait_ge(hn_ready, 6)
            step(V.tensor_copy(qs[0:DH, 0, :], qn[0:DH, 0, :]))
            V.tensor_tensor(qs[DH:P, 0, :], qn[0:DH, 0, :], qs[0:DH, 0, :].bitcast(F32), ALU.subtract).then_inc(qs_ready, 1)
            step(V.tensor_copy(qs[DH:P, 1, :], qn[DH:P, 0, :]))
            V.tensor_tensor(qs[0:DH, 1, :], qn[DH:P, 0, :], qs[DH:P, 1, :].bitcast(F32), ALU.subtract).then_inc(qs_ready, 1)
            dve.wait_ge(w2_mm, 1)
            dve.wait_ge(kcstd_ready, 1)
            step(V.memset(vcf[:, :, :], 0.0))
            step(V.tensor_copy(vcf[0:NC, :, :], ps[0:NC, 1, P:P + NG * DH].rearrange("n (g d) -> n g d", g=NG)))
            step(V.memset(u[:, 3 * P * 4:3 * P * 4 + NG * NCP], 0.0))
            zero = u[:, 3 * P * 4:3 * P * 4 + NG * NCP].rearrange("p (g n) -> p g n", g=NG)
            step(V.tensor_copy(kch[:, :, :], zero))
            step(V.tensor_copy(kcl[:, :, :], zero))
            step(V.reciprocal(kct[:, 1, :], kct[:, 1, :]))
            step(V.scalar_tensor_tensor(kcf, ps[0:DH, 1, 0:GN], qkg[0:DH, 1:2], kct[:, 1, :], ALU.mult, ALU.mult))
            ksrc = kcf.rearrange("p (g n) -> p g n", g=NG)
            for half in (0, DH):
                step(V.tensor_copy(kch[half:half + DH, :, 0:NC], ksrc))
            for half in (0, DH):
                step(V.tensor_tensor(kcl[half:half + DH, :, 0:NC], ksrc, kch[0:DH, :, 0:NC].bitcast(F32), ALU.subtract))
            V.memset(mark[:, 0:1], 0.0).then_inc(cmp_ready, 1)
            for b in range(2):
                V.memset(pr[:, b, 2 * PB:PW], 0.0).then_inc(cmp_ready, 1)

            def stage_q(h, tile, hh, b, half):
                s = DH * (hh % 2)
                src = qn[s:s + DH, tile, :]
                if half == 0:
                    step.add(V.tensor_copy(qs[s:s + DH, b, :], src))
                else:
                    step.wait()
                    V.tensor_tensor(qs[DH - s:P - s, b, :], src, qs[s:s + DH, b, :].bitcast(F32),
                                    ALU.subtract).then_inc(qs_ready, 1)

            def read_score(h, b, k):
                br, ti = k // TT, k % TT
                o, n = p_slice(br, ti)
                c, st = (ti * P + P - CMP_LEN, CMP_STRIDE) if br == CMPB else (ti * P + P - 1, 1)
                t = tn[:, b, c:c + 1]
                bias = bass.AP(t.tensor, t.offset, [list(t.ap[0]), [-st, n]])
                dve.wait_ge(sc_mm, h * NS + k + 1)
                V.memset(mark[:, k + 1:k + 2], 0.0)
                V.tensor_tensor_reduce(out=pr[:, b, o:o + n], in0=ps[:, k % 3, 0:n], in1=bias, scale=1.0,
                                       scalar=3e38, op0=ALU.add, op1=ALU.min,
                                       accum_out=mn[:, b, k:k + 1]).then_inc(sc_read, 1)

            def coefficients(h, b, br, half):
                k = br * TT
                if half == 0:
                    dve.wait_ge(exp_done, h * NS + (k + TT))
                    step.add(V.reciprocal(coef[:, b, k:k + TT], rsum[:, b, k:k + TT]))
                else:
                    step.wait()
                    V.tensor_tensor(coef[:, b, k:k + TT], coef[:, b, k:k + TT], gates[:, h, br, :],
                                    ALU.mult).then_inc(coef_ready, 1)

            def pt_low(h, hh, k):
                dve.wait_ge(pt_hi, h * NTT + k + 1)
                np_, n = (NCP, T) if k == 8 else (P, T - P * (k % 4))
                V.tensor_tensor(ptl[k % 3][0:np_, 0:n], ps[0:np_, 3 + k % 3, 0:n],
                                pth[k % 3][0:np_, 0:n].bitcast(F32), ALU.subtract).then_inc(pt_ready, 1)

            def o_low(h, tile, hh):
                s = DH * (hh % 2)
                dve.wait_ge(o_half, h + 1)
                V.tensor_tensor(xl[s:s + DH, tile, :], ps[0:DH, 6 + hh % 2, :], xh[s:s + DH, tile, :].bitcast(F32),
                                ALU.subtract).then_inc(o_ready, 1)

            def step_of(h, hh, g, more=True):
                first = isinstance(h, int) and h == 0
                last_q = not more or (hh == HPG - 2 and isinstance(g, int) and g == NG - 1)
                if more:
                    dve.wait_ge(bias_landed[(hh + 1) % 2], (g * 2 + (hh + 1) // 2) * 16 + 16)
                for k in range(NS):
                    if more:
                        read_score(h + 1, (hh + 1) % 2, k)
                    if LAG <= k < LAG + NTT:
                        pt_low(h, hh, k - LAG)
                    if k in (1, 2):
                        coefficients(h, hh % 2, CMPB, k - 1)
                    if more and k in (5, 6):
                        coefficients(h + 1, (hh + 1) % 2, SLC, k - 5)
                    if more and k in (9, 10):
                        coefficients(h + 1, (hh + 1) % 2, WIN, k - 9)
                    if k == O_AT and not first:
                        o_low(h - 1, g * 2 + (hh - 1) // 2, (hh + 1) % 2)
                    if k in (7, 8) and not last_q:
                        n = hh + 2
                        stage_q(h + 2, g * 2 + n // 2, n % 2, n % 2, k - 7)

            dve.wait_ge(cmp_ready, 3)
            dve.wait_ge(bias_landed[0], 16)
            for k in range(NS):
                read_score(0, 0, k)
            for br in (SLC, WIN):
                for half in range(2):
                    coefficients(0, 0, br, half)
            for hh in range(HPG):
                step_of(hh, hh, 0)
            with dve.Fori(1, NG - 1) as g4:
                step.loop(g4, 4 * HPG, 1)
                for hh in range(HPG):
                    step_of(g4 * HPG + hh, hh, g4)
                step.end(NG - 2, 1)
            for hh in range(HPG):
                step_of(NH - HPG + hh, hh, NG - 1, more=hh < HPG - 1)
            o_low(NH - 1, NH // 2 - 1, HPG - 1)
            residual(3, C_FFN[3] - 1, 1.0, 5)
            ffn(3)
            for t in (0, 2):
                dve.wait_ge(y_mm, 4 + t + 1)
                V.tensor_copy(xin[:, t, T:2 * T], ps[:, 4 + t, :]).then_inc(y_even, 1)


def constants():
    sq = np.zeros((P, 2 * P + 1), np.float32)
    sq[:, 0:P] = np.eye(P)
    sq[0:64, P:P + 64] = 1
    sq[64:P, P + 64:2 * P] = 1
    sq[:, 2 * P] = np.arange(P) >= CMP_LEN - 1
    half = DK // 2
    inv = np.float32(10000.0) ** (-np.arange(half, dtype=np.float32) / np.float32(half))
    ang = (np.arange(T, dtype=np.float32)[None, :] * inv[:, None]).astype(np.float32)
    rot = np.stack([np.cos(ang), np.sin(ang)], 1).astype(np.float32)
    lg = np.log(1.0 - 2.0 ** (-5.0 - np.arange(RH, dtype=np.float64)))
    diff = np.arange(T)[None, None, :] - np.arange(P)[:, None, None]
    dec = np.where(diff >= 0, np.exp(lg[None, :, None] * np.maximum(diff, 0)) * DK ** -0.5, 0.0).astype(np.float32)
    dist = np.arange(REL) - P
    n = np.maximum(dist, 0)
    nf = np.maximum(n, 16).astype(np.float32)
    large = 16 + (np.log(nf / np.float32(16)) / np.float32(np.log(8.0)) * np.float32(16)).astype(np.int32)
    bucket = np.where(n < 16, n, np.minimum(large, 31))
    onehot = np.zeros((BUCKETS + 1, REL), np.float32)
    onehot[bucket[dist >= 0], np.arange(REL)[dist >= 0]] = -1
    onehot[BUCKETS, dist < 0] = 1
    return sq, rot, dec, onehot


def tall_chunks(w):
    k, n = w.shape
    return w.reshape(k // T, 4, P, n // 256, 256).transpose(3, 0, 2, 1, 4).reshape(-1, P, CW)


def wide_chunks(w):
    return w.reshape(-1, P, CW)


def natural_chunks(w):
    return w.reshape(4, 2, P, T).transpose(0, 2, 1, 3).reshape(-1, P, CW)


def ffn_chunks(gu, down):
    gu = gu.reshape(D, 2, FT, P).transpose(0, 2, 1, 3).reshape(D, 2 * F)
    return [tall_chunks(gu), wide_chunks(down)]


def kernel(**inputs):
    import concourse.bacc as bacc
    from concourse.bass_utils import run_bass_kernel_spmd

    a = {k: np.ascontiguousarray(v) for k, v in inputs.items()}
    gu1, dn1, gu2, dn2 = a["ffn1_w_gu"], a["ffn1_w_down"], a["ffn2_w_gu"], a["ffn2_w_down"]
    win, wout = a["ret_w_in"][0], a["ret_w_out"][0]
    rq = [tall_chunks(win[:, DK * h:DK * (h + 1)]) for h in range(RH)]
    rk = [tall_chunks(win[:, D + DK * h:D + DK * (h + 1)]) for h in range(RH)]
    rv = [natural_chunks(win[:, 2 * D + DV * h:2 * D + DV * (h + 1)]) for h in range(RH)]
    rg = [tall_chunks(win[:, 4 * D + DV * h:4 * D + DV * (h + 1)]) for h in range(RH)]
    ro = [tall_chunks(wout[DV * h:DV * (h + 1)]) for h in range(RH)]
    nin = a["nsa_w_in"][0]
    kc, vc, ks, vs, kw, vw = [nin[:, D + 256 * i:D + 256 * (i + 1)] for i in range(6)]
    parts = ffn_chunks(gu1[0], dn1[0]) + [rq[0], rk[0]]
    for h in range(RH):
        parts += [rv[h], rg[h]] + ([rq[h + 1], rk[h + 1]] if h < RH - 1 else []) + [ro[h]]
    parts += ffn_chunks(gu2[0], dn2[0]) + ffn_chunks(gu1[1], dn1[1])
    w1 = a["nsa_cmp_w1"][0]
    parts += [tall_chunks(w) for w in (kc, vc, ks, w1[0], kw, w1[1], nin[:, 0:D])]
    parts += [natural_chunks(np.concatenate([vs, vw], 1))]
    parts += [wide_chunks(a["nsa_w_out"][0])] + ffn_chunks(gu2[1], dn2[1])
    stream = np.ascontiguousarray(np.concatenate(parts, 0))
    assert stream.shape == (NCHUNK, P, CW)
    norms = [a["ffn1_norm"][0], a["mix_norm"][0], a["ffn2_norm"][0], a["ffn1_norm"][1], a["mix_norm"][1], a["ffn2_norm"][1]]
    gains = [a["nsa_q_gain"][0], a["nsa_k_gain"][0, 0], a["nsa_k_gain"][0, 1], a["nsa_k_gain"][0, 2]]
    sq, rot, dec, onehot = constants()
    arrays = {
        "x_in": a["x"].reshape(T, D),
        "stream": stream,
        "norm_g": np.stack(norms).reshape(6, KT, P).transpose(2, 0, 1),
        "gate_w": nin[:, -48:].reshape(D, 3, NH)[:, [1, 2, 0]].reshape(KT, P, 48).transpose(1, 0, 2),
        "cmp_w2": a["nsa_cmp_w2"][0].reshape(2, 2, P, DH).transpose(2, 0, 1, 3),
        "cmp_pos": a["nsa_cmp_pos"][0].reshape(2, LP, 2, DH).transpose(2, 3, 0, 1).reshape(P, 2, LP),
        "qk_gain": np.tile(np.stack(gains, 1), (2, 1)),
        "rel": a["rel_bias"],
        "c_sq": sq, "c_rot": rot, "c_dec": dec, "c_rel": onehot,
    }
    arrays = {k: np.ascontiguousarray(v) for k, v in arrays.items()}
    nc = bacc.Bacc("TRN2", target_bir_lowering=False, num_devices=1)
    args = {k: nc.dram_tensor(k, v.shape, mybir.dt.from_np(v.dtype), kind="ExternalInput").ap() for k, v in arrays.items()}
    rel_rows = nc.dram_tensor("rel_rows", (NH, REL), F32, kind="Internal").ap()
    out = nc.dram_tensor("out", (T, D), F32, kind="ExternalOutput").ap()
    trunk(nc, **args, rel_rows=rel_rows, out=out)
    r = run_bass_kernel_spmd(nc, [arrays], core_ids=[0])
    return r.results[0]["out"].reshape(1, T, D)
```
